# Optimizing a Trainium2 kernel written in Bass

```python
import jax
import jax.numpy as jnp
from jax import lax
import numpy as np
import math
import jax, jax.numpy as jnp

D_MODEL = 1024
BATCH = 1
SEQ = 256
DEPTH = 2

D_FF = 2816
DN_HEADS = 4
DN_HEAD_DIM = 128
DN_KEY_DIM = DN_HEADS * DN_HEAD_DIM
DN_VAL_DIM = DN_HEADS * DN_HEAD_DIM
DN_CONV = 4
DN_CHUNK = 64
CV_CHANNELS = 512
CV_KERNEL = 31
MLA_HEADS = 4
MLA_Q_LORA = 384
MLA_KV_LORA = 256
MLA_NOPE = 128
MLA_ROPE = 64
MLA_V = 128
ATTN_BLOCK = 128
ROPE_THETA = 10000.0
N_BRANCHES = 3
DEEPNORM_ALPHA = (2 * DEPTH) ** 0.25
DEEPNORM_BETA = (8 * DEPTH) ** -0.25
NORM_EPS = 1e-5
IN_SIZES = (DN_KEY_DIM, DN_KEY_DIM, DN_VAL_DIM, DN_VAL_DIM, DN_HEADS, DN_HEADS,
            2 * CV_CHANNELS, MLA_Q_LORA, MLA_KV_LORA, MLA_ROPE, N_BRANCHES * D_MODEL)
D_IN = sum(IN_SIZES)


def _split_points():
    return [int(v) for v in np.cumsum(IN_SIZES)[:-1]]

def layer_norm(x, g, b):
    xf = x.astype(jnp.float32)
    mu = jnp.mean(xf, axis=-1, keepdims=True)
    var = jnp.mean(jnp.square(xf - mu), axis=-1, keepdims=True)
    return ((xf - mu) * lax.rsqrt(var + NORM_EPS) * g + b).astype(x.dtype)

def rms_norm(x, w):
    xf = x.astype(jnp.float32)
    return (xf * lax.rsqrt(jnp.mean(jnp.square(xf), axis=-1, keepdims=True) + NORM_EPS) * w).astype(x.dtype)

def l2_normalize(x):
    xf = x.astype(jnp.float32)
    return xf * lax.rsqrt(jnp.sum(jnp.square(xf), axis=-1, keepdims=True) + 1e-6)

def swiglu(x, w_gate, w_up, w_down):
    return (jax.nn.silu(x @ w_gate) * (x @ w_up)) @ w_down

def causal_depthwise_conv(x, w):
    k, c = w.shape
    return lax.conv_general_dilated(
        x, w[:, None, :].astype(x.dtype), window_strides=(1,), padding=[(k - 1, 0)],
        dimension_numbers=('NWC', 'WIO', 'NWC'), feature_group_count=c)

def rope_tables(positions):
    half = MLA_ROPE // 2
    inv_freq = ROPE_THETA ** (-jnp.arange(half, dtype=jnp.float32) / half)
    ang = positions.astype(jnp.float32)[..., None] * inv_freq
    return jnp.cos(ang), jnp.sin(ang)

def apply_rope(x, cos, sin):
    half = x.shape[-1] // 2
    xf = x.astype(jnp.float32)
    x1, x2 = xf[..., :half], xf[..., half:]
    return jnp.concatenate([x1 * cos - x2 * sin, x2 * cos + x1 * sin], axis=-1).astype(x.dtype)

def gated_delta_rule(q, k, v, g, beta):
    b, t, h, dk = q.shape
    dv = v.shape[-1]
    c = DN_CHUNK
    n = t // c
    f32 = jnp.float32

    def chunks(a):
        a = a.reshape(b, n, c, h, *a.shape[3:])
        return jnp.moveaxis(a, (1, 3), (0, 2))

    q = chunks(q.astype(f32)) * (dk ** -0.5)
    k = chunks(k.astype(f32))
    v = chunks(v.astype(f32))
    beta = chunks(beta.astype(f32))
    g = jnp.cumsum(chunks(g.astype(f32)), axis=-1)
    causal = jnp.tril(jnp.ones((c, c), dtype=bool))
    strict = jnp.tril(jnp.ones((c, c), dtype=bool), -1)
    decay = jnp.exp(jnp.where(causal, g[..., :, None] - g[..., None, :], -jnp.inf))
    kk = jnp.einsum('nbhik,nbhjk->nbhij', k, k)
    a_mat = jnp.where(strict, beta[..., None] * kk * decay, 0.0) + jnp.eye(c, dtype=f32)
    rhs = jnp.concatenate([v * beta[..., None], k * (beta * jnp.exp(g))[..., None]], axis=-1)
    sol = lax.linalg.triangular_solve(a_mat, rhs, left_side=True, lower=True, unit_diagonal=True)
    u, w = sol[..., :dv], sol[..., dv:]
    qk = jnp.where(causal, jnp.einsum('nbhik,nbhjk->nbhij', q, k) * decay, 0.0)
    q_dec = q * jnp.exp(g)[..., None]
    g_last = g[..., -1]
    k_dec = k * jnp.exp(g_last[..., None] - g)[..., None]

    def step(state, xs):
        u_i, w_i, qk_i, q_dec_i, k_dec_i, gl_i = xs
        v_new = u_i - jnp.einsum('bhck,bhkv->bhcv', w_i, state)
        o = jnp.einsum('bhck,bhkv->bhcv', q_dec_i, state) + jnp.einsum('bhij,bhjv->bhiv', qk_i, v_new)
        state = state * jnp.exp(gl_i)[..., None, None] + jnp.einsum('bhck,bhcv->bhkv', k_dec_i, v_new)
        return state, o

    s0 = jnp.zeros((b, h, dk, dv), f32)
    _, o = lax.scan(step, s0, (u, w, qk, q_dec, k_dec, g_last))
    return jnp.moveaxis(o, (0, 2), (1, 3)).reshape(b, t, h, dv)

def deltanet_branch(q, k, v, z, a, beta_logit, conv_w, a_log, dt_bias, norm_w, w_o):
    b, t, _ = q.shape
    qkv = jax.nn.silu(causal_depthwise_conv(jnp.concatenate([q, k, v], axis=-1), conv_w))
    q, k, v = jnp.split(qkv, [DN_KEY_DIM, 2 * DN_KEY_DIM], axis=-1)
    q = l2_normalize(q.reshape(b, t, DN_HEADS, DN_HEAD_DIM))
    k = l2_normalize(k.reshape(b, t, DN_HEADS, DN_HEAD_DIM))
    v = v.reshape(b, t, DN_HEADS, DN_HEAD_DIM)
    beta = jax.nn.sigmoid(beta_logit.astype(jnp.float32))
    g = -jnp.exp(a_log.astype(jnp.float32)) * jax.nn.softplus(a.astype(jnp.float32) + dt_bias.astype(jnp.float32))
    o = gated_delta_rule(q, k, v, g, beta)
    o = rms_norm(o, norm_w) * jax.nn.silu(z.reshape(b, t, DN_HEADS, DN_HEAD_DIM).astype(jnp.float32))
    return o.reshape(b, t, DN_VAL_DIM).astype(z.dtype) @ w_o

def conv_branch(u, glu_b, dw_w, dw_b, ln_g, ln_b, w_pw2, b_pw2):
    u = u + glu_b
    h = u[..., :CV_CHANNELS] * jax.nn.sigmoid(u[..., CV_CHANNELS:])
    h = causal_depthwise_conv(h, dw_w) + dw_b
    h = jax.nn.silu(layer_norm(h, ln_g, ln_b))
    return h @ w_pw2 + b_pw2

def causal_block_attention(q_nope, q_rope, k_nope, k_rope, v):
    t = q_nope.shape[1]
    scale = (MLA_NOPE + MLA_ROPE) ** -0.5
    outs = []
    for i in range(t // ATTN_BLOCK):
        q0, q1 = i * ATTN_BLOCK, (i + 1) * ATTN_BLOCK
        s = (jnp.einsum('bqhd,bkhd->bhqk', q_nope[:, q0:q1], k_nope[:, :q1])
             + jnp.einsum('bqhr,bkr->bhqk', q_rope[:, q0:q1], k_rope[:, :q1])).astype(jnp.float32) * scale
        mask = jnp.arange(q1)[None, :] <= jnp.arange(q0, q1)[:, None]
        p = jax.nn.softmax(jnp.where(mask, s, -jnp.inf), axis=-1).astype(v.dtype)
        outs.append(jnp.einsum('bhqk,bkhv->bqhv', p, v[:, :q1]))
    return jnp.concatenate(outs, axis=1)

def mla_branch(c_q, c_kv, k_r, cos, sin, q_norm_w, w_uq, kv_norm_w, w_ukv, w_o):
    b, t, _ = c_q.shape
    q = (rms_norm(c_q, q_norm_w) @ w_uq).reshape(b, t, MLA_HEADS, MLA_NOPE + MLA_ROPE)
    q_nope = q[..., :MLA_NOPE]
    q_rope = apply_rope(q[..., MLA_NOPE:], cos[:, :, None, :], sin[:, :, None, :])
    kv = (rms_norm(c_kv, kv_norm_w) @ w_ukv).reshape(b, t, MLA_HEADS, MLA_NOPE + MLA_V)
    k_nope, v = kv[..., :MLA_NOPE], kv[..., MLA_NOPE:]
    k_rope = apply_rope(k_r, cos, sin)
    o = causal_block_attention(q_nope, q_rope, k_nope, k_rope, v)
    return o.reshape(b, t, MLA_HEADS * MLA_V) @ w_o

def hybrid_mixer(x, cos, sin, w_in, b_gate,
                 dn_conv_w, dn_a_log, dn_dt_bias, dn_norm_w, dn_w_o,
                 cv_glu_b, cv_dw_w, cv_dw_b, cv_ln_g, cv_ln_b, cv_w_pw2, cv_b_pw2,
                 mla_q_norm_w, mla_w_uq, mla_kv_norm_w, mla_w_ukv, mla_w_o, w_out):
    b, t, d = x.shape
    proj = x @ w_in
    (dq, dk, dv, dz, da, dbeta, glu, c_q, c_kv, k_r, gate_logits) = jnp.split(proj, _split_points(), axis=-1)
    y_dn = deltanet_branch(dq, dk, dv, dz, da, dbeta, dn_conv_w, dn_a_log, dn_dt_bias, dn_norm_w, dn_w_o)
    y_cv = conv_branch(glu, cv_glu_b, cv_dw_w, cv_dw_b, cv_ln_g, cv_ln_b, cv_w_pw2, cv_b_pw2)
    y_mla = mla_branch(c_q, c_kv, k_r, cos, sin, mla_q_norm_w, mla_w_uq, mla_kv_norm_w, mla_w_ukv, mla_w_o)
    gates = jax.nn.sigmoid((gate_logits + b_gate).astype(jnp.float32)).astype(x.dtype).reshape(b, t, N_BRANCHES, d)
    merged = gates[:, :, 0] * y_dn + gates[:, :, 1] * y_cv + gates[:, :, 2] * y_mla
    return merged @ w_out

def first_inputs(seed: int = 0) -> dict:
    key = jax.random.key(seed)
    ks = iter(jax.random.split(key, 48))
    L = DEPTH
    f32 = jnp.float32

    def w(shape, fan_in, scale=1.0):
        return jax.random.normal(next(ks), shape, f32) * (scale * fan_in ** -0.5)

    def gain(shape):
        return 1.0 + 0.02 * jax.random.normal(next(ks), shape, f32)

    def bias(shape):
        return 0.02 * jax.random.normal(next(ks), shape, f32)

    x = jax.random.normal(next(ks), (BATCH, SEQ, D_MODEL), f32)
    positions = (jax.random.randint(next(ks), (BATCH, 1), 0, 4096, dtype=jnp.int32)
                 + jnp.arange(SEQ, dtype=jnp.int32)[None, :])
    dt = jnp.exp(jax.random.uniform(next(ks), (L, DN_HEADS), f32, np.log(1e-3), np.log(1e-1)))
    return {
        'x': x,
        'positions': positions,
        'ln1_g': gain((L, D_MODEL)),
        'ln1_b': bias((L, D_MODEL)),
        'ffn1_w_gate': w((L, D_MODEL, D_FF), D_MODEL),
        'ffn1_w_up': w((L, D_MODEL, D_FF), D_MODEL),
        'ffn1_w_down': w((L, D_FF, D_MODEL), D_FF, DEEPNORM_BETA),
        'w_in': w((L, D_MODEL, D_IN), D_MODEL),
        'b_gate': bias((L, N_BRANCHES * D_MODEL)),
        'dn_conv_w': w((L, DN_CONV, 2 * DN_KEY_DIM + DN_VAL_DIM), DN_CONV),
        'dn_a_log': jnp.log(jax.random.uniform(next(ks), (L, DN_HEADS), f32, 1.0, 16.0)),
        'dn_dt_bias': dt + jnp.log(-jnp.expm1(-dt)),
        'dn_norm_w': gain((L, DN_HEAD_DIM)),
        'dn_w_o': w((L, DN_VAL_DIM, D_MODEL), DN_VAL_DIM, DEEPNORM_BETA),
        'cv_glu_b': bias((L, 2 * CV_CHANNELS)),
        'cv_dw_w': w((L, CV_KERNEL, CV_CHANNELS), CV_KERNEL),
        'cv_dw_b': bias((L, CV_CHANNELS)),
        'cv_ln_g': gain((L, CV_CHANNELS)),
        'cv_ln_b': bias((L, CV_CHANNELS)),
        'cv_w_pw2': w((L, CV_CHANNELS, D_MODEL), CV_CHANNELS, DEEPNORM_BETA),
        'cv_b_pw2': bias((L, D_MODEL)),
        'mla_q_norm_w': gain((L, MLA_Q_LORA)),
        'mla_w_uq': w((L, MLA_Q_LORA, MLA_HEADS * (MLA_NOPE + MLA_ROPE)), MLA_Q_LORA),
        'mla_kv_norm_w': gain((L, MLA_KV_LORA)),
        'mla_w_ukv': w((L, MLA_KV_LORA, MLA_HEADS * (MLA_NOPE + MLA_V)), MLA_KV_LORA),
        'mla_w_o': w((L, MLA_HEADS * MLA_V, D_MODEL), MLA_HEADS * MLA_V, DEEPNORM_BETA),
        'w_out': w((L, D_MODEL, D_MODEL), D_MODEL, DEEPNORM_BETA),
        'ln2_g': gain((L, D_MODEL)),
        'ln2_b': bias((L, D_MODEL)),
        'ffn2_w_gate': w((L, D_MODEL, D_FF), D_MODEL),
        'ffn2_w_up': w((L, D_MODEL, D_FF), D_MODEL),
        'ffn2_w_down': w((L, D_FF, D_MODEL), D_FF, DEEPNORM_BETA),
        'ln3_g': gain((L, D_MODEL)),
        'ln3_b': bias((L, D_MODEL)),
    }

def first_block(x, positions, ln1_g, ln1_b, ffn1_w_gate, ffn1_w_up, ffn1_w_down, w_in, b_gate,
              dn_conv_w, dn_a_log, dn_dt_bias, dn_norm_w, dn_w_o,
              cv_glu_b, cv_dw_w, cv_dw_b, cv_ln_g, cv_ln_b, cv_w_pw2, cv_b_pw2,
              mla_q_norm_w, mla_w_uq, mla_kv_norm_w, mla_w_ukv, mla_w_o,
              w_out, ln2_g, ln2_b, ffn2_w_gate, ffn2_w_up, ffn2_w_down, ln3_g, ln3_b):
    cos, sin = rope_tables(positions)
    h = x
    for l in range(DEPTH):
        h = layer_norm(DEEPNORM_ALPHA * h + 0.5 * swiglu(h, ffn1_w_gate[l], ffn1_w_up[l], ffn1_w_down[l]),
                       ln1_g[l], ln1_b[l])
        mix = hybrid_mixer(h, cos, sin, w_in[l], b_gate[l],
                           dn_conv_w[l], dn_a_log[l], dn_dt_bias[l], dn_norm_w[l], dn_w_o[l],
                           cv_glu_b[l], cv_dw_w[l], cv_dw_b[l], cv_ln_g[l], cv_ln_b[l], cv_w_pw2[l], cv_b_pw2[l],
                           mla_q_norm_w[l], mla_w_uq[l], mla_kv_norm_w[l], mla_w_ukv[l], mla_w_o[l], w_out[l])
        h = layer_norm(DEEPNORM_ALPHA * h + mix, ln2_g[l], ln2_b[l])
        h = layer_norm(DEEPNORM_ALPHA * h + 0.5 * swiglu(h, ffn2_w_gate[l], ffn2_w_up[l], ffn2_w_down[l]),
                       ln3_g[l], ln3_b[l])
    return h


DEPTH_2 = 1

D_MIX = D_MODEL
D_LRU = D_MIX // 2
D_ATTN = D_MIX - D_LRU
N_LRU_BLOCKS = 8
LRU_BLOCK = D_LRU // N_LRU_BLOCKS
CONV_WIDTH = 4
LRU_C = 8.0
N_HEADS = 8
HEAD_DIM = D_ATTN // N_HEADS
MOBA_BLOCK = 256
MOBA_TOPK = 3
Q_CHUNK = 32
REL_BUCKETS = 32
REL_MAX_DIST = 128
N_GROUPS = 4
EXPERTS_PER_GROUP = 8
N_EXPERTS = N_GROUPS * EXPERTS_PER_GROUP
EXPERT_TOPK = 2
D_EXPERT = 256
MOE_ROWS = 128
LN_EPS = 1e-5
DEEPNORM_ALPHA_2 = (2.0 * DEPTH_2) ** 0.25
DEEPNORM_BETA_2 = (8.0 * DEPTH_2) ** -0.25
N_MOD = 6
D_IN_PROJ = 2 * D_LRU + 3 * D_ATTN


def _normalize(x):
    xf = x.astype(jnp.float32)
    mu = jnp.mean(xf, axis=-1, keepdims=True)
    var = jnp.mean(jnp.square(xf - mu), axis=-1, keepdims=True)
    return (xf - mu) * lax.rsqrt(var + LN_EPS)

def layernorm(x, g, b):
    return (_normalize(x) * g + b).astype(x.dtype)

def rmsnorm(x, g):
    xf = x.astype(jnp.float32)
    y = xf * lax.rsqrt(jnp.mean(jnp.square(xf), axis=-1, keepdims=True) + LN_EPS)
    return (y * g).astype(x.dtype)

def modulate(x, shift, scale):
    return (_normalize(x) * (1.0 + scale) + shift).astype(x.dtype)

def causal_depthwise_conv_2(x, w, b):
    s = x.shape[1]
    xp = jnp.pad(x, ((0, 0), (CONV_WIDTH - 1, 0), (0, 0)))
    return sum(w[k] * xp[:, k:k + s] for k in range(CONV_WIDTH)) + b

def rg_lru(xc, w_a, b_a, w_x, b_x, lam):
    bsz, s, _ = xc.shape
    xb = xc.reshape(bsz, s, N_LRU_BLOCKS, LRU_BLOCK)
    r = jax.nn.sigmoid(jnp.einsum('bsni,nij->bsnj', xb, w_a) + b_a).reshape(bsz, s, D_LRU)
    i = jax.nn.sigmoid(jnp.einsum('bsni,nij->bsnj', xb, w_x) + b_x).reshape(bsz, s, D_LRU)
    log_a = -LRU_C * r.astype(jnp.float32) * jax.nn.softplus(-lam.astype(jnp.float32))
    a = jnp.exp(log_a)
    mult = jnp.sqrt(-jnp.expm1(2.0 * log_a))
    u = mult * (i * xc).astype(jnp.float32)

    def combine(left, right):
        a1, b1 = left
        a2, b2 = right
        return a1 * a2, a2 * b1 + b2

    _, h = lax.associative_scan(combine, (a, u), axis=1)
    return h.astype(xc.dtype)

def t5_bucket(rel):
    n = jnp.maximum(rel, 0)
    max_exact = REL_BUCKETS // 2
    large = max_exact + (jnp.log(jnp.maximum(n, 1).astype(jnp.float32) / max_exact)
                         / math.log(REL_MAX_DIST / max_exact)
                         * (REL_BUCKETS - max_exact)).astype(jnp.int32)
    large = jnp.minimum(large, REL_BUCKETS - 1)
    return jnp.where(n < max_exact, n, large)

def moba_attention(q, k, v, rel_bias):
    bsz, s, h, dh = q.shape
    nb = -(-s // MOBA_BLOCK)
    sp = nb * MOBA_BLOCK
    pad = ((0, 0), (0, sp - s), (0, 0), (0, 0))
    qp = jnp.pad(q, pad).transpose(0, 2, 1, 3)
    kp = jnp.pad(k, pad).transpose(0, 2, 1, 3)
    vp = jnp.pad(v, pad).transpose(0, 2, 1, 3)
    scale = HEAD_DIM ** -0.5
    k_blocks = kp.reshape(bsz, h, nb, MOBA_BLOCK, dh)
    v_blocks = vp.reshape(bsz, h, nb, MOBA_BLOCK, dh)
    k_mean = jnp.mean(k_blocks, axis=3)

    own_all = jnp.arange(sp) // MOBA_BLOCK
    past = jnp.arange(nb)[None, :] < own_all[:, None]
    gate = jnp.einsum('bhqd,bhnd->bhqn', qp, k_mean).astype(jnp.float32)
    gate = jnp.where(past, gate, -jnp.inf)
    if nb < MOBA_TOPK:
        gate = jnp.pad(gate, ((0, 0), (0, 0), (0, 0), (0, MOBA_TOPK - nb)), constant_values=-jnp.inf)
    _, sel = lax.top_k(gate, MOBA_TOPK)

    table_h = rel_bias.T
    b_idx = jnp.arange(bsz)
    h_idx = jnp.arange(h)
    kv_offsets = jnp.arange(MOBA_BLOCK)

    def chunk(ci):
        start = ci * Q_CHUNK
        qc = lax.dynamic_slice_in_dim(qp, start, Q_CHUNK, axis=2)
        selc = lax.dynamic_slice_in_dim(sel, start, Q_CHUNK, axis=2)
        qpos = start + jnp.arange(Q_CHUNK)
        own = start // MOBA_BLOCK
        valid = selc < own
        selg = jnp.minimum(selc, nb - 1)
        kg = k_blocks[b_idx[:, None, None, None], h_idx[None, :, None, None], selg]
        vg = v_blocks[b_idx[:, None, None, None], h_idx[None, :, None, None], selg]
        kpos_p = selg[..., None] * MOBA_BLOCK + kv_offsets
        s_p = jnp.einsum('bhqd,bhqnkd->bhqnk', qc, kg).astype(jnp.float32) * scale
        s_p = s_p + table_h[h_idx[None, :, None, None, None], t5_bucket(qpos[:, None, None] - kpos_p)]
        s_p = jnp.where(valid[..., None], s_p, -jnp.inf)
        ko = lax.dynamic_slice_in_dim(kp, own * MOBA_BLOCK, MOBA_BLOCK, axis=2)
        vo = lax.dynamic_slice_in_dim(vp, own * MOBA_BLOCK, MOBA_BLOCK, axis=2)
        rel_o = qpos[:, None] - (own * MOBA_BLOCK + kv_offsets)[None, :]
        s_o = jnp.einsum('bhqd,bhkd->bhqk', qc, ko).astype(jnp.float32) * scale
        s_o = s_o + table_h[:, t5_bucket(rel_o)]
        s_o = jnp.where(rel_o >= 0, s_o, -jnp.inf)
        logits = jnp.concatenate([s_p.reshape(bsz, h, Q_CHUNK, MOBA_TOPK * MOBA_BLOCK), s_o], axis=-1)
        p = jax.nn.softmax(logits, axis=-1)
        p_p = p[..., :MOBA_TOPK * MOBA_BLOCK].reshape(bsz, h, Q_CHUNK, MOBA_TOPK, MOBA_BLOCK).astype(v.dtype)
        p_o = p[..., MOBA_TOPK * MOBA_BLOCK:].astype(v.dtype)
        return (jnp.einsum('bhqnk,bhqnkd->bhqd', p_p, vg)
                + jnp.einsum('bhqk,bhkd->bhqd', p_o, vo))

    outs = lax.map(chunk, jnp.arange(sp // Q_CHUNK))
    out = outs.transpose(1, 2, 0, 3, 4).reshape(bsz, h, sp, dh)[:, :, :s]
    return out.transpose(0, 2, 1, 3).reshape(bsz, s, h * dh)

def hybrid_mixer_2(u, w_in, conv_w, conv_b, w_gate_a, b_gate_a, w_gate_x, b_gate_x,
                 lru_lambda, rel_bias, norm_lru_g, norm_attn_g, w_out):
    bsz, s, _ = u.shape
    proj = u @ w_in
    x_lru, y_lru, q, k, v = jnp.split(
        proj, [D_LRU, 2 * D_LRU, 2 * D_LRU + D_ATTN, 2 * D_LRU + 2 * D_ATTN], axis=-1)
    h = rg_lru(causal_depthwise_conv_2(x_lru, conv_w, conv_b),
               w_gate_a, b_gate_a, w_gate_x, b_gate_x, lru_lambda)
    lru_out = h * jax.nn.gelu(y_lru)
    attn_out = moba_attention(q.reshape(bsz, s, N_HEADS, HEAD_DIM),
                              k.reshape(bsz, s, N_HEADS, HEAD_DIM),
                              v.reshape(bsz, s, N_HEADS, HEAD_DIM), rel_bias)
    merged = jnp.concatenate([rmsnorm(lru_out, norm_lru_g), rmsnorm(attn_out, norm_attn_g)], axis=-1)
    return merged @ w_out

def hierarchical_moe(u, w_rg, b_rg, w_re, b_re, w1, w3, w2):
    bsz, s, d = u.shape
    nc = s // MOE_ROWS
    xt = u.reshape(bsz, nc, MOE_ROWS, d).transpose(1, 0, 2, 3).reshape(nc, bsz * MOE_ROWS, d)

    def body(xc):
        g_prob = jax.nn.softmax((xc @ w_rg + b_rg).astype(jnp.float32), axis=-1)
        g_top, g_idx = lax.top_k(g_prob, 1)
        e_logits = (xc @ w_re + b_re).astype(jnp.float32).reshape(-1, N_GROUPS, EXPERTS_PER_GROUP)
        e_in = jnp.take_along_axis(e_logits, g_idx[:, :, None], axis=1)[:, 0]
        e_top, e_loc = lax.top_k(jax.nn.softmax(e_in, axis=-1), EXPERT_TOPK)
        e_top = e_top / jnp.sum(e_top, axis=-1, keepdims=True)
        weights = g_top * e_top
        e_glob = g_idx * EXPERTS_PER_GROUP + e_loc
        gate = jnp.sum(jax.nn.one_hot(e_glob, N_EXPERTS, dtype=jnp.float32) * weights[..., None], axis=1)
        hdn = jax.nn.silu(jnp.einsum('td,edf->tef', xc, w1)) * jnp.einsum('td,edf->tef', xc, w3)
        return jnp.einsum('tef,efd->td', hdn * gate[:, :, None].astype(hdn.dtype), w2)

    ys = lax.map(body, xt)
    return ys.reshape(nc, bsz, MOE_ROWS, d).transpose(1, 0, 2, 3).reshape(bsz, s, d)

def second_inputs(seed: int = 0) -> dict:
    key = jax.random.key(seed)
    ks = jax.random.split(key, 28)
    f32 = jnp.float32
    L = DEPTH_2

    def nrm(k, shape, scale):
        return jax.random.normal(k, shape, f32) * scale

    a_c = jax.random.uniform(ks[11], (L, D_LRU), f32, 0.9, 0.999)
    a_base = a_c ** (1.0 / LRU_C)
    return {
        'x': nrm(ks[0], (BATCH, SEQ, D_MODEL), 1.0),
        'c': nrm(ks[1], (BATCH, D_MODEL), 1.0),
        'w_ada': nrm(ks[2], (L, D_MODEL, N_MOD * D_MODEL), 0.5 * D_MODEL ** -0.5),
        'b_ada': nrm(ks[3], (L, N_MOD * D_MODEL), 0.02),
        'w_in': nrm(ks[4], (L, D_MODEL, D_IN_PROJ), D_MODEL ** -0.5),
        'conv_w': nrm(ks[5], (L, CONV_WIDTH, D_LRU), CONV_WIDTH ** -0.5),
        'conv_b': nrm(ks[6], (L, D_LRU), 0.02),
        'w_gate_a': nrm(ks[7], (L, N_LRU_BLOCKS, LRU_BLOCK, LRU_BLOCK), LRU_BLOCK ** -0.5),
        'b_gate_a': nrm(ks[8], (L, N_LRU_BLOCKS, LRU_BLOCK), 0.02),
        'w_gate_x': nrm(ks[9], (L, N_LRU_BLOCKS, LRU_BLOCK, LRU_BLOCK), LRU_BLOCK ** -0.5),
        'b_gate_x': nrm(ks[10], (L, N_LRU_BLOCKS, LRU_BLOCK), 0.02),
        'lru_lambda': jnp.log(a_base) - jnp.log1p(-a_base),
        'rel_bias': nrm(ks[12], (REL_BUCKETS, N_HEADS), 0.5),
        'norm_lru_g': 1.0 + nrm(ks[13], (L, D_LRU), 0.05),
        'norm_attn_g': 1.0 + nrm(ks[14], (L, D_ATTN), 0.05),
        'w_out': nrm(ks[15], (L, D_MIX, D_MODEL), DEEPNORM_BETA_2 * D_MIX ** -0.5),
        'ln1_g': 1.0 + nrm(ks[16], (L, D_MODEL), 0.05),
        'ln1_b': nrm(ks[17], (L, D_MODEL), 0.02),
        'w_router_group': nrm(ks[18], (L, D_MODEL, N_GROUPS), D_MODEL ** -0.5),
        'b_router_group': nrm(ks[19], (L, N_GROUPS), 0.01),
        'w_router_expert': nrm(ks[20], (L, D_MODEL, N_EXPERTS), D_MODEL ** -0.5),
        'b_router_expert': nrm(ks[21], (L, N_EXPERTS), 0.01),
        'w1': nrm(ks[22], (L, N_EXPERTS, D_MODEL, D_EXPERT), D_MODEL ** -0.5),
        'w3': nrm(ks[23], (L, N_EXPERTS, D_MODEL, D_EXPERT), D_MODEL ** -0.5),
        'w2': nrm(ks[24], (L, N_EXPERTS, D_EXPERT, D_MODEL), DEEPNORM_BETA_2 * D_EXPERT ** -0.5),
        'ln2_g': 1.0 + nrm(ks[25], (L, D_MODEL), 0.05),
        'ln2_b': nrm(ks[26], (L, D_MODEL), 0.02),
    }

def second_block(x, c, w_ada, b_ada, w_in, conv_w, conv_b, w_gate_a, b_gate_a, w_gate_x, b_gate_x,
              lru_lambda, rel_bias, norm_lru_g, norm_attn_g, w_out, ln1_g, ln1_b,
              w_router_group, b_router_group, w_router_expert, b_router_expert,
              w1, w3, w2, ln2_g, ln2_b):
    bsz, _, d = x.shape
    silu_c = jax.nn.silu(c)
    for l in range(DEPTH_2):
        mod = (silu_c @ w_ada[l] + b_ada[l]).reshape(bsz, N_MOD, d)
        sh1, sc1, g1, sh2, sc2, g2 = [mod[:, j, None, :] for j in range(N_MOD)]
        u = modulate(x, sh1, sc1)
        mix = hybrid_mixer_2(u, w_in[l], conv_w[l], conv_b[l], w_gate_a[l], b_gate_a[l],
                           w_gate_x[l], b_gate_x[l], lru_lambda[l], rel_bias,
                           norm_lru_g[l], norm_attn_g[l], w_out[l])
        x = layernorm(DEEPNORM_ALPHA_2 * x + g1 * mix, ln1_g[l], ln1_b[l])
        u2 = modulate(x, sh2, sc2)
        ffn = hierarchical_moe(u2, w_router_group[l], b_router_group[l], w_router_expert[l],
                               b_router_expert[l], w1[l], w3[l], w2[l])
        x = layernorm(DEEPNORM_ALPHA_2 * x + g2 * ffn, ln2_g[l], ln2_b[l])
    return x


def setup_inputs(seed=0):
    out = dict(first_inputs(seed))
    for name, value in second_inputs(seed + 1).items():
        if name != "x":
            out[name + "_2"] = value
    return out


def reference(
    x, positions, ln1_g, ln1_b, ffn1_w_gate, ffn1_w_up, ffn1_w_down, w_in, b_gate, dn_conv_w,
    dn_a_log, dn_dt_bias, dn_norm_w, dn_w_o, cv_glu_b, cv_dw_w, cv_dw_b, cv_ln_g, cv_ln_b,
    cv_w_pw2, cv_b_pw2, mla_q_norm_w, mla_w_uq, mla_kv_norm_w, mla_w_ukv, mla_w_o, w_out, ln2_g,
    ln2_b, ffn2_w_gate, ffn2_w_up, ffn2_w_down, ln3_g, ln3_b, c_2, w_ada_2, b_ada_2, w_in_2,
    conv_w_2, conv_b_2, w_gate_a_2, b_gate_a_2, w_gate_x_2, b_gate_x_2, lru_lambda_2,
    rel_bias_2, norm_lru_g_2, norm_attn_g_2, w_out_2, ln1_g_2, ln1_b_2, w_router_group_2,
    b_router_group_2, w_router_expert_2, b_router_expert_2, w1_2, w3_2, w2_2, ln2_g_2, ln2_b_2,
):
    x = first_block(
        x, positions, ln1_g, ln1_b, ffn1_w_gate, ffn1_w_up, ffn1_w_down, w_in, b_gate,
        dn_conv_w, dn_a_log, dn_dt_bias, dn_norm_w, dn_w_o, cv_glu_b, cv_dw_w, cv_dw_b, cv_ln_g,
        cv_ln_b, cv_w_pw2, cv_b_pw2, mla_q_norm_w, mla_w_uq, mla_kv_norm_w, mla_w_ukv, mla_w_o,
        w_out, ln2_g, ln2_b, ffn2_w_gate, ffn2_w_up, ffn2_w_down, ln3_g, ln3_b,
    )
    return second_block(
        x, c_2, w_ada_2, b_ada_2, w_in_2, conv_w_2, conv_b_2, w_gate_a_2, b_gate_a_2,
        w_gate_x_2, b_gate_x_2, lru_lambda_2, rel_bias_2, norm_lru_g_2, norm_attn_g_2, w_out_2,
        ln1_g_2, ln1_b_2, w_router_group_2, b_router_group_2, w_router_expert_2,
        b_router_expert_2, w1_2, w3_2, w2_2, ln2_g_2, ln2_b_2,
    )


_drawn_inputs = setup_inputs


def setup_inputs(seed=0):
    import zlib

    import numpy as np

    out = dict(_drawn_inputs(seed))
    spreads = {}
    factors = {'b_gate': 8.0,
     'dn_a_log': 3.704,
     'dn_norm_w': 27.286,
     'cv_glu_b': 8.0,
     'cv_dw_b': 8.0,
     'cv_ln_g': 8.0,
     'cv_ln_b': 8.0,
     'cv_b_pw2': 8.0,
     'mla_q_norm_w': 8.0,
     'mla_kv_norm_w': 8.0,
     'b_ada_2': 3.498,
     'conv_b_2': 6.182,
     'w_gate_a_2': 2.793,
     'b_gate_a_2': 55.992,
     'b_gate_x_2': 8.0,
     'norm_lru_g_2': 8.0,
     'norm_attn_g_2': 8.0,
     'ln1_b_2': 2.717,
     'b_router_group_2': 56.506,
     'b_router_expert_2': 54.953,
     'ln2_b_2': 2.76}
    for name, (base, spread) in spreads.items():
        noise = np.random.default_rng([zlib.crc32(name.encode()), seed]).standard_normal(out[name].shape)
        drawn = base * np.exp(spread * noise) if base else spread * noise
        out[name] = jnp.asarray(drawn.astype(out[name].dtype))
    for name, factor in factors.items():
        out[name] = (out[name] * factor).astype(out[name].dtype)
    return out
```

```python
from contextlib import ExitStack

import numpy as np

import concourse.bass as bass
from concourse import mybir

F32 = mybir.dt.float32
I32 = mybir.dt.int32
ALU = mybir.AluOpType
ACT = mybir.ActivationFunctionType
AX = mybir.AxisListType.X
ds = bass.ds

P = 128
T = 256
NT = T // P
D = 1024
KD = D // P
DEPTH = 2
FF = 2816
NF = FF // P
HEADS = 4
HD = 128
CONV = 4
CVC = 512
CVK = 31
QL, KVL, NOPE, ROPE, VD = 384, 256, 128, 64, 128
THETA = 10000.0
EPS = 1e-5
ALPHA = (2 * DEPTH) ** 0.25
ALPHA_2 = 2.0 ** 0.25
MASKED = -1e30
LEVELS = 7
DL = 512
H2 = 8
HD2 = 64
LRU_C = 8.0
GROUPS, PER_GROUP = 4, 8
EXPERTS = GROUPS * PER_GROUP
DE = 256
BUCKETS, MAX_DIST = 32, 128
PAD = CVK - 1
RAMP = 384

OFF_QKV = 0
OFF_Z = 3 * HEADS * HD
OFF_GLU = OFF_Z + HEADS * HD + 2 * HEADS
OFF_CQ = OFF_GLU + 2 * CVC
OFF_CKV = OFF_CQ + QL
OFF_GATE = OFF_CKV + KVL + ROPE

C_ID, C_TRI, C_LEV, C_CAUSAL = 0, 128, 256, 256 + 128 * LEVELS
C_BUCKET = C_CAUSAL + 3 * P
C_FREQ = C_BUCKET + RAMP
C_IOTA = C_FREQ + 32
C_ALL = C_IOTA + 32

ROWS = {}
for _tile, _group in enumerate((
        (("ln1_g", 8), ("ln1_b", 8), ("ln2_g", 8), ("ln2_b", 8), ("ln3_g", 8), ("ln3_b", 8),
         ("b_gate", 24), ("dn_conv_w", 48), ("cv_glu_b", 8)),
        (("cv_dw_w", 124),),
        (("cv_dw_b", 4), ("cv_ln_g", 4), ("cv_ln_b", 4), ("cv_b_pw2", 8), ("mla_q_norm_w", 3),
         ("mla_kv_norm_w", 2), ("dn_norm_w", 1)))):
    _at = 0
    for _name, _n in _group:
        ROWS[_name] = (_tile, _at, _n)
        _at += _n


def shape_constants():
    c = np.zeros((P, C_ALL), np.float32)
    i = np.arange(P)
    c[:, C_ID:C_ID + P] = np.eye(P)
    c[:, C_TRI:C_TRI + P] = i[:, None] <= i[None, :]
    for lev in range(LEVELS):
        s = 1 << lev
        pair = (i[:, None] // (2 * s)) == (i[None, :] // (2 * s))
        c[:, C_LEV + lev * P:C_LEV + (lev + 1) * P] = pair & (i[None, :] % (2 * s) >= s) & (i[:, None] % (2 * s) < s)
    above = np.where(i[None, :] > i[:, None], MASKED, 0.0)
    c[:, C_CAUSAL:C_CAUSAL + P] = above
    c[:, C_CAUSAL + 2 * P:C_CAUSAL + 3 * P] = above
    rel = T - 1 - np.arange(RAMP)
    n = np.maximum(rel, 0)
    exact = BUCKETS // 2
    large = exact + (np.log(np.maximum(n, 1).astype(np.float32) / np.float32(exact)) / np.float32(np.log(MAX_DIST / exact))
                     * np.float32(BUCKETS - exact)).astype(np.int32)
    bucket = np.where(n < exact, n, np.minimum(large, BUCKETS - 1))
    bucket = np.where(rel < 0, BUCKETS, bucket)
    c[bucket, C_BUCKET + np.arange(RAMP)] = 1.0
    half = ROPE // 2
    c[:, C_FREQ:C_FREQ + half] = np.float32(THETA) ** (-np.arange(half, dtype=np.float32) / np.float32(half))
    c[:, C_IOTA:C_IOTA + EXPERTS] = np.arange(EXPERTS)
    return c


UNITS = (["glu_value", "glu_gate", "q", "k", "v", "z_ab", "c_q", "c_kv", "w_uq", "w_ukv"]
         + ["gates"] * KD + ["w_out"] * 2)
UNIT_DMAS = {"gates": 6}
W_SLOT = 4608
F_SLOT = 3072
E_SLOT = 6144
UNITS_PER_SLOT = len(UNITS) // 2
LANDED = []
for _u, _name in enumerate(UNITS):
    LANDED.append((LANDED[_u - 2] if _u >= 2 else 0) + 16 * UNIT_DMAS.get(_name, 1))
LANDED_PER_LAYER = [LANDED[-2], LANDED[-1]]

JOBS = (["gv0", "gv1", "gg0", "gg1", "q0", "q1", "k0", "k1", "v0", "v1", "z0", "z1", "ab",
         "cq0", "cq1", "ck0", "ck1", "G"]
        + ["tok_q0", "tok_q1", "tok_k0", "tok_k1", "tok_v0", "tok_v1"]
        + ["cqTa", "cqTb", "ckvT", "krT", "Gb0", "Gb1", "qn0", "qn1", "qr"]
        + ["qT0", "qT1", "kT0", "kT1", "kbT0", "kbT1", "kn0", "kn1", "mv0", "mv1"]
        + ["kk0", "kk1", "qk0", "qk1", "qrT", "s0", "s1", "s2", "s3"]
        + [f"{w}{t}.{lev}" for lev in range(LEVELS) for w in ("P", "MP", "MPT") for t in range(NT)]
        + ["p0", "p1", "p2", "p3", "mo0", "mo1", "vn0", "S1", "KS", "vn1", "O0", "O1", "O1s", "oT0", "oT1"]
        + ["cvt0", "cvt1", "cvb0", "cvb1"])
JOBS_2 = (["rows2"] + [f"ramp{n}" for n in range(H2)] + [f"ada{n}" for n in range(4)] + [f"u{n}" for n in range(4)]
          + ["xl0", "xl1", "yl0", "yl1", "ada4", "ada5", "qq0", "qq1", "ada6", "kk20", "kk21", "ada7", "vv0", "vv1",
             "g1b0", "g1b1", "ga0", "ga1", "gx0", "gx1"]
          + [f"a{n}" for n in range(H2)] + ["rms0"]
          + ["b0", "b1", "c0", "b2", "b3", "c1", "b4", "b5", "c2", "b6", "b7", "c3"]
          + ["rms1", "ada8", "ada9", "ada10", "ada11", "wo00", "wo10", "wo01", "wo11", "g2b0", "g2b1"]
          + [f"w{n}" for n in range(4)] + ["router"])
BANKS = 8
BANK = {name: n % BANKS for jobs in (JOBS, JOBS_2) for n, name in enumerate(jobs)}
ROUND = {name: n // BANKS for jobs in (JOBS, JOBS_2) for n, name in enumerate(jobs)}


TWO_PI = (6.28125, 0.001934051513671875, float(2 * np.pi - 6.28125 - 0.001934051513671875))


class Steps:

    def __init__(self, eng, sem):
        self.eng, self.sem, self.n = eng, sem, 0

    def step(self, ins):
        ins.then_inc(self.sem, 1)
        self.n += 1
        return self.n

    def sync(self, n=None):
        if n is None:
            n = self.n
        if n > 0:
            self.eng.wait_ge(self.sem, n)

    def restart(self):
        self.eng.sem_clear(self.sem)
        self.n = 0


def build(nc, A, out):
    ctx = ExitStack()
    with ctx:
        def sb(name, shape, dt=F32):
            return ctx.enter_context(nc.sbuf_tensor(name, shape, dt))

        names = {}

        def S(name):
            if name not in names:
                names[name] = ctx.enter_context(nc.semaphore(name))
            return names[name]

        cst = sb("cst", [P, C_ALL])
        ones = sb("ones", [P, P])
        h = sb("h", [P, NT, D])
        hT = sb("hT", [P, KD, T])
        gain = sb("gain", [P, D])
        bias = sb("bias", [P, D])
        wbuf = sb("wbuf", [P, 2 * W_SLOT + 2 * F_SLOT])
        R1 = sb("R1", [P, 12 * (T + CONV - 1)])
        R2 = sb("R2", [P, 12 * T])
        R3 = sb("R3", [P, 12 * T])
        cvpad = sb("cvpad", [P, 4, T + PAD])
        cvu = sb("cvu", [P, 4, T])
        cvg = sb("cvg", [P, 4, T])
        mA = sb("mA", [P, 2176])
        ckvT = sb("ckvT", [P, 2, T])
        qnT = sb("qnT", [P, HEADS, T])
        qr = sb("qr", [P, NT, HEADS, ROPE])
        qrT = sb("qrT", [P, 2, T])
        krT = sb("krT", [P, T])
        krd = sb("krd", [P, NT, 2, ROPE])
        knT = sb("knT", [P, HEADS, T])
        mv = sb("mv", [P, NT, HEADS, VD])
        prob2 = sb("prob2", [P, 2, 3 * P])
        qt = sb("qt", [P, NT, HEADS, HD])
        kt = sb("kt", [P, NT, HEADS, HD])
        vt = sb("vt", [P, NT, HEADS, HD])
        kdec = sb("kdec", [P, HEADS, HD])
        qT = sb("qT", [P, NT, HEADS, P])
        kT = sb("kT", [P, NT, HEADS, P])
        kbT = sb("kbT", [P, NT, HEADS, P])
        z = sb("z", [P, NT, HEADS, HD])
        pcol = sb("pcol", [P, 3, P])
        phalf = sb("phalf", [P, 3, P])
        cos = sb("cos", [P, NT, 32])
        sin = sb("sin", [P, NT, 32])
        stats = sb("stats", [P, NT, 2, 6])
        mvar = sb("mvar", [P, NT, 2])
        ry = sb("ry", [P, 16])
        rt = sb("rt", [P, 16])
        rv = sb("rv", [P, 16])
        dtab = sb("dtab", [P, 8])
        rel = sb("rel", [BUCKETS + 1, H2])
        pos = sb("pos", [P, NT], I32)
        abt = sb("abt", [P, NT, 8])
        ab1 = sb("ab1", [P, NT, 4])
        ab2 = sb("ab2", [P, NT, 4])
        ea = sb("ea", [P, 4])
        beta = sb("beta", [P, NT, 4])
        betah = sb("betah", [P, NT, 4])
        g = sb("g", [P, NT, 4])
        Gs = sb("Gs", [P, NT, 8])
        eG = sb("eG", [P, NT, 4])
        dG = sb("dG", [P, 4])
        eD = sb("eD", [P, 4])
        nmax = sb("nmax", [P, HEADS, 2])
        psums = sb("psums", [P, HEADS, 2])
        ps = [ctx.enter_context(nc.psum_tensor(f"bank{b}", [P, 512], F32)) for b in range(BANKS)]

        ident = cst[:, C_ID:C_ID + P]
        tri = cst[:, C_TRI:C_TRI + P]
        dnpad = R1[:, :].rearrange("p (c t) -> p c t", c=12)
        AT = R1[:, 0:1024].rearrange("p (t h j) -> p t h j", t=NT, h=HEADS)
        Pm = R1[:, 1024:2048].rearrange("p (t h j) -> p t h j", t=NT, h=HEADS)
        ATl = [R1[:, 2048:3072].rearrange("p (t h j) -> p t h j", t=NT, h=HEADS), qt[:, :, :, :]]
        kb = ATl[0]
        dn = R2[:, :].rearrange("p (c t) -> p c t", c=12)
        M = R2[:, 0:1024].rearrange("p (t h j) -> p t h j", t=NT, h=HEADS)
        MT = R2[:, 1024:2048].rearrange("p (t h j) -> p t h j", t=NT, h=HEADS)
        DT = R2[:, 2048:3072].rearrange("p (t h j) -> p t h j", t=NT, h=HEADS)
        merged = R2[:, 0:2048].rearrange("p (k t) -> p k t", k=KD)
        prow = R2[:, 0:384].rearrange("p (a n) -> p a n", a=3)
        dnth = R3[:, :].rearrange("p (c t) -> p c t", c=12)
        QK = R3[:, 0:1024].rearrange("p (t h j) -> p t h j", t=NT, h=HEADS)
        vn0 = R3[:, 1024:1536].rearrange("p (h j) -> p h j", h=HEADS)
        S1 = R3[:, 1536:2048].rearrange("p (h j) -> p h j", h=HEADS)
        Rn = R3[:, 2048:2560].rearrange("p (h j) -> p h j", h=HEADS)
        vn1 = R3[:, 2560:3072].rearrange("p (h j) -> p h j", h=HEADS)
        o = qt
        oT = kt[:, :, :, :].rearrange("p a b c -> p (a b c)").rearrange("p (h t) -> p h t", h=HEADS)
        th = [R3[:, 256 * s:256 * s + 256] for s in range(2)]
        yb = [R3[:, 512 + 256 * s:768 + 256 * s] for s in range(2)]
        act = [R3[:, 1024 + 256 * s:1280 + 256 * s] for s in range(2)]
        gth = [[R3[:, 768 * s + 256 * b:768 * s + 256 * b + 256] for b in range(3)] for s in range(2)]
        gyb = [R3[:, 1536 + 256 * s:1792 + 256 * s] for s in range(2)]
        gm = [R3[:, 2048 + 512 * s:2304 + 512 * s] for s in range(2)]
        gt = [R3[:, 2304 + 512 * s:2560 + 512 * s] for s in range(2)]
        cqn = mA[:, 0:768].rearrange("p (t n) -> p t n", t=NT)
        ckn = mA[:, 768:1408].rearrange("p (t n) -> p t n", t=NT)
        cqT = mA[:, 1408:2176].rearrange("p (k t) -> p k t", k=3)
        PT = mA[:, 0:1536].rearrange("p (h n) -> p h n", h=HEADS)
        moT = qnT
        cvg_flat = cvg[:, :, :].rearrange("p a b -> p (a b)")
        cvn = cvg_flat.rearrange("p (t n) -> p t n", t=NT)
        sq = cvg_flat[:, 0:QL]
        qraw = cvg_flat[:, 640:896].rearrange("p (a b) -> p a b", a=HEADS)
        rope1, rope2 = cvg_flat[:, 384:512], cvg_flat[:, 512:640]
        angle, turnsf = (R3[:, 64 * n:64 * n + 64].rearrange("p (t n) -> p t n", t=NT) for n in range(2))
        turnsi = R3[:, 128:192].bitcast(I32).rearrange("p (t n) -> p t n", t=NT)
        prob = [prob2[:, 0, :], prob2[:, 1, :], cvg_flat[:, 0:384], cvg_flat[:, 384:768]]
        W = [wbuf[:, s * W_SLOT:(s + 1) * W_SLOT] for s in range(2)]
        F = [wbuf[:, 2 * W_SLOT + s * F_SLOT:2 * W_SLOT + (s + 1) * F_SLOT] for s in range(2)]

        def col(name, k=0, half=False):
            tile, at, _ = ROWS[name]
            return (phalf if half else pcol)[:, tile, at + k:at + k + 1]

        bank_full = [S(f"bank_full{b}") for b in range(BANKS)]
        bank_free = [S(f"bank_free{b}") for b in range(BANKS)]
        F_gu_landed = [S(f"ffn_gate_up_landed{s}") for s in range(2)]
        F_d_landed = [S(f"ffn_down_landed{s}") for s in range(2)]
        F_gu_free = [S(f"ffn_gate_up_free{s}") for s in range(2)]
        F_d_free = [S(f"ffn_down_free{s}") for s in range(2)]
        W_landed = [S(f"unit_landed{s}") for s in range(2)]
        W_free = [S(f"unit_free{s}") for s in range(2)]
        all_in, all_out, met = S("all_in"), S("all_out"), S("met")

        def take(eng, job):
            eng.wait_ge(bank_full[BANK[job]], ROUND[job] + 1)

        def bank(job):
            return ps[BANK[job]]

        def read(eng, job):
            eng.wait_ge(bank_free[BANK[job]], ROUND[job] + 1)

        def free(job):
            return bank_free[BANK[job]]

        per_layer = [f"bank_full{b}" for b in range(BANKS)] + [f"bank_free{b}" for b in range(BANKS)] + [
            "gu_full", "ffn_tanh", "ffn_y", "ffn_act", "acc_full", "xn_ready", "tr_full", "hT_act", "hT_dve",
            "h_ready", "rows_full", "cols_ready", "half_ready",
            "glu_pad", "tap", "dn_zero", "dn_tap", "dn_tanh", "dn_silu", "z_tanh",
            "beta_tanh", "nabs", "ln_ready", "expa", "beta_ready", "g_ready", "eG_ready", "dG_ready", "eD_ready",
            "qk_norm", "kb_ready", "vb_ready", "kdec_ready", "trig", "dt_exp", "cq_ready", "ck_ready",
            "kr_ready", "qr_ready", "M_init", "lev_mask", "negmax", "exp_s", "p_ready", "o_ready",
            "cv_tanh", "cv_ready", "gate_full", "gate_act", "gate_sum", "gate_used"]
        for name in per_layer:
            S(name)
        clears = {"tensor": per_layer[0::4], "scalar": per_layer[1::4], "vector": per_layer[2::4],
                  "gpsimd": per_layer[3::4]}

        def meet(eng, who, l, steps):
            steps.sync()
            eng.sem_inc(all_in, 1)
            eng.wait_ge(all_in, l * 4 + 4)
            eng.sem_inc(met, 1)
            for name in clears[who]:
                eng.sem_clear(S(name))
            steps.restart()
            eng.sem_inc(all_out, 1)
            eng.wait_ge(all_out, l * 4 + 4)
            eng.sem_inc(met, 1)

        def rsqrt(dve, st, y, v, tmp):
            st.sync()
            st.step(dve.tensor_scalar(y.bitcast(I32), v.bitcast(I32), -0.5, 1597463007.0, ALU.mult, ALU.add))
            for _ in range(4):
                st.sync()
                st.step(dve.tensor_tensor(tmp, y, y, ALU.mult))
                st.sync()
                st.step(dve.scalar_tensor_tensor(tmp, tmp, -0.5, v, ALU.mult, ALU.mult))
                st.sync()
                st.step(dve.scalar_tensor_tensor(y, tmp, 1.5, y, ALU.add, ALU.mult))
            st.sync()


        rows2 = R2[:, 1024:1152]
        ramp_tab = R2[:, 0:1024].rearrange("p (h n) -> p h n", h=H2)
        toep = R2[:, 0:2048].rearrange("p (h n) -> p h n", h=H2)
        yacc = R2[:, 0:2048].rearrange("p (t n) -> p t n", t=NT)
        pflat = pcol[:, :, :].rearrange("p a b -> p (a b)")
        hflat = phalf[:, :, :].rearrange("p a b -> p (a b)")
        modc = pflat[:, 96:144]
        silc = pflat[:, 144:152]
        rbias = pflat[:, 160:196]
        lamc = pflat[:, 200:204]
        lam1 = pflat[:, 204:208]
        lam2 = pflat[:, 208:212]
        cvflat = cvpad[:, :, :].rearrange("p a b -> p (a b)")
        pflat2 = prob2[:, :, :].rearrange("p a b -> p (a b)")
        stage = [mA[:, RAMP * n:RAMP * (n + 1)] for n in range(5)] + [pflat2[:, 0:RAMP], pflat2[:, RAMP:2 * RAMP], cvflat[:, 0:RAMP]]
        xlpad = R1[:, 0:4 * (T + CONV - 1)].rearrange("p (c t) -> p c t", c=4)
        ada_acc = [R1[:, 1036 + 512 * n:1036 + 512 * (n + 1)] for n in range(4)]
        yl, xc = cvu, cvg
        gate_a, gate_x = qnT, knT
        decay = mv[:, :, :, :].rearrange("p t h j -> p (t h j)").rearrange("p (c t) -> p c t", c=4)
        lru = z[:, :, :, :].rearrange("p t h j -> p (t h j)").rearrange("p (c t) -> p c t", c=4)
        attn = decay
        spare = R3[:, 2048:3072].rearrange("p (c t) -> p c t", c=4)
        xn = R3[:, 0:2048].rearrange("p (t n) -> p t n", t=NT)
        wbd = qt[:, :, :, :].rearrange("p t h j -> p (t h) j")
        diag = kdec
        g1row = kt[:, :, :, :].rearrange("p t h j -> p (t h j)")
        g2row = vt[:, :, :, :].rearrange("p t h j -> p (t h j)")
        q2T = kT[:, :, :, :].rearrange("p t h j -> p (t h j)").rearrange("p (c t) -> p c t", c=4)
        k2T = kbT[:, :, :, :].rearrange("p t h j -> p (t h j)").rearrange("p (c t) -> p c t", c=4)
        v2 = qT[:, :, :, :].rearrange("p t h j -> p t (h j)")
        rms_v, rms_y, rms_t = krT[:, :], ckvT[:, 0, :], ckvT[:, 1, :]
        probs2 = R3[:, :].rearrange("p (h n) -> p h n", h=H2)
        PT2 = mA[:, 0:4 * 3 * P].rearrange("p (h n) -> p h n", h=4)
        nmax2 = hflat[:, 96:112].rearrange("p (h t) -> p h t", t=NT)
        sums2 = hflat[:, 112:128].rearrange("p (h t) -> p h t", t=NT)
        logit = cvflat[:, 400:472].rearrange("p (t n) -> p t n", t=NT)
        rt1, rt2, rt3, oh1, oh2, gate_e = (cvflat[:, 480 + 64 * n:544 + 64 * n].rearrange("p (t n) -> p t n", t=NT)
                                          for n in range(6))
        ohg = cvflat[:, 864:872].rearrange("p (t n) -> p t n", t=NT)
        rg1 = cvflat[:, 872:880].rearrange("p (t n) -> p t n", t=NT)
        rg2 = cvflat[:, 880:888].rearrange("p (t n) -> p t n", t=NT)
        rmx, rix, rs1, rs2, rs3, rm1 = (cvflat[:, 896 + 2 * n:898 + 2 * n] for n in range(6))
        moe_t = [qT[:, :, :, :].rearrange("p t h j -> p (t h j)")[:, 256 * n:256 * (n + 1)] for n in range(2)]
        moe_a = [[R3[:, 2048 + 512 * s + 256 * n:2304 + 512 * s + 256 * n] for n in range(2)] for s in range(2)]
        E = [wbuf[:, s * E_SLOT:(s + 1) * E_SLOT] for s in range(2)]
        E_landed = [S(f"expert_unit_landed{s}") for s in range(2)]
        E_free = [S(f"expert_unit_free{s}") for s in range(2)]
        D_landed = [S(f"expert_w2_landed{s}") for s in range(2)]
        D_free = [S(f"expert_w2_free{s}") for s in range(2)]
        ramp_dram = nc.dram_tensor("ramp", (H2, P, RAMP), F32, kind="Internal").ap()

        ADA_FIRST = 4
        UNITS2 = (["ada"] * 4 + ["x_lru", "y_lru", "ada", "ada", "q", "ada", "k", "ada", "v", "ada", "ada", "ada", "ada",
                  "w_out0", "w_out1", "router"])
        ada_units = [u for u, name in enumerate(UNITS2) if name == "ada"]
        assert len(ada_units) == 12 and len(UNITS2) % 2 == 0
        landed2 = []
        for u, name in enumerate(UNITS2):
            landed2.append((landed2[u - 2] if u >= 2 else 0) + (32 if name == "router" else 16))

        def land2(eng, name, n=0):
            u = [k for k, x in enumerate(UNITS2) if x == name][n]
            eng.wait_ge(E_landed[u % 2], landed2[u])
            return E[u % 2]

        def second_sync(sp):
            for s in range(2):
                sp.wait_ge(F_gu_free[s], DEPTH * NF + 1)
                sp.wait_ge(F_d_free[s], DEPTH * NF + 1)
                sp.wait_ge(W_free[s], DEPTH * UNITS_PER_SLOT + 1)
            w_ada = A["w_ada_2"][0].rearrange("(k p) n -> p k n", p=P)
            w_in2 = A["w_in_2"][0].rearrange("(k p) n -> p k n", p=P)
            w_out2 = A["w_out_2"][0].rearrange("(k p) n -> p k n", p=P)
            source = {"x_lru": w_in2[:, :, 0:512], "y_lru": w_in2[:, :, 512:1024], "q": w_in2[:, :, 1024:1536],
                      "k": w_in2[:, :, 1536:2048], "v": w_in2[:, :, 2048:2560], "w_out0": w_out2[:, :, 0:512],
                      "w_out1": w_out2[:, :, 512:1024]}
            stored = False
            n_ada = 0
            for u, name in enumerate(UNITS2):
                s = u % 2
                if u >= 2:
                    sp.wait_ge(E_free[s], u // 2)
                if name == "router":
                    sp.dma_start(E[s][:, 0:KD * 4].rearrange("p (k n) -> p k n", k=KD),
                                 A["w_router_group_2"][0].rearrange("(k p) n -> p k n", p=P)).then_inc(E_landed[s], 16)
                    sp.dma_start(E[s][:, 32:32 + KD * 32].rearrange("p (k n) -> p k n", k=KD),
                                 A["w_router_expert_2"][0].rearrange("(k p) n -> p k n", p=P)).then_inc(E_landed[s], 16)
                    continue
                src = source.get(name)
                if name == "ada":
                    src = w_ada[:, :, n_ada * 512:(n_ada + 1) * 512]
                    n_ada += 1
                sp.dma_start(E[s][:, 0:4096].rearrange("p (k n) -> p k n", k=KD), src).then_inc(E_landed[s], 16)
            with sp.Fori(0, EXPERTS // 2) as i:
                for s in range(2):
                    slot_wait2(sp, E_free[s], i + len(UNITS2) // 2)
                    for n, w in enumerate(("w1_2", "w3_2")):
                        sp.dma_start(E[s][:, n * 2048:(n + 1) * 2048].rearrange("p (k n) -> p k n", k=KD),
                                     A[w][0].rearrange("e (k p) n -> e p k n", p=P)[i * 2 + s]).then_inc(E_landed[s], 16)
                    slot_wait2(sp, D_free[s], i + 1)
                    sp.dma_start(E[s][:, 4096:6144].rearrange("p (k n) -> p k n", k=2),
                                 A["w2_2"][0].rearrange("e (k p) n -> e p k n", p=P)[i * 2 + s]).then_inc(D_landed[s], 16)
            sp.wait_ge(S("out_ready"), 2)
            sp.dma_start(out.rearrange("b (t p) d -> p (b t) d", p=P), h[:, :, :]).then_inc(S("out_stored"), 16)
            sp.wait_ge(S("out_stored"), 16)

        def slot_wait2(sp, sem, n):
            sp.wait_ge(sem, n)
            sp.sem_inc(S("sp_waited"), 1)

        def second_tensor(pe, mm, turn, owed, begin, end):
            meet(pe, "tensor", DEPTH, Steps(pe, S("pe_steps2")))

            def features(name, jobs, rhs):
                w = land2(pe, name)
                for n, job in enumerate(jobs):
                    b = begin(job)
                    for c in range(2):
                        for k in range(KD):
                            ins = mm(b[:, c * T:(c + 1) * T], w[:, k * 512 + (2 * n + c) * P:k * 512 + (2 * n + c + 1) * P],
                                     rhs[:, k, :], k == 0, k == KD - 1)
                    end(job, ins)
                owed.append(E_free[UNITS2.index(name) % 2])

            def ada(n):
                b = begin(f"ada{n}")
                pe.wait_ge(S("ada_acc"), n + 1)
                for c in range(4):
                    ins = mm(b[:, c:c + 1], ada_acc[n % 4][:, c * P:(c + 1) * P], ones[:, 0:1], True, True)
                end(f"ada{n}", ins)

            def turn_rows(prefix, sem):
                pe.wait_ge(sem, 2)
                for b4 in range(4):
                    b = begin(f"{prefix}{b4}")
                    for c in range(2):
                        for t in range(NT):
                            ins = turn(b[:, c * T + t * P:c * T + (t + 1) * P], xn[:, t, (2 * b4 + c) * P:(2 * b4 + c + 1) * P])
                    end(f"{prefix}{b4}", ins)

            def row_of(jobs, sem):
                for n, job in enumerate(jobs):
                    pe.wait_ge(sem, n + 1)
                    b = begin(job)
                    for c in range(4):
                        ins = mm(b[:, c * P:(c + 1) * P], ones[:, :], diag[:, c, :], True, True)
                    end(job, ins)

            pe.wait_ge(S("rows2_landed"), 16 * 9)
            b = begin("rows2")
            end("rows2", turn(b[:, 0:P], rows2))
            pe.wait_ge(S("ramp_tab"), 1)
            for hd in range(H2):
                b = begin(f"ramp{hd}")
                end(f"ramp{hd}", mm(b[:, 0:RAMP], ramp_tab[0:BUCKETS + 1, hd, :], cst[0:BUCKETS + 1, C_BUCKET:C_BUCKET + RAMP],
                                    True, True))
            for n in range(4):
                ada(n)
            turn_rows("u", S("xn2_ready"))
            for n in range(4):
                read(pe, f"u{n}")
            features("x_lru", ("xl0", "xl1"), hT)
            features("y_lru", ("yl0", "yl1"), hT)
            ada(4)
            ada(5)
            features("q", ("qq0", "qq1"), hT)
            ada(6)
            features("k", ("kk20", "kk21"), hT)
            ada(7)
            w = land2(pe, "v")
            for t in range(NT):
                b = begin(f"vv{t}")
                for k in range(KD):
                    ins = mm(b[:, :], hT[:, k, t * P:(t + 1) * P], w[:, k * 512:(k + 1) * 512], k == 0, k == KD - 1)
                end(f"vv{t}", ins)
            owed.append(E_free[UNITS2.index("v") % 2])
            row_of(("g1b0", "g1b1"), S("diag1"))
            pe.wait_ge(S("wbd_landed"), 32 * H2)
            pe.wait_ge(S("xc_ready"), 1)
            for n, name in enumerate(("ga", "gx")):
                for pr in range(2):
                    b = begin(f"{name}{pr}")
                    for c in range(2):
                        ins = mm(b[:, c * T:(c + 1) * T], wbd[:, n * 4 + 2 * pr + c, :], xc[:, 2 * pr + c, :], True, True)
                    end(f"{name}{pr}", ins)
            for job in ("qq0", "qq1", "kk20", "kk21", "vv0", "vv1"):
                read(pe, job)
            for hd in range(H2):
                b = begin(f"a{hd}")
                half = slice(64 * (hd % 2), 64 * (hd % 2) + 64)
                for t in range(NT):
                    n = (t + 1) * P
                    ins = mm(b[:, t * P:t * P + n], q2T[half, hd // 2, t * P:(t + 1) * P], k2T[half, hd // 2, 0:n], True, True)
                end(f"a{hd}", ins)
            pe.wait_ge(S("sq_ready"), 1)
            b = begin("rms0")
            for c in range(4):
                ins = mm(b[:, 0:T], ones[:, :], lsq[:, c, :], c == 0, c == 3)
            end("rms0", ins)
            for hd in range(H2):
                pe.wait_ge(S("p2_ready"), hd + 1)
                b = begin(f"b{hd}")
                for c in range(3):
                    ins = turn(b[:, c * P:(c + 1) * P], probs2[:, hd, c * P:(c + 1) * P])
                end(f"b{hd}", ins)
                if hd >= 1:
                    value(pe, mm, begin, end, hd - 1)
            value(pe, mm, begin, end, H2 - 1)
            pe.wait_ge(S("sq_ready"), 2)
            b = begin("rms1")
            for c in range(4):
                ins = mm(b[:, 0:T], ones[:, :], lsq[:, c, :], c == 0, c == 3)
            end("rms1", ins)
            for n in range(8, 12):
                ada(n)
            pe.wait_ge(S("merged2"), 8)
            for n in range(2):
                w = land2(pe, f"w_out{n}")
                for t in range(NT):
                    b = begin(f"wo{t}{n}")
                    for k in range(KD):
                        src = lru if k < 4 else attn
                        ins = mm(b[:, :], src[:, k % 4, t * P:(t + 1) * P], w[:, k * 512:(k + 1) * 512], k == 0, k == KD - 1)
                    end(f"wo{t}{n}", ins)
                owed.append(E_free[UNITS2.index(f"w_out{n}") % 2])
            row_of(("g2b0", "g2b1"), S("diag2"))
            turn_rows("w", S("xn3_ready"))
            for n in range(4):
                read(pe, f"w{n}")
            w = land2(pe, "router")
            b = begin("router")
            for t in range(NT):
                for at, width, src in ((0, GROUPS, w[:, 0:32]), (GROUPS, EXPERTS, w[:, 32:288])):
                    for k in range(KD):
                        ins = mm(b[:, t * 36 + at:t * 36 + at + width], hT[:, k, t * P:(t + 1) * P],
                                 src[:, k * width:(k + 1) * width], k == 0, k == KD - 1)
            end("router", ins)
            owed.append(E_free[1])
            read(pe, "router")

            def up(s, use, freed=None):
                pe.wait_ge(E_landed[s], use * 32 + landed2[-2 + s])
                for fc in range(2):
                    b = ps[2 * s + fc]
                    for n in range(2):
                        for k in range(KD):
                            ins = mm(b[:, n * T:(n + 1) * T], E[s][:, n * 2048 + k * DE + fc * P:n * 2048 + k * DE + (fc + 1) * P],
                                     hT[:, k, :], k == 0, k == KD - 1)
                            if freed is not None and (fc, n, k) == (0, 0, 0):
                                ins.then_inc(freed, 1)
                    ins.then_inc(S("up_full"), 1)

            def down2(e1, s, use, freed=None):
                pe.wait_ge(S("moe_act"), e1 * 2 + 2)
                pe.wait_ge(S("down_used"), e1)
                pe.wait_ge(D_landed[s], use * 16)
                for t in range(NT):
                    for n in range(2):
                        b = ps[4 + t * 2 + n]
                        for fc in range(2):
                            ins = mm(b[:, :], moe_a[s][fc][:, t * P:(t + 1) * P],
                                     E[s][:, 4096 + fc * D + n * 512:4096 + fc * D + (n + 1) * 512], fc == 0, fc == 1)
                            if freed is not None and (t, n, fc) == (0, 0, 0):
                                ins.then_inc(freed, 1)
                ins.then_inc(S("down_full"), 1)

            for s in range(2):
                pe.sem_inc(D_free[s], 1)
            pe.sem_inc(S("down_used"), 1)
            up(0, 1)
            up(1, 1, E_free[0])
            with pe.Fori(0, EXPERTS // 2 - 1) as i:
                down2(i * 2 + 1, 0, i + 1, E_free[1])
                up(0, i + 2, D_free[0])
                down2(i * 2 + 2, 1, i + 1, E_free[0])
                up(1, i + 2, D_free[1])
            down2(EXPERTS - 1, 0, EXPERTS // 2)
            down2(EXPERTS, 1, EXPERTS // 2)

        lsq = cvu

        def value(pe, mm, begin, end, hd):
            job = f"c{hd // 2}"
            b = begin(job) if hd % 2 == 0 else bank(job)
            read(pe, f"b{hd}")
            half = slice(64 * (hd % 2), 64 * (hd % 2) + 64)
            p = PT2[:, hd % 4, :]
            v = slice(hd * HD2, (hd + 1) * HD2)
            mm(b[half, 0:P], v2[:, 0, v], p[:, 0:P], True, True)
            mm(b[half, P:T], v2[:, 0, v], p[:, P:2 * P], True, False)
            ins = mm(b[half, P:T], v2[:, 1, v], p[:, 2 * P:3 * P], False, True)
            if hd % 2:
                end(job, ins)

        def second_scalar(act_, st, copy):
            sc = nc.scalar
            meet(act_, "scalar", DEPTH, st)
            take(act_, "rows2")
            sc.activation(pflat[:, 0:96], bank("rows2")[:, 0:96], ACT.Copy).then_inc(free("rows2"), 1)
            read(act_, "rows2")
            sc.activation(silc, pflat[:, 0:8], ACT.Tanh, scale=0.5).then_inc(S("sil_tanh"), 1)
            for hd in range(H2):
                copy(f"ramp{hd}", stage[hd], n=RAMP)
            for hd in range(H2):
                read(act_, f"ramp{hd}")
                act_.dma_start(ramp_dram[hd], stage[hd]).then_inc(S("ramp_stored"), 16)
            for n in range(4):
                take(act_, f"u{n}")
                for c in (2 * n, 2 * n + 1):
                    if n == 0 and c == 0:
                        act_.wait_ge(S("scale1"), 1)
                    ins = sc.activation(hT[:, c, :], bank(f"u{n}")[:, (c % 2) * T:(c % 2 + 1) * T], ACT.Identity,
                                        bias=modc[:, c:c + 1], scale=modc[:, 8 + c:9 + c])
                    if c % 2 == 0:
                        st.step(ins)
                ins.then_inc(free(f"u{n}"), 1)
            act_.wait_ge(S("ramp_stored"), 16 * H2)
            skew = bass.AP(ramp_dram.tensor, P - 1, [[RAMP - 1, P], [P * RAMP, H2], [1, T]])
            act_.dma_start(toep, skew).then_inc(S("toep_landed"), 16)
            act_.wait_ge(S("xl_zero"), 1)
            for n in range(2):
                copy(f"xl{n}", xlpad[:, 2 * n:2 * n + 2, CONV - 1:])
            for n in range(2):
                copy(f"yl{n}", yl[:, 2 * n:2 * n + 2, :])
            for n in range(2):
                copy(f"qq{n}", q2T[:, 2 * n:2 * n + 2, :])
            for n in range(2):
                copy(f"kk2{n}", k2T[:, 2 * n:2 * n + 2, :])
            for t in range(NT):
                copy(f"vv{t}", v2[:, t, :])
            for n in range(2):
                copy(f"g1b{n}", g1row[:, n * 512:(n + 1) * 512])
            for x, (name, dst, at) in enumerate((("ga", gate_a, 76), ("gx", gate_x, 80))):
                for n in range(2):
                    take(act_, f"{name}{n}")
                    for c in (2 * n, 2 * n + 1):
                        ins = sc.activation(dst[:, c, :], bank(f"{name}{n}")[:, (c % 2) * T:(c % 2 + 1) * T], ACT.Tanh,
                                            bias=hflat[:, at + c:at + c + 1], scale=0.5)
                        if c % 2 == 0:
                            st.step(ins)
                    ins.then_inc(free(f"{name}{n}"), 1)
            act_.wait_ge(S("lam_abs"), 1)
            st.step(sc.activation(lam2, lam2, ACT.Exp))
            st.sync()
            sc.activation(lam2, lam2, ACT.Ln, bias=1.0).then_inc(S("lam_ln"), 1)
            act_.wait_ge(S("log_a"), 1)
            sc.activation(decay, gate_a[:, :, :], ACT.Exp).then_inc(S("decay_ready"), 1)
            sc.activation(spare, gate_a[:, :, :], ACT.Tanh).then_inc(S("tanh_log_a"), 1)
            act_.wait_ge(S("gelu_in"), 1)
            sc.activation(gelu_t, gelu_t, ACT.Tanh, scale=0.7978845608028654).then_inc(S("gelu_tanh"), 1)
            act_.wait_ge(S("mult2"), 1)
            sc.activation(spare, spare, ACT.Sqrt).then_inc(S("mult_ready"), 1)
            for hd in range(H2):
                act_.wait_ge(S("negmax2"), hd + 1)
                for t in range(NT):
                    cols = slice(0, P) if t == 0 else slice(P, 3 * P)
                    sc.activation(probs2[:, hd, cols], probs2[:, hd, cols], ACT.Exp, bias=nmax2[:, hd, t:t + 1],
                                  accum_out=sums2[:, hd, t:t + 1]).then_inc(S("exp2"), 1)
            for hd in range(H2):
                if hd >= 4:
                    take(act_, f"c{(hd - 4) // 2}")
                copy(f"b{hd}", PT2[:, hd % 4, :], n=3 * P)
                if hd % 2 and hd >= 3:
                    copy(f"c{hd // 2 - 1}", attn[:, hd // 2 - 1, :], n=T)
            copy("c3", attn[:, 3, :], n=T)
            for n in range(2):
                copy(f"g2b{n}", g2row[:, n * 512:(n + 1) * 512])
            for n in range(4):
                take(act_, f"w{n}")
                for c in (2 * n, 2 * n + 1):
                    if c == 0:
                        act_.wait_ge(S("scale2"), 1)
                    ins = sc.activation(hT[:, c, :], bank(f"w{n}")[:, (c % 2) * T:(c % 2 + 1) * T], ACT.Identity,
                                        bias=modc[:, 24 + c:25 + c], scale=modc[:, 32 + c:33 + c])
                    if c % 2 == 0:
                        st.step(ins)
                ins.then_inc(free(f"w{n}"), 1)
            act_.wait_ge(S("group_shift"), 1)
            sc.activation(rg2, rg2, ACT.Exp).then_inc(S("group_exp"), 1)
            act_.wait_ge(S("pair_shift"), 1)
            sc.activation(rs2, rs2, ACT.Exp).then_inc(S("pair_exp"), 1)
            with act_.Fori(0, EXPERTS // 2) as i:
                for s in range(2):
                    for fc in range(2):
                        n = i * 4 + (2 * s + fc + 1)
                        act_.wait_ge(S("up_full"), n)
                        act_.wait_ge(S("moe_act"), n)
                        sc.activation(moe_t[fc], ps[2 * s + fc][:, 0:T], ACT.Tanh, scale=0.5).then_inc(S("moe_tanh"), 1)

        gelu_t = R1[:, 0:1024].rearrange("p (c t) -> p c t", c=4)

        def second_vector(dve, st):
            meet(dve, "vector", DEPTH, st)

            def rsq(y, v, tmp):
                rsqrt(dve, st, y, v, tmp)

            dve.wait_ge(S("rel_landed"), 16)
            dve.wait_ge(S("rel_mask"), 1)
            dve.tensor_copy(ramp_tab[0:BUCKETS + 1, :, :], rel[:, :].unsqueeze(2).broadcast_to([BUCKETS + 1, H2, P])
                            ).then_inc(S("ramp_tab"), 1)

            def moments(src, eps=EPS):
                for t in range(NT):
                    for n in range(2):
                        st.step(dve.bn_stats(stats[:, t, n, :], src[:, t, n * 512:(n + 1) * 512]))
                    st.sync()
                    st.step(dve.bn_aggr(mvar[:, t, :], stats[:, t, :, :].rearrange("p a b -> p (a b)")))
                st.sync()
                st.step(dve.tensor_scalar(rv[:, 0:NT], mvar[:, :, 1], eps, None, ALU.add))
                rsq(ry[:, 0:NT], rv[:, 0:NT], rt[:, 0:NT])

            def normed(dst, sem):
                for t in range(NT):
                    ins = dve.tensor_scalar(dst[:, t, :], h[:, t, :], mvar[:, t, 0:1], ry[:, t:t + 1], ALU.subtract, ALU.mult)
                    if sem is None:
                        st.step(ins)
                    else:
                        ins.then_inc(sem, 1)

            moments(h)
            normed(xn, S("xn2_ready"))
            read(dve, "rows2")
            st.step(dve.tensor_scalar(hflat[:, 0:96], pflat[:, 0:96], 0.5, None, ALU.mult))
            dve.wait_ge(S("sil_tanh"), 1)
            st.sync()
            st.step(dve.scalar_tensor_tensor(silc, silc, 1.0, hflat[:, 0:8], ALU.add, ALU.mult))
            st.sync()

            def ada(n):
                u = ada_units[n]
                w = E[u % 2]
                dve.wait_ge(E_landed[u % 2], landed2[u])
                if n >= 4:
                    take(dve, f"ada{n - 4}")
                acc = ada_acc[n % 4]
                st.step(dve.tensor_scalar(acc, w[:, 0:512], silc[:, 0:1], None, ALU.mult))
                for k in range(1, KD):
                    st.sync()
                    ins = dve.scalar_tensor_tensor(acc, w[:, k * 512:(k + 1) * 512], silc[:, k:k + 1], acc, ALU.mult, ALU.add)
                    if k < KD - 1:
                        st.step(ins)
                ins.then_inc(S("ada_acc"), 1)
                dve.wait_ge(S("ada_acc"), n + 1)
                dve.sem_inc(E_free[u % 2], 1)

            def ada_out(n):
                take(dve, f"ada{n}")
                dve.tensor_tensor(modc[:, 4 * n:4 * n + 4], bank(f"ada{n}")[:, 0:4], pflat[:, 8 + 4 * n:12 + 4 * n], ALU.add
                                  ).then_inc(free(f"ada{n}"), 1)

            def conv_tap(k, c):
                w = pflat[:, 56 + 4 * k + c:57 + 4 * k + c]
                src = xlpad[:, c, k:k + T]
                if k == 0:
                    return dve.tensor_scalar(xc[:, c, :], src, w, pflat[:, 72 + c:73 + c], ALU.mult, ALU.add)
                return dve.scalar_tensor_tensor(xc[:, c, :], src, w, xc[:, c, :], ALU.mult, ALU.add)

            for n in range(4):
                ada(n)
            for n in range(4):
                ada_out(n)
            read(dve, "ada3")
            dve.tensor_scalar(modc[:, 8:16], modc[:, 8:16], 1.0, None, ALU.add).then_inc(S("scale1"), 1)
            ada(4)
            ada(5)
            read(dve, "xl0")
            read(dve, "xl1")
            for k in range(CONV):
                for c in range(4):
                    if k:
                        st.sync(st.n - 3)
                    if (k, c) == (CONV - 1, 3):
                        conv_tap(k, c).then_inc(S("xc_ready"), 1)
                    else:
                        st.step(conv_tap(k, c))
            ada_out(4)
            ada_out(5)
            read(dve, "ada5")
            ada(6)
            ada(7)
            ada_out(6)
            ada_out(7)
            for half in range(2):
                if half:
                    take(dve, "g1b0")
                for c in range(4):
                    at = 16 + 4 * half + c
                    ins = dve.tensor_scalar(diag[:, c, :], ident, modc[:, at:at + 1], None, ALU.mult)
                    if c < 3:
                        st.step(ins)
                ins.then_inc(S("diag1"), 1)
            lam = pflat[:, 84:88]
            st.step(dve.tensor_scalar(lam1, lam, -1.0, None, ALU.mult))
            st.sync()
            dve.tensor_tensor(lam2, lam, lam1, ALU.min).then_inc(S("lam_abs"), 1)
            dve.wait_ge(S("lam_ln"), 1)
            st.step(dve.scalar_tensor_tensor(lamc, lam1, 0.0, lam2, ALU.max, ALU.add))
            st.sync()
            st.step(dve.tensor_scalar(lamc, lamc, -LRU_C / 2, None, ALU.mult))
            st.sync()
            for n in range(2):
                read(dve, f"ga{n}")
            for c in range(4):
                ins = dve.tensor_scalar(gate_a[:, c, :], gate_a[:, c, :], 1.0, lamc[:, c:c + 1], ALU.add, ALU.mult)
                if c < 3:
                    st.step(ins)
            ins.then_inc(S("log_a"), 1)
            for n in range(2):
                read(dve, f"yl{n}")
            dve.wait_ge(S("xc_ready"), 1)
            st.step(dve.tensor_tensor(gelu_t, yl[:, :, :], yl[:, :, :], ALU.mult))
            st.sync()
            st.step(dve.tensor_scalar(gelu_t, gelu_t, 0.044715, 1.0, ALU.mult, ALU.add))
            st.sync()
            dve.tensor_tensor(gelu_t, gelu_t, yl[:, :, :], ALU.mult).then_inc(S("gelu_in"), 1)
            dve.wait_ge(S("tanh_log_a"), 1)
            st.step(dve.tensor_scalar(gate_a[:, :, :], spare, -1.0, 1.0, ALU.mult, ALU.add))
            st.sync()
            st.step(dve.reciprocal(gate_a[:, :, :], gate_a[:, :, :]))
            st.sync()
            dve.scalar_tensor_tensor(spare, spare, -2.0, gate_a[:, :, :], ALU.mult, ALU.mult).then_inc(S("mult2"), 1)
            for n in range(2):
                read(dve, f"gx{n}")
            st.step(dve.scalar_tensor_tensor(gate_x[:, :, :], gate_x[:, :, :], 1.0, xc[:, :, :], ALU.add, ALU.mult))
            st.sync()
            dve.wait_ge(S("mult_ready"), 1)
            st.step(dve.scalar_tensor_tensor(gate_x[:, :, :], gate_x[:, :, :], 0.5, spare, ALU.mult, ALU.mult))
            st.sync()
            dve.wait_ge(S("decay_ready"), 1)
            for c in range(4):
                st.step(dve.tensor_tensor_scan(lru[:, c, :], decay[:, c, :], gate_x[:, c, :], 0.0, ALU.mult, ALU.add))
            dve.wait_ge(S("gelu_tanh"), 1)
            st.step(dve.scalar_tensor_tensor(yl[:, :, :], gelu_t, 1.0, yl[:, :, :], ALU.add, ALU.mult))
            st.sync()
            st.step(dve.scalar_tensor_tensor(lru, lru, 0.5, yl[:, :, :], ALU.mult, ALU.mult))
            st.sync()
            dve.tensor_tensor(lsq[:, :, :], lru, lru, ALU.mult).then_inc(S("sq_ready"), 1)

            def rms(job, x, at):
                take(dve, job)
                dve.tensor_scalar(rms_v, bank(job)[:, 0:T], 1.0 / DL, EPS, ALU.mult, ALU.add).then_inc(free(job), 1)
                read(dve, job)
                rsq(rms_y, rms_v, rms_t)
                for c in range(4):
                    dve.scalar_tensor_tensor(x[:, c, :], x[:, c, :], pflat[:, at + c:at + c + 1], rms_y, ALU.mult, ALU.mult
                                             ).then_inc(S("merged2"), 1)

            dve.wait_ge(S("toep_landed"), 16)
            for hd in range(H2):
                take(dve, f"a{hd}")
                b = bank(f"a{hd}")
                st.step(dve.scalar_tensor_tensor(probs2[:, hd, 0:P], b[:, 0:P], HD2 ** -0.5, toep[:, hd, P:T], ALU.mult, ALU.add))
                dve.scalar_tensor_tensor(probs2[:, hd, P:3 * P], b[:, P:3 * P], HD2 ** -0.5, toep[:, hd, :], ALU.mult, ALU.add
                                         ).then_inc(free(f"a{hd}"), 1)
                read(dve, f"a{hd}")
                st.step(dve.tensor_reduce(nmax2[:, hd, 0:1], probs2[:, hd, 0:P], AX, ALU.max))
                st.step(dve.tensor_reduce(nmax2[:, hd, 1:2], probs2[:, hd, P:3 * P], AX, ALU.max))
                st.sync()
                dve.tensor_scalar(nmax2[:, hd, :], nmax2[:, hd, :], -1.0, None, ALU.mult).then_inc(S("negmax2"), 1)
            rms("rms0", lru, 88)
            for hd in range(H2):
                dve.wait_ge(S("exp2"), 2 * hd + 2)
                st.step(dve.reciprocal(sums2[:, hd, :], sums2[:, hd, :]))
                st.sync()
                st.step(dve.tensor_scalar(probs2[:, hd, 0:P], probs2[:, hd, 0:P], sums2[:, hd, 0:1], None, ALU.mult))
                dve.tensor_scalar(probs2[:, hd, P:3 * P], probs2[:, hd, P:3 * P], sums2[:, hd, 1:2], None, ALU.mult
                                  ).then_inc(S("p2_ready"), 1)
            for c in range(4):
                read(dve, f"c{c}")
            dve.tensor_tensor(lsq[:, :, :], attn, attn, ALU.mult).then_inc(S("sq_ready"), 1)
            for n in range(8, 12):
                ada(n)
            rms("rms1", attn, 92)
            for n in range(8, 12):
                ada_out(n)
            read(dve, "ada11")
            dve.tensor_scalar(modc[:, 32:40], modc[:, 32:40], 1.0, None, ALU.add).then_inc(S("scale2"), 1)
            for half in range(2):
                take(dve, "g2b0" if half else "g1b1")
                for c in range(4):
                    at = 40 + 4 * half + c
                    ins = dve.tensor_scalar(diag[:, c, :], ident, modc[:, at:at + 1], None, ALU.mult)
                    if c < 3:
                        st.step(ins)
                ins.then_inc(S("diag2"), 1)
            read(dve, "g1b0")
            read(dve, "g1b1")
            for n in range(2):
                for t in range(NT):
                    job = f"wo{t}{n}"
                    take(dve, job)
                    part = h[:, t, n * 512:(n + 1) * 512]
                    tmp = xn[:, t, n * 512:(n + 1) * 512]
                    dve.tensor_tensor(tmp, bank(job)[:, :], g1row[:, n * 512:(n + 1) * 512], ALU.mult).then_inc(free(job), 1)
                    read(dve, job)
                    st.step(dve.scalar_tensor_tensor(part, part, ALPHA_2, tmp, ALU.mult, ALU.add))
            st.sync()
            moments(h)
            normed(h, None)
            st.sync()
            dve.wait_ge(S("gain2_landed"), 32)
            affine(dve, st)
            st.sync()
            moments(h)
            normed(xn, S("xn3_ready"))
            dve.wait_ge(S("xn3_ready"), 2)
            dve.sem_inc(S("gain_used"), 1)
            take(dve, "router")
            dve.wait_ge(S("rbias_landed"), 32)
            dve.tensor_tensor(logit, bank("router")[:, 0:72].rearrange("p (t n) -> p t n", t=NT),
                              rbias.unsqueeze(1).broadcast_to([P, NT, 36]), ALU.add).then_inc(free("router"), 1)
            read(dve, "router")

            def wide(x, n):
                return x.unsqueeze(2).broadcast_to([P, NT, n])

            def first_max(src, n, mx, t1, dst):
                iota = cst[:, C_IOTA:C_IOTA + n].unsqueeze(1).broadcast_to([P, NT, n])
                st.sync()
                st.step(dve.tensor_reduce(mx, src, AX, ALU.max))
                st.sync()
                st.step(dve.tensor_tensor(t1, src, wide(mx, n), ALU.is_lt))
                st.sync()
                st.step(dve.scalar_tensor_tensor(t1, t1, 100.0, iota, ALU.mult, ALU.add))
                st.sync()
                st.step(dve.tensor_reduce(rix, t1, AX, ALU.min))
                st.sync()
                st.step(dve.tensor_tensor(dst, iota, wide(rix, n), ALU.is_equal))
                st.sync()

            first_max(logit[:, :, 0:4], GROUPS, rmx, rg1, ohg)
            dve.tensor_tensor(rg2, logit[:, :, 0:4], wide(rmx, 4), ALU.subtract).then_inc(S("group_shift"), 1)
            dve.wait_ge(S("group_exp"), 1)
            st.step(dve.tensor_reduce(rs1, rg2, AX, ALU.add))
            st.sync()
            st.step(dve.reciprocal(rs1, rs1))
            st.step(dve.tensor_scalar(rg1, ohg, 1.0, 1e30, ALU.subtract, ALU.mult))
            st.sync()
            for t in range(NT):
                st.step(dve.tensor_tensor(rt1[:, t, :].rearrange("p (g n) -> p g n", g=GROUPS),
                                          logit[:, t, 4:36].rearrange("p (g n) -> p g n", g=GROUPS),
                                          rg1[:, t, :].unsqueeze(2).broadcast_to([P, GROUPS, PER_GROUP]), ALU.add))
            first_max(rt1, EXPERTS, rm1, rt2, oh1)
            st.step(dve.scalar_tensor_tensor(rt3, oh1, -3e30, rt1, ALU.mult, ALU.add))
            first_max(rt3, EXPERTS, rmx, rt2, oh2)
            dve.tensor_tensor(rs2, rmx, rm1, ALU.subtract).then_inc(S("pair_shift"), 1)
            dve.wait_ge(S("pair_exp"), 1)
            st.step(dve.tensor_scalar(rs3, rs2, 1.0, None, ALU.add))
            st.sync()
            st.step(dve.reciprocal(rs3, rs3))
            st.sync()
            st.step(dve.tensor_tensor(rs3, rs3, rs1, ALU.mult))
            st.sync()
            st.step(dve.tensor_tensor(rs2, rs2, rs3, ALU.mult))
            st.sync()
            st.step(dve.tensor_tensor(rt1, oh1, wide(rs3, EXPERTS), ALU.mult))
            st.step(dve.tensor_tensor(rt2, oh2, wide(rs2, EXPERTS), ALU.mult))
            st.sync()
            st.step(dve.tensor_tensor(gate_e, rt1, rt2, ALU.add))
            st.step(dve.memset(yacc, 0.0))
            st.sync()
            dve.sem_inc(S("moe_act"), 2)
            with dve.Fori(0, EXPERTS // 2) as i:
                for s in range(2):
                    for fc in range(2):
                        n = i * 4 + (2 * s + fc + 1)
                        b = ps[2 * s + fc]
                        dve.wait_ge(S("moe_tanh"), n)
                        dve.scalar_tensor_tensor(moe_t[fc], moe_t[fc], 1.0, b[:, 0:T], ALU.add, ALU.mult).then_inc(S("moe_y"), 1)
                        dve.wait_ge(S("moe_y"), n)
                        dve.scalar_tensor_tensor(moe_a[s][fc], moe_t[fc], 0.5, b[:, T:2 * T], ALU.mult, ALU.mult
                                                 ).then_inc(S("moe_act"), 1)
                    dve.wait_ge(S("down_full"), i * 2 + (s + 1))
                    for t in range(NT):
                        for n in range(2):
                            acc = yacc[:, t, n * 512:(n + 1) * 512]
                            ins = dve.scalar_tensor_tensor(acc, ps[4 + 2 * t + n][:, :], gate_e[:, t, ds(i * 2 + s, 1)], acc,
                                                           ALU.mult, ALU.add)
                            if (t, n) == (1, 1):
                                ins.then_inc(S("down_used"), 1)
            dve.wait_ge(S("down_used"), EXPERTS + 1)
            read(dve, "g2b0")
            read(dve, "g2b1")
            for t in range(NT):
                st.step(dve.tensor_tensor(yacc[:, t, :], yacc[:, t, :], g2row, ALU.mult))
                st.sync()
                st.step(dve.scalar_tensor_tensor(h[:, t, :], h[:, t, :], ALPHA_2, yacc[:, t, :], ALU.mult, ALU.add))
            st.sync()
            moments(h)
            normed(h, None)
            st.sync()
            dve.wait_ge(S("gain2_landed"), 64)
            for t in range(NT):
                st.step(dve.tensor_tensor(h[:, t, :], h[:, t, :], gain[:, :], ALU.mult))
                st.sync()
                dve.tensor_tensor(h[:, t, :], h[:, t, :], bias[:, :], ALU.add).then_inc(S("out_ready"), 1)

        def affine(dve, st):
            for t in range(NT):
                st.step(dve.tensor_tensor(h[:, t, :], h[:, t, :], gain[:, :], ALU.mult))
                st.sync()
                st.step(dve.tensor_tensor(h[:, t, :], h[:, t, :], bias[:, :], ALU.add))

        def second_pool(pool, st):
            meet(pool, "gpsimd", DEPTH, st)
            st.step(pool.memset(rows2, 0.0))
            st.sync()
            at = 0
            for name, src in (("c", A["c_2"].rearrange("b (c p) -> (b c) p", p=P)),
                              ("ada", A["b_ada_2"].rearrange("l (c p) -> (l c) p", p=P)),
                              ("conv", A["conv_w_2"].rearrange("l k (c p) -> (l k c) p", p=P)),
                              ("conv_b", A["conv_b_2"].rearrange("l (c p) -> (l c) p", p=P)),
                              ("ba", A["b_gate_a_2"].rearrange("l (c two) n -> (l c) (two n)", two=2)),
                              ("bx", A["b_gate_x_2"].rearrange("l (c two) n -> (l c) (two n)", two=2)),
                              ("lam", A["lru_lambda_2"].rearrange("l (c p) -> (l c) p", p=P)),
                              ("nl", A["norm_lru_g_2"].rearrange("l (c p) -> (l c) p", p=P)),
                              ("na", A["norm_attn_g_2"].rearrange("l (c p) -> (l c) p", p=P))):
                n = src.shape[0]
                pool.dma_start(rows2[at:at + n, :], src).then_inc(S("rows2_landed"), 16)
                at += n
            assert at == 96
            pool.dma_start(rel[0:BUCKETS, :], A["rel_bias_2"]).then_inc(S("rel_landed"), 16)
            pool.memset(rel[BUCKETS:BUCKETS + 1, :], MASKED).then_inc(S("rel_mask"), 1)
            pool.wait_ge(S("rel_mask"), 1)
            st.step(pool.memset(wbd, 0.0))
            pool.memset(xlpad[:, :, 0:CONV - 1], 0.0).then_inc(S("xl_zero"), 1)
            st.sync()
            for n, name in enumerate(("w_gate_a_2", "w_gate_x_2")):
                for b in range(H2):
                    half = slice(64 * (b % 2), 64 * (b % 2) + 64)
                    pool.dma_start(wbd[half, 4 * n + b // 2, half], A[name][0, b]).then_inc(S("wbd_landed"), 16)
            for dst, name in ((gain, "ln1_g_2"), (bias, "ln1_b_2")):
                pool.dma_start(dst[:, :], A[name].broadcast_to([P, D])).then_inc(S("gain2_landed"), 16)
            pool.wait_ge(S("gain2_landed"), 32)
            read(pool, "rows2")
            for at, n, name in ((0, GROUPS, "b_router_group_2"), (GROUPS, EXPERTS, "b_router_expert_2")):
                pool.dma_start(rbias[:, at:at + n], A[name].broadcast_to([P, n])).then_inc(S("rbias_landed"), 16)
            pool.wait_ge(S("gain_used"), 1)
            for dst, name in ((gain, "ln2_g_2"), (bias, "ln2_b_2")):
                pool.dma_start(dst[:, :], A[name].broadcast_to([P, D])).then_inc(S("gain2_landed"), 16)


        block = ctx.enter_context(nc.Block())

        @block.sync
        def _(sp):
            def slot_wait(sem, n):
                sp.wait_ge(sem, n)
                sp.sem_inc(S("sp_waited"), 1)

            sp.dma_start(cst[:, :], A["const"]).then_inc(S("const_landed"), 16)
            sp.dma_start(h[:, :, :], A["x"].rearrange("b (t p) d -> p (b t) d", p=P)).then_inc(S("x_landed"), 16)

            def ffn_weights(l, f):
                wg, wu, wd = A[f"ffn{f + 1}_w_gate"], A[f"ffn{f + 1}_w_up"], A[f"ffn{f + 1}_w_down"]
                with sp.Fori(0, NF // 2) as i:
                    use = l * NF + i + (f * (NF // 2) + 1)
                    for s in range(2):
                        cols = ds(i * (2 * P) + s * P, P)
                        slot_wait(F_gu_free[s], use)
                        for n, w in enumerate((wg, wu)):
                            sp.dma_start(F[s][:, n * D:(n + 1) * D].rearrange("p (k n) -> p k n", k=KD),
                                         w[l].rearrange("(k p) n -> p k n", p=P)[:, :, cols]).then_inc(F_gu_landed[s], 16)
                        slot_wait(F_d_free[s], use)
                        sp.dma_start(F[s][:, 2 * D:3 * D], wd[l, cols, :]).then_inc(F_d_landed[s], 16)

            w_in = A["w_in"].rearrange("l (k p) n -> l p k n", p=P)

            def unit(l, u, src, cols, at=0, wait=True):
                s = u % 2
                if wait:
                    slot_wait(W_free[s], l * UNITS_PER_SLOT + (u // 2 + 1))
                k = src.shape[1]
                sp.dma_start(W[s][:, at:at + k * cols].rearrange("p (k n) -> p k n", k=k), src).then_inc(W_landed[s], 16)

            with sp.Fori(0, DEPTH) as l:
                ffn_weights(l, 0)
                win = w_in[l]
                for u, (at, n) in enumerate(((OFF_GLU, 512), (OFF_GLU + 512, 512), (0, 512), (512, 512), (1024, 512),
                                             (OFF_Z, 520), (OFF_CQ, QL), (OFF_CKV, KVL + ROPE))):
                    unit(l, u, win[:, :, at:at + n], n)
                unit(l, 8, A["mla_w_uq"][l].rearrange("(k p) n -> p k n", p=P), HEADS * (NOPE + ROPE))
                unit(l, 9, A["mla_w_ukv"][l].rearrange("(k p) n -> p k n", p=P), HEADS * (NOPE + VD))
                with sp.Fori(0, KD // 2) as i:
                    for s in range(2):
                        slot_wait(W_free[s], l * UNITS_PER_SLOT + i + 6)
                        for b, w in enumerate(("dn_w_o", "cv_w_pw2", "mla_w_o")):
                            sp.dma_start(W[s][:, b * D:(b + 1) * D].rearrange("p (k n) -> p k n", k=KD),
                                         win[:, :, ds(i * (2 * P) + (OFF_GATE + b * D + s * P), P)]).then_inc(W_landed[s], 16)
                            sp.dma_start(W[s][:, 3 * D + b * 512:3 * D + (b + 1) * 512].rearrange("p (k n) -> p k n", k=4),
                                         A[w][l].rearrange("(k p) n -> p k n", p=P)[:, :, ds(i * (2 * P) + s * P, P)]
                                         ).then_inc(W_landed[s], 16)
                for n in range(2):
                    unit(l, 18 + n, A["w_out"][l].rearrange("(k p) n -> p k n", p=P)[:, :, n * 512:(n + 1) * 512], 512)
                ffn_weights(l, 1)
            second_sync(sp)

        @block.tensor
        def _(pe):
            owed = []

            def mm(out_, lhsT, rhs, start, stop):
                ins = pe.matmul(out_, lhsT, rhs, start=start, stop=stop)
                if owed:
                    ins.then_inc(owed.pop(0), 1)
                return ins

            def turn(out_, in_, n=P):
                ins = pe.transpose(out_, in_, ident[0:n, 0:n])
                if owed:
                    ins.then_inc(owed.pop(0), 1)
                return ins

            def begin(job):
                if ROUND[job]:
                    pe.wait_ge(bank_free[BANK[job]], ROUND[job])
                return ps[BANK[job]]

            def end(job, ins):
                ins.then_inc(bank_full[BANK[job]], 1)

            def gate_up(c, s, use, first=False, base=0):
                pe.wait_ge(F_gu_landed[s], use * 32)
                if not first:
                    pe.wait_ge(S("ffn_act"), c + (base - 1))
                for n in range(2):
                    for k in range(KD):
                        ins = mm(ps[4 + s][:, n * T:(n + 1) * T], F[s][:, n * D + k * P:n * D + (k + 1) * P],
                                 hT[:, k, :], k == 0, k == KD - 1)
                ins.then_inc(S("gu_full"), 1)
                owed.append(F_gu_free[s])

            def down(c, s, use, start=False, stop=False, base=0):
                pe.wait_ge(F_d_landed[s], use * 16)
                pe.wait_ge(S("ffn_act"), c + (base + 1))
                for t in range(NT):
                    for n in range(2):
                        ins = mm(ps[t * 2 + n][:, :], act[s][:, t * P:(t + 1) * P],
                                 F[s][:, 2 * D + n * 512:2 * D + (n + 1) * 512], start, stop)
                if stop:
                    ins.then_inc(S("acc_full"), 1)
                    owed.append(F_d_free[s])
                else:
                    ins.then_inc(F_d_free[s], 1)

            def ffn(l, f):
                use = l * NF + (f * (NF // 2) + 1)
                b = f * NF
                gate_up(0, 0, use, first=True)
                gate_up(1, 1, use, first=True)
                down(0, 0, use, start=True, base=b)
                with pe.Fori(0, NF // 2 - 1) as i:
                    c = i * 2
                    gate_up(c, 0, use + i + 1, base=b + 2)
                    down(c, 1, use + i, base=b + 1)
                    gate_up(c, 1, use + i + 1, base=b + 3)
                    down(c, 0, use + i + 1, base=b + 2)
                down(NF - 1, 1, use + (NF // 2 - 1), stop=True, base=b)

            def turn_h(k):
                for t in range(NT):
                    pe.wait_ge(S("xn_ready"), NT * k + t + 1)
                    for c in range(KD):
                        ins = turn(ps[4 + c // 2][:, (c % 2) * T + t * P:(c % 2) * T + (t + 1) * P],
                                   h[:, t, c * P:(c + 1) * P])
                        if t == NT - 1 and c % 2:
                            ins.then_inc(S("tr_full"), 1)

            def hT_wait(k):
                pe.wait_ge(S("hT_act"), k)
                pe.wait_ge(S("hT_dve"), k)

            def land(l, u):
                pe.wait_ge(W_landed[u % 2], l * LANDED_PER_LAYER[u % 2] + LANDED[u])

            def features(l, u, jobs, width, K, rhs, offs):
                land(l, u)
                for n, job in enumerate(jobs):
                    b = begin(job)
                    for c in range(2):
                        off = offs[2 * n + c]
                        for k in range(K):
                            ins = mm(b[:, c * T:(c + 1) * T], W[u % 2][:, k * width + off:k * width + off + P],
                                     rhs[:, k, :], k == 0, k == K - 1)
                    end(job, ins)

            def tokens(l, u, jobs, width, K, lhs, a, n):
                for t, job in enumerate(jobs):
                    b = begin(job)
                    for k in range(K):
                        ins = mm(b[:, 0:n], lhs[:, k, t * P:(t + 1) * P],
                                 W[u % 2][:, k * width + a:k * width + a + n], k == 0, k == K - 1)
                    end(job, ins)

            def turns(job, blocks):
                b = begin(job)
                for at, src in blocks:
                    ins = turn(b[:, at:at + P], src)
                end(job, ins)

            def heads(job, lhs, rhs):
                b = begin(job)
                for hd in range(HEADS):
                    ins = mm(b[:, hd * P:(hd + 1) * P], lhs(hd), rhs(hd), True, True)
                end(job, ins)

            for s in range(2):
                for q in (F_gu_free[s], F_d_free[s], W_free[s]):
                    pe.sem_inc(q, 1)
            pe.wait_ge(S("const_landed"), 16)
            pe.wait_ge(S("x_landed"), 16)
            for c in range(KD):
                for t in range(NT):
                    ins = turn(ps[4 + c // 2][:, (c % 2) * T + t * P:(c % 2) * T + (t + 1) * P], h[:, t, c * P:(c + 1) * P])
                if c % 2:
                    ins.then_inc(S("x_turned"), 1)

            with pe.Fori(0, DEPTH) as l:
                meet(pe, "tensor", l, Steps(pe, S("pe_steps")))
                ffn(l, 0)
                pe.wait_ge(S("rows_landed"), l * (16 * len(ROWS)) + 16 * len(ROWS))
                for a in range(3):
                    ins = turn(ps[6][:, a * P:(a + 1) * P], prow[:, a, :])
                ins.then_inc(S("rows_full"), 1)
                pe.wait_ge(S("cols_ready"), 1)
                turn_h(0)
                hT_wait(1)

                for u, jobs in enumerate((("gv0", "gv1"), ("gg0", "gg1"), ("q0", "q1"), ("k0", "k1"), ("v0", "v1"))):
                    features(l, u, jobs, 512, KD, hT, [0, P, 2 * P, 3 * P])
                    owed.append(W_free[u % 2])
                land(l, 5)
                tokens(l, 5, ("z0", "z1"), 520, KD, hT, 0, 512)
                b = begin("ab")
                for t in range(NT):
                    for k in range(KD):
                        ins = mm(b[:, t * 8:(t + 1) * 8], hT[:, k, t * P:(t + 1) * P],
                                 W[1][:, k * 520 + 512:k * 520 + 520], k == 0, k == KD - 1)
                end("ab", ins)
                owed.append(W_free[1])
                land(l, 6)
                tokens(l, 6, ("cq0", "cq1"), QL, KD, hT, 0, QL)
                owed.append(W_free[0])
                land(l, 7)
                tokens(l, 7, ("ck0", "ck1"), KVL + ROPE, KD, hT, 0, KVL + ROPE)
                owed.append(W_free[1])

                b = begin("G")
                pe.wait_ge(S("g_ready"), 1)
                for t in range(NT):
                    mm(b[:, t * 8:t * 8 + 4], tri, g[:, t, :], True, True)
                    ins = mm(b[:, t * 8 + 4:t * 8 + 8], ones[:, :], g[:, t, :], True, True)
                end("G", ins)
                for x, part in enumerate("qkv"):
                    pe.wait_ge(S("dn_silu"), x + 1)
                    for t in range(NT):
                        turns(f"tok_{part}{t}", [(hd * P, dn[:, x * 4 + hd, t * P:(t + 1) * P]) for hd in range(HEADS)])
                pe.wait_ge(S("cq_ready"), 2)
                turns("cqTa", [(c * T + t * P, cqn[:, t, c * P:(c + 1) * P]) for c in range(2) for t in range(NT)])
                turns("cqTb", [(t * P, cqn[:, t, 2 * P:3 * P]) for t in range(NT)])
                pe.wait_ge(S("ck_ready"), 2)
                turns("ckvT", [(c * T + t * P, ckn[:, t, c * P:(c + 1) * P]) for c in range(2) for t in range(NT)])
                pe.wait_ge(S("kr_ready"), 1)
                turns("krT", [(t * P, krd[:, t, :, :].rearrange("p a b -> p (a b)")) for t in range(NT)])
                for t in range(NT):
                    b = begin(f"Gb{t}")
                    pe.wait_ge(S("trig"), 1)
                    end(f"Gb{t}", mm(b[:, :], ones[:, :], Pm[:, t, :, :].rearrange("p h j -> p (h j)"), True, True))
                for job in ("cqTa", "cqTb", "ckvT"):
                    read(pe, job)
                features(l, 8, ("qn0", "qn1"), HEADS * (NOPE + ROPE), 3, cqT, [hd * (NOPE + ROPE) for hd in range(HEADS)])
                b = begin("qr")
                uq = W[0][:, 0:3 * HEADS * (NOPE + ROPE)].rearrange("p (k h n) -> p k h n", k=3, h=HEADS)
                for t in range(NT):
                    for k in range(3):
                        ins = mm(b[:, t * T:(t + 1) * T], cqT[:, k, t * P:(t + 1) * P], uq[:, k, :, NOPE:], k == 0, k == 2)
                end("qr", ins)
                owed.append(W_free[0])
                pe.wait_ge(S("qk_norm"), 2)
                for t in range(NT):
                    turns(f"qT{t}", [(hd * P, qt[:, t, hd, :]) for hd in range(HEADS)])
                for t in range(NT):
                    turns(f"kT{t}", [(hd * P, kt[:, t, hd, :]) for hd in range(HEADS)])
                pe.wait_ge(S("kb_ready"), 1)
                for t in range(NT):
                    turns(f"kbT{t}", [(hd * P, kb[:, t, hd, :]) for hd in range(HEADS)])
                features(l, 9, ("kn0", "kn1"), HEADS * (NOPE + VD), 2, ckvT, [hd * (NOPE + VD) for hd in range(HEADS)])
                ukv = W[1][:, 0:2 * HEADS * (NOPE + VD)].rearrange("p (k h n) -> p k h n", k=2, h=HEADS)
                for t in range(NT):
                    b = begin(f"mv{t}")
                    for k in range(2):
                        ins = mm(b[:, :], ckvT[:, k, t * P:(t + 1) * P], ukv[:, k, :, NOPE:], k == 0, k == 1)
                    end(f"mv{t}", ins)
                owed.append(W_free[1])
                for job in ("qT0", "qT1", "kT0", "kT1", "kbT0", "kbT1"):
                    read(pe, job)
                for t in range(NT):
                    heads(f"kk{t}", lambda hd: kT[:, t, hd, :], lambda hd: kbT[:, t, hd, :])
                for t in range(NT):
                    heads(f"qk{t}", lambda hd: kT[:, t, hd, :], lambda hd: qT[:, t, hd, :])
                pe.wait_ge(S("qr_ready"), 2)
                turns("qrT", [(pr * T + t * P, qr[:, t, 2 * pr:2 * pr + 2, :].rearrange("p a b -> p (a b)"))
                              for pr in range(2) for t in range(NT)])
                for job in ("qn0", "qn1", "kn0", "kn1", "krT", "qrT"):
                    read(pe, job)
                for hd in range(HEADS):
                    b = begin(f"s{hd}")
                    half = slice(64 * (hd % 2), 64 * (hd % 2) + 64)
                    for t in range(NT):
                        n = (t + 1) * P
                        o_ = b[:, t * P:t * P + n]
                        mm(o_, qnT[:, hd, t * P:(t + 1) * P], knT[:, hd, 0:n], True, False)
                        ins = mm(o_, qrT[half, hd // 2, t * P:(t + 1) * P], krT[half, 0:n], False, True)
                    end(f"s{hd}", ins)
                for lev in range(LEVELS):
                    for t in range(NT):
                        pe.wait_ge(S("lev_mask"), NT * lev + t + 1)
                        if lev:
                            read(pe, f"MP{t}.{lev - 1}")
                        else:
                            pe.wait_ge(S("M_init"), 2)
                        heads(f"P{t}.{lev}", lambda hd: ATl[lev % 2][:, t, hd, :], lambda hd: M[:, t, hd, :])
                    for t in range(NT):
                        read(pe, f"P{t}.{lev}")
                        if lev:
                            read(pe, f"MPT{t}.{lev - 1}")
                        heads(f"MP{t}.{lev}", lambda hd: MT[:, t, hd, :], lambda hd: Pm[:, t, hd, :])
                        heads(f"MPT{t}.{lev}", lambda hd: Pm[:, t, hd, :], lambda hd: MT[:, t, hd, :])
                for hd in range(HEADS):
                    pe.wait_ge(S("p_ready"), hd + 1)
                    turns(f"p{hd}", [(c * P, prob[hd][:, c * P:(c + 1) * P]) for c in range(3)])
                read(pe, "mv0")
                read(pe, "mv1")
                for pr in range(2):
                    b = begin(f"mo{pr}")
                    for hd in (2 * pr, 2 * pr + 1):
                        read(pe, f"p{hd}")
                        at = (hd % 2) * T
                        mm(b[:, at:at + P], mv[:, 0, hd, :], PT[:, hd, 0:P], True, True)
                        mm(b[:, at + P:at + T], mv[:, 0, hd, :], PT[:, hd, P:2 * P], True, False)
                        ins = mm(b[:, at + P:at + T], mv[:, 1, hd, :], PT[:, hd, 2 * P:3 * P], False, True)
                    end(f"mo{pr}", ins)
                for t in range(NT):
                    read(pe, f"MPT{t}.{LEVELS - 1}")
                pe.wait_ge(S("vb_ready"), 1)
                heads("vn0", lambda hd: MT[:, 0, hd, :], lambda hd: vt[:, 0, hd, :])
                pe.wait_ge(S("kdec_ready"), 1)
                read(pe, "vn0")
                heads("S1", lambda hd: kdec[:, hd, :], lambda hd: vn0[:, hd, :])
                read(pe, "S1")
                heads("KS", lambda hd: kbT[:, 1, hd, :], lambda hd: S1[:, hd, :])
                read(pe, "KS")
                heads("vn1", lambda hd: MT[:, 1, hd, :], lambda hd: Rn[:, hd, :])
                read(pe, "qk0")
                read(pe, "qk1")
                heads("O0", lambda hd: QK[:, 0, hd, :], lambda hd: vn0[:, hd, :])
                read(pe, "vn1")
                heads("O1", lambda hd: QK[:, 1, hd, :], lambda hd: vn1[:, hd, :])
                heads("O1s", lambda hd: qT[:, 1, hd, :], lambda hd: S1[:, hd, :])
                pe.wait_ge(S("o_ready"), 1)
                for pr in range(2):
                    turns(f"oT{pr}", [(c * T + t * P, o[:, t, 2 * pr + c, :]) for c in range(2) for t in range(NT)])
                pe.wait_ge(S("tap"), 4 * CVK)
                for t in range(NT):
                    turns(f"cvt{t}", [(c * P, cvu[:, c, t * P:(t + 1) * P]) for c in range(4)])
                read(pe, "cvt0")
                read(pe, "cvt1")
                for pr in range(2):
                    turns(f"cvb{pr}", [(c * T + t * P, cvn[:, t, (2 * pr + c) * P:(2 * pr + c + 1) * P])
                                       for c in range(2) for t in range(NT)])
                read(pe, "oT0")
                read(pe, "oT1")
                read(pe, "mo0")
                read(pe, "mo1")
                pe.wait_ge(S("cv_ready"), 1)
                pe.sem_inc(S("gate_used"), 2)
                with pe.Fori(0, KD // 2) as i:
                    for s in range(2):
                        pe.wait_ge(W_landed[s], l * LANDED_PER_LAYER[s] + i * 96 + LANDED[10 + s])
                        pe.wait_ge(S("gate_used"), i * 2 + (s + 1))
                        for b, y in enumerate((oT, cvu, moT)):
                            bk = ps[s * 3 + b]
                            for k in range(KD):
                                mm(bk[:, 0:T], W[s][:, b * D + k * P:b * D + (k + 1) * P], hT[:, k, :], k == 0, k == KD - 1)
                            for k in range(4):
                                ins = mm(bk[:, T:2 * T], W[s][:, 3 * D + b * 512 + k * P:3 * D + b * 512 + (k + 1) * P],
                                         y[:, k, :], k == 0, k == 3)
                            ins.then_inc(S("gate_full"), 1)
                        pe.wait_ge(S("gate_full"), i * 6 + (3 * s + 3))
                        pe.sem_inc(W_free[s], 1)
                pe.wait_ge(S("gate_used"), KD + 2)
                for n in range(2):
                    land(l, 18 + n)
                    for t in range(NT):
                        for k in range(KD):
                            ins = mm(ps[t * 2 + n][:, :], merged[:, k, t * P:(t + 1) * P],
                                     W[n][:, k * 512:(k + 1) * 512], k == 0, k == KD - 1)
                    if n == 0:
                        owed.append(W_free[0])
                ins.then_inc(S("acc_full"), 1)
                owed.append(W_free[1])
                turn_h(1)
                hT_wait(2)
                ffn(l, 1)
                turn_h(2)
                assert not owed
            second_tensor(pe, mm, turn, owed, begin, end)

        @block.scalar
        def _(act_):
            sc = nc.scalar
            st = Steps(act_, S("act_steps"))

            def ffn(f):
                with act_.Fori(0, NF // 2) as i:
                    for s in range(2):
                        act_.wait_ge(S("gu_full"), i * 2 + (f * NF + s + 1))
                        sc.activation(th[s], ps[4 + s][:, 0:T], ACT.Tanh, scale=0.5).then_inc(S("ffn_tanh"), 1)

            def columns(k, which):
                for b in (0, 2):
                    act_.wait_ge(S("tr_full"), 4 * k + b + 1)
                    for c in (2 * b, 2 * b + 1):
                        ins = sc.activation(hT[:, c, :], ps[4 + b][:, (c % 2) * T:(c % 2 + 1) * T], ACT.Identity,
                                            bias=col(f"ln{which}_b", c), scale=col(f"ln{which}_g", c))
                        if c < 5:
                            st.step(ins)
                ins.then_inc(S("hT_act"), 1)

            def copy(job, dst, scale=1.0, n=512):
                take(act_, job)
                src = bank(job)[:, 0:n]
                if len(dst.shape) == 3:
                    src = src.rearrange("p (a b) -> p a b", a=dst.shape[1])
                sc.activation(dst, src, ACT.Copy, scale=scale).then_inc(free(job), 1)

            for b in (0, 2):
                act_.wait_ge(S("x_turned"), b + 1)
                st.step(sc.activation(hT[:, 2 * b:2 * b + 2, :].rearrange("p a b -> p (a b)"), ps[4 + b][:, :], ACT.Copy))
            act_.wait_ge(S("angle_ready"), 2)
            st.step(sc.activation(cos[:, :, :], cos[:, :, :], ACT.Sin))
            st.step(sc.activation(sin[:, :, :], sin[:, :, :], ACT.Sin))

            with act_.Fori(0, DEPTH) as l:
                meet(act_, "scalar", l, st)
                ffn(0)
                act_.wait_ge(S("rows_full"), 1)
                sc.activation(pcol[:, :, :], ps[6][:, 0:384].rearrange("p (a n) -> p a n", a=3),
                              ACT.Copy).then_inc(S("cols_ready"), 1)
                act_.wait_ge(S("cols_ready"), 1)
                columns(0, 1)
                act_.wait_ge(S("half_ready"), 1)
                for n in range(2):
                    take(act_, f"gg{n}")
                    for c in (2 * n, 2 * n + 1):
                        ins = sc.activation(cvg[:, c, :], bank(f"gg{n}")[:, (c % 2) * T:(c % 2 + 1) * T], ACT.Tanh,
                                            bias=col("cv_glu_b", 4 + c, half=True), scale=0.5)
                        if c % 2 == 0:
                            st.step(ins)
                    ins.then_inc(free(f"gg{n}"), 1)
                for x, part in enumerate("qkv"):
                    for n in range(2):
                        copy(f"{part}{n}", dnpad[:, 4 * x + 2 * n:4 * x + 2 * n + 2, CONV - 1:])
                for t in range(NT):
                    take(act_, f"z{t}")
                    sc.activation(z[:, t, :, :].rearrange("p a b -> p (a b)"), bank(f"z{t}")[:, :], ACT.Tanh,
                                  scale=0.5).then_inc(S("z_tanh"), 1)
                for x in range(3):
                    act_.wait_ge(S("dn_tap"), 16 * (x + 1))
                    sc.activation(dnth[:, 4 * x:4 * x + 4, :], dn[:, 4 * x:4 * x + 4, :], ACT.Tanh,
                                  scale=0.5).then_inc(S("dn_tanh"), 1)
                read(act_, "ab")
                sc.activation(beta[:, :, :], abt[:, :, 4:8], ACT.Tanh, scale=0.5).then_inc(S("beta_tanh"), 1)
                act_.wait_ge(S("dt_landed"), l * 32 + 32)
                sc.activation(ea[:, :], dtab[:, 0:4], ACT.Exp).then_inc(S("expa"), 1)
                act_.wait_ge(S("nabs"), 1)
                n = st.step(sc.activation(ab2[:, :, :], ab2[:, :, :], ACT.Exp))
                st.sync(n)
                sc.activation(ab2[:, :, :], ab2[:, :, :], ACT.Ln, bias=1.0).then_inc(S("ln_ready"), 1)
                read(act_, "G")
                sc.activation(eG[:, :, :], Gs[:, :, 0:4], ACT.Exp).then_inc(S("eG_ready"), 1)
                act_.wait_ge(S("dG_ready"), 1)
                sc.activation(eD[:, :], dG[:, :], ACT.Exp).then_inc(S("eD_ready"), 1)
                for part, dst in (("q", qt), ("k", kt), ("v", vt)):
                    for t in range(NT):
                        copy(f"tok_{part}{t}", dst[:, t, :, :])
                for job, chunks in (("cqTa", (0, 1)), ("cqTb", (2,))):
                    take(act_, job)
                    for c in chunks:
                        ins = sc.activation(cqT[:, c, :], bank(job)[:, (c % 2) * T:(c % 2 + 1) * T], ACT.Copy,
                                            scale=col("mla_q_norm_w", c))
                        if c == 0:
                            st.step(ins)
                    ins.then_inc(free(job), 1)
                take(act_, "ckvT")
                for c in range(2):
                    ins = sc.activation(ckvT[:, c, :], bank("ckvT")[:, c * T:(c + 1) * T], ACT.Copy,
                                        scale=col("mla_kv_norm_w", c))
                    if c == 0:
                        st.step(ins)
                ins.then_inc(free("ckvT"), 1)
                copy("krT", krT[:, :], n=T)
                for t in range(NT):
                    read(act_, f"Gb{t}")
                    sc.activation(DT[:, t, :, :], DT[:, t, :, :], ACT.Exp).then_inc(S("dt_exp"), 1)
                for n in range(2):
                    copy(f"qn{n}", qnT[:, 2 * n:2 * n + 2, :])
                for part, dst in (("q", qT), ("k", kT), ("kb", kbT)):
                    for t in range(NT):
                        copy(f"{part}T{t}", dst[:, t, :, :])
                for n in range(2):
                    copy(f"kn{n}", knT[:, 2 * n:2 * n + 2, :])
                for t in range(NT):
                    copy(f"mv{t}", mv[:, t, :, :])
                copy("qrT", qrT[:, :, :])
                for hd in range(HEADS):
                    act_.wait_ge(S("negmax"), 2 * hd + 2)
                    for t in range(NT):
                        cols = slice(0, P) if t == 0 else slice(P, 3 * P)
                        sc.activation(prob[hd][:, cols], prob[hd][:, cols], ACT.Exp, bias=nmax[:, hd, t:t + 1],
                                      scale=(NOPE + ROPE) ** -0.5, accum_out=psums[:, hd, t:t + 1]).then_inc(S("exp_s"), 1)
                for lev in range(LEVELS):
                    for t in range(NT):
                        copy(f"P{t}.{lev}", Pm[:, t, :, :])
                for hd in range(HEADS):
                    copy(f"p{hd}", PT[:, hd, :], n=3 * P)
                for n in range(2):
                    copy(f"mo{n}", moT[:, 2 * n:2 * n + 2, :])
                copy("vn0", vn0)
                copy("S1", S1)
                copy("vn1", vn1, scale=-1.0)
                copy("O0", o[:, 0, :, :])
                copy("O1", o[:, 1, :, :])
                for n in range(2):
                    take(act_, f"oT{n}")
                    sc.activation(oT[:, 2 * n:2 * n + 2, :], bank(f"oT{n}")[:, :].rearrange("p (a b) -> p a b", a=2),
                                  ACT.Copy, scale=col("dn_norm_w", half=True)).then_inc(free(f"oT{n}"), 1)
                for n in range(2):
                    take(act_, f"cvb{n}")
                    for c in (2 * n, 2 * n + 1):
                        ins = sc.activation(cvu[:, c, :], bank(f"cvb{n}")[:, (c % 2) * T:(c % 2 + 1) * T], ACT.Identity,
                                            bias=col("cv_ln_b", c), scale=col("cv_ln_g", c))
                        if c % 2 == 0:
                            st.step(ins)
                    ins.then_inc(free(f"cvb{n}"), 1)
                for n in range(2):
                    read(act_, f"cvb{n}")
                sc.activation(cvg[:, :, :], cvu[:, :, :], ACT.Tanh, scale=0.5).then_inc(S("cv_tanh"), 1)
                with act_.Fori(0, KD // 2) as i:
                    for s in range(2):
                        for b in range(3):
                            act_.wait_ge(S("gate_full"), i * 6 + (3 * s + b + 1))
                            tile, at, _ = ROWS["cv_b_pw2"]
                            if b == 1:
                                sc.activation(gyb[s], ps[s * 3 + b][:, T:2 * T], ACT.Identity,
                                              bias=pcol[:, tile, ds(i * 2 + (at + s), 1)], scale=0.5)
                            tile, at, _ = ROWS["b_gate"]
                            sc.activation(gth[s][b], ps[s * 3 + b][:, 0:T], ACT.Tanh,
                                          bias=phalf[:, tile, ds(i * 2 + (at + b * KD + s), 1)],
                                          scale=0.5).then_inc(S("gate_act"), 1)
                columns(1, 2)
                ffn(1)
                columns(2, 3)
                act_.wait_ge(S("hT_act"), 3)
            second_scalar(act_, st, copy)

        @block.vector
        def _(dve):
            st = Steps(dve, S("dve_steps"))

            def rsq(y, v, tmp):
                rsqrt(dve, st, y, v, tmp)

            def ffn(f):
                with dve.Fori(0, NF // 2) as i:
                    for s in range(2):
                        done = i * 2 + (f * NF + s + 1)
                        dve.wait_ge(S("ffn_tanh"), done)
                        dve.scalar_tensor_tensor(yb[s], th[s], 1.0, ps[4 + s][:, 0:T], ALU.add, ALU.mult
                                                 ).then_inc(S("ffn_y"), 1)
                        dve.wait_ge(S("ffn_y"), done)
                        dve.tensor_tensor(act[s], yb[s], ps[4 + s][:, T:2 * T], ALU.mult).then_inc(S("ffn_act"), 1)

            def norm(k, which, scale, eps):
                dve.wait_ge(S("acc_full"), k + 1)
                if k:
                    dve.wait_ge(S("h_ready"), k)
                at = {}
                for t in range(NT):
                    for n in range(2):
                        part = h[:, t, n * 512:(n + 1) * 512]
                        at[t, n] = st.step(dve.scalar_tensor_tensor(part, part, scale, ps[t * 2 + n][:, :], ALU.mult, ALU.add))
                for t in range(NT):
                    for n in range(2):
                        st.sync(at[t, n])
                        st.step(dve.bn_stats(stats[:, t, n, :], h[:, t, n * 512:(n + 1) * 512]))
                    st.sync()
                    st.step(dve.bn_aggr(mvar[:, t, :], stats[:, t, :, :].rearrange("p a b -> p (a b)")))
                st.sync()
                st.step(dve.tensor_scalar(rv[:, 0:NT], mvar[:, :, 1], eps, None, ALU.add))
                rsq(ry[:, 0:NT], rv[:, 0:NT], rt[:, 0:NT])
                for t in range(NT):
                    dve.tensor_scalar(h[:, t, :], h[:, t, :], mvar[:, t, 0:1], ry[:, t:t + 1], ALU.subtract, ALU.mult
                                      ).then_inc(S("xn_ready"), 1)
                for b in (1, 3):
                    dve.wait_ge(S("tr_full"), 4 * k + b + 1)
                    for c in (2 * b, 2 * b + 1):
                        ins = dve.tensor_scalar(hT[:, c, :], ps[4 + b][:, (c % 2) * T:(c % 2 + 1) * T],
                                                col(f"ln{which}_g", c), col(f"ln{which}_b", c), ALU.mult, ALU.add)
                        if c < 7:
                            st.step(ins)
                ins.then_inc(S("hT_dve"), 1)

            def scaled(out_, in_, by, n):
                return dve.tensor_tensor(out_, in_, by.unsqueeze(2).broadcast_to([P, n, HD]), ALU.mult)

            def flat(x):
                return x.rearrange("p t h j -> p (t h) j")

            for b in (1, 3):
                dve.wait_ge(S("x_turned"), b + 1)
                st.step(dve.tensor_copy(hT[:, 2 * b:2 * b + 2, :].rearrange("p a b -> p (a b)"), ps[4 + b][:, :]))
            dve.wait_ge(S("pos_landed"), 16 * NT)
            dve.wait_ge(S("const_landed"), 16)
            st.step(dve.tensor_copy(mvar[:, :, 0], pos[:, :]))
            for t in range(NT):
                st.sync()
                st.step(dve.tensor_scalar(angle[:, t, :], cst[:, C_FREQ:C_FREQ + 32], mvar[:, t, 0:1], None, ALU.mult))
            for tab, shift in ((cos, 0.25), (sin, 0.0)):
                st.sync()
                st.step(dve.tensor_scalar(turnsi[:, :, :], angle[:, :, :], 1.0 / (2 * np.pi), shift, ALU.mult, ALU.add))
                st.sync()
                st.step(dve.tensor_copy(turnsf[:, :, :], turnsi[:, :, :]))
                st.sync()
                st.step(dve.scalar_tensor_tensor(tab[:, :, :], turnsf[:, :, :], -TWO_PI[0], angle[:, :, :], ALU.mult, ALU.add))
                for piece in TWO_PI[1:]:
                    st.sync()
                    st.step(dve.scalar_tensor_tensor(tab[:, :, :], turnsf[:, :, :], -piece, tab[:, :, :], ALU.mult, ALU.add))
                st.sync()
                if shift:
                    st.step(dve.tensor_scalar(tab[:, :, :], tab[:, :, :], float(np.pi / 2), None, ALU.add))
                    st.sync()
                dve.tensor_scalar(tab[:, :, :], tab[:, :, :], 3.1415925, -3.1415925, ALU.min, ALU.max
                                  ).then_inc(S("angle_ready"), 1)

            with dve.Fori(0, DEPTH) as l:
                meet(dve, "vector", l, st)
                ffn(0)
                dve.wait_ge(S("cols_ready"), 1)
                dve.tensor_scalar(phalf[:, :, :], pcol[:, :, :], 0.5, None, ALU.mult).then_inc(S("half_ready"), 1)
                norm(0, 1, 4 * ALPHA, 16 * EPS)
                for n in range(2):
                    take(dve, f"gv{n}")
                    for c in (2 * n, 2 * n + 1):
                        ins = dve.tensor_scalar(cvu[:, c, :], bank(f"gv{n}")[:, (c % 2) * T:(c % 2 + 1) * T],
                                                col("cv_glu_b", c), None, ALU.add)
                        if c % 2 == 0:
                            st.step(ins)
                    ins.then_inc(free(f"gv{n}"), 1)
                for n in range(2):
                    read(dve, f"gg{n}")
                    read(dve, f"gv{n}")
                dve.wait_ge(S("half_ready"), 1)
                dve.wait_ge(S("cvpad_zero"), 1)
                dve.scalar_tensor_tensor(cvpad[:, :, PAD:], cvg[:, :, :], 1.0, cvu[:, :, :], ALU.add, ALU.mult
                                         ).then_inc(S("glu_pad"), 1)
                dve.wait_ge(S("glu_pad"), 1)
                tile, at, _ = ROWS["cv_dw_w"]
                for c in range(4):
                    dve.tensor_scalar(cvu[:, c, :], cvpad[:, c, 0:T], phalf[:, tile, at + c:at + c + 1],
                                      col("cv_dw_b", c), ALU.mult, ALU.add).then_inc(S("tap"), 1)
                with dve.Fori(1, CVK) as k:
                    for c in range(4):
                        dve.wait_ge(S("tap"), k * 4 + (c - 3))
                        dve.scalar_tensor_tensor(cvu[:, c, :], cvpad[:, c, ds(k, T)], phalf[:, tile, ds(k * 4 + (at + c), 1)],
                                                 cvu[:, c, :], ALU.mult, ALU.add).then_inc(S("tap"), 1)
                dve.wait_ge(S("dn_zero"), 1)
                tile, at, _ = ROWS["dn_conv_w"]
                for job in ("q0", "q1", "k0", "k1", "v0", "v1"):
                    read(dve, job)
                with dve.Fori(0, 3) as x:
                    for k in range(CONV):
                        for c in range(4):
                            w = pcol[:, tile, ds(x * 4 + (at + 12 * k + c), 1)]
                            src = dnpad[:, ds(x * 4 + c, 1), k:k + T]
                            dst = dn[:, ds(x * 4 + c, 1), :]
                            if k == 0:
                                dve.tensor_scalar(dst, src, w, None, ALU.mult).then_inc(S("dn_tap"), 1)
                            else:
                                dve.wait_ge(S("dn_tap"), x * 16 + (4 * k + c - 3))
                                dve.scalar_tensor_tensor(dst, src, w, dst, ALU.mult, ALU.add).then_inc(S("dn_tap"), 1)
                for x in range(3):
                    dve.wait_ge(S("dn_tanh"), x + 1)
                    part = dn[:, 4 * x:4 * x + 4, :]
                    dve.scalar_tensor_tensor(part, dnth[:, 4 * x:4 * x + 4, :], 1.0, part, ALU.add, ALU.mult
                                             ).then_inc(S("dn_silu"), 1)
                for t in range(NT):
                    dve.wait_ge(S("z_tanh"), t + 1)
                    zt = z[:, t, :, :].rearrange("p a b -> p (a b)")
                    dve.scalar_tensor_tensor(zt, zt, 1.0, bank(f"z{t}")[:, :], ALU.add, ALU.mult).then_inc(free(f"z{t}"), 1)
                take(dve, "ab")
                dve.tensor_copy(abt[:, :, :], bank("ab")[:, 0:16].rearrange("p (t n) -> p t n", t=NT)).then_inc(free("ab"), 1)
                read(dve, "ab")
                dve.wait_ge(S("dt_landed"), l * 32 + 32)
                st.step(dve.tensor_tensor(ab1[:, :, :], abt[:, :, 0:4], dtab[:, 4:8].unsqueeze(1).broadcast_to([P, NT, 4]), ALU.add))
                st.sync()
                st.step(dve.tensor_scalar(ab2[:, :, :], ab1[:, :, :], -1.0, None, ALU.mult))
                st.sync()
                dve.tensor_tensor(ab2[:, :, :], ab2[:, :, :], ab1[:, :, :], ALU.min).then_inc(S("nabs"), 1)
                dve.wait_ge(S("beta_tanh"), 1)
                st.step(dve.tensor_scalar(betah[:, :, :], beta[:, :, :], 0.25, 0.25, ALU.mult, ALU.add))
                dve.tensor_scalar(beta[:, :, :], beta[:, :, :], 0.5, 0.5, ALU.mult, ALU.add).then_inc(S("beta_ready"), 1)
                dve.wait_ge(S("ln_ready"), 1)
                st.step(dve.scalar_tensor_tensor(ab1[:, :, :], ab1[:, :, :], 0.0, ab2[:, :, :], ALU.max, ALU.add))
                st.sync()
                dve.wait_ge(S("expa"), 1)
                dve.scalar_tensor_tensor(g[:, :, :], ab1[:, :, :], -1.0, ea[:, :].unsqueeze(1).broadcast_to([P, NT, 4]),
                                         ALU.mult, ALU.mult).then_inc(S("g_ready"), 1)
                dve.wait_ge(S("g_ready"), 1)
                for t in range(NT):
                    for hd in range(HEADS):
                        ins = dve.tensor_scalar(Pm[:, t, hd, :], tri, g[:, t, hd:hd + 1], None, ALU.mult)
                        if (t, hd) != (NT - 1, HEADS - 1):
                            st.step(ins)
                ins.then_inc(S("trig"), 1)
                for t in range(NT):
                    for n, (job, dst, width, w) in enumerate(((f"cq{t}", cqn, QL, QL), (f"ck{t}", ckn, KVL + ROPE, KVL))):
                        take(dve, job)
                        dve.tensor_copy(dst[:, t, :], bank(job)[:, 0:width]).then_inc(free(job), 1)
                        read(dve, job)
                        st.step(dve.tensor_tensor(sq[:, 0:w], dst[:, t, 0:w], dst[:, t, 0:w], ALU.mult))
                        st.sync()
                        st.step(dve.tensor_reduce(rv[:, 2 * n + t:2 * n + t + 1], sq[:, 0:w], AX, ALU.add))
                st.sync()
                st.step(dve.tensor_scalar(rv[:, 0:2], rv[:, 0:2], 1.0 / QL, EPS, ALU.mult, ALU.add))
                st.step(dve.tensor_scalar(rv[:, 2:4], rv[:, 2:4], 1.0 / KVL, EPS, ALU.mult, ALU.add))
                rsq(ry[:, 0:4], rv[:, 0:4], rt[:, 0:4])
                for t in range(NT):
                    dve.tensor_scalar(cqn[:, t, :], cqn[:, t, :], ry[:, t:t + 1], None, ALU.mult).then_inc(S("cq_ready"), 1)
                for t in range(NT):
                    dve.tensor_scalar(ckn[:, t, 0:KVL], ckn[:, t, 0:KVL], ry[:, 2 + t:3 + t], None, ALU.mult
                                      ).then_inc(S("ck_ready"), 1)
                def rotate(x, y, cs, sn, n, sig):
                    t1 = rope1[:, 0:n].rearrange("p (a b) -> p a b", b=32)
                    t2 = rope2[:, 0:n].rearrange("p (a b) -> p a b", b=32)
                    lo, hi = x[:, :, 0:32], x[:, :, 32:64]
                    for first, second, op, dst in ((lo, hi, ALU.subtract, y[:, :, 0:32]), (hi, lo, ALU.add, y[:, :, 32:64])):
                        st.sync()
                        st.step(dve.tensor_tensor(t1, first, cs, ALU.mult))
                        st.step(dve.tensor_tensor(t2, second, sn, ALU.mult))
                        st.sync()
                        last = dve.tensor_tensor(dst, t1, t2, op)
                        if op is ALU.subtract or sig is None:
                            st.step(last)
                    if sig is not None:
                        last.then_inc(sig, 1)

                dve.wait_ge(S("ck_ready"), 2)
                rotate(ckn[:, :, KVL:], krd[:, :, 0, :], cos[:, :, :], sin[:, :, :], 2 * 32, None)
                st.sync()
                dve.tensor_copy(krd[:, :, 1, :], krd[:, :, 0, :]).then_inc(S("kr_ready"), 1)
                take(dve, "G")
                dve.tensor_copy(Gs[:, :, :], bank("G")[:, 0:16].rearrange("p (t n) -> p t n", t=NT)).then_inc(free("G"), 1)
                read(dve, "G")
                dve.tensor_tensor(dG[:, :], Gs[:, 0, 4:8], Gs[:, 0, 0:4], ALU.subtract).then_inc(S("dG_ready"), 1)
                square = R1[:, 0:1024]
                for n, (x, part) in enumerate(((qt, "q"), (kt, "k"))):
                    for t in range(NT):
                        read(dve, f"tok_{part}{t}")
                    st.sync()
                    fx = x[:, :, :, :].rearrange("p t h j -> p (t h j)")
                    st.step(dve.tensor_tensor(square, fx, fx, ALU.mult))
                    st.sync()
                    st.step(dve.tensor_reduce(rv[:, 8 * n:8 * n + 8], square.rearrange("p (n j) -> p n j", j=HD), AX, ALU.add))
                st.sync()
                st.step(dve.tensor_scalar(rv[:, :], rv[:, :], 4e-6, None, ALU.add))
                rsq(ry[:, :], rv[:, :], rt[:, :])
                st.step(dve.tensor_scalar(ry[:, 0:8], ry[:, 0:8], HD ** -0.5, None, ALU.mult))
                st.sync()
                scaled(flat(qt[:, :, :, :]), flat(qt[:, :, :, :]), ry[:, 0:8], 8).then_inc(S("qk_norm"), 1)
                scaled(flat(kt[:, :, :, :]), flat(kt[:, :, :, :]), ry[:, 8:16], 8).then_inc(S("qk_norm"), 1)
                dve.wait_ge(S("qk_norm"), 2)
                dve.wait_ge(S("beta_ready"), 1)
                scaled(flat(kb), flat(kt[:, :, :, :]), beta[:, :, :].rearrange("p t h -> p (t h)"), 8
                       ).then_inc(S("kb_ready"), 1)
                for t in range(NT):
                    take(dve, f"Gb{t}")
                    for hd in range(HEADS):
                        ins = dve.tensor_scalar(DT[:, t, hd, :], bank(f"Gb{t}")[:, hd * P:(hd + 1) * P],
                                                Gs[:, t, hd:hd + 1], 0.0, ALU.subtract, ALU.min)
                        if hd < HEADS - 1:
                            st.step(ins)
                    ins.then_inc(free(f"Gb{t}"), 1)
                for t in range(NT):
                    dve.wait_ge(S("dt_exp"), t + 1)
                    st.step(dve.tensor_tensor(DT[:, t, :, :], DT[:, t, :, :], tri.unsqueeze(1).broadcast_to([P, HEADS, P]), ALU.mult))
                take(dve, "qr")
                qr_in = bank("qr")[:, :].rearrange("p (t h n) -> p t h n", t=NT, h=HEADS)
                for t in range(NT):
                    st.step(dve.tensor_copy(qraw[:, :, :], qr_in[:, t, :, :]))
                    rotate(qraw, qr[:, t, :, :], cos[:, t:t + 1, :].broadcast_to([P, HEADS, 32]),
                           sin[:, t:t + 1, :].broadcast_to([P, HEADS, 32]), HEADS * 32, S("qr_ready"))
                    dve.wait_ge(S("qr_ready"), t + 1)
                dve.sem_inc(free("qr"), 1)
                for w, dst in (("kk", AT), ("qk", QK)):
                    for t in range(NT):
                        take(dve, f"{w}{t}")
                        st.sync()
                        dve.tensor_tensor(dst[:, t, :, :].rearrange("p h j -> p (h j)"), bank(f"{w}{t}")[:, :],
                                          DT[:, t, :, :].rearrange("p h j -> p (h j)"), ALU.mult).then_inc(free(f"{w}{t}"), 1)
                for hd in range(HEADS):
                    take(dve, f"s{hd}")
                    dve.tensor_tensor(prob[hd], bank(f"s{hd}")[:, 0:3 * P], cst[:, C_CAUSAL:C_CAUSAL + 3 * P], ALU.add
                                      ).then_inc(free(f"s{hd}"), 1)
                    read(dve, f"s{hd}")
                    st.step(dve.tensor_reduce(nmax[:, hd, 0:1], prob[hd][:, 0:P], AX, ALU.max))
                    st.step(dve.tensor_reduce(nmax[:, hd, 1:2], prob[hd][:, P:3 * P], AX, ALU.max))
                    st.sync()
                    dve.tensor_scalar(nmax[:, hd, :], nmax[:, hd, :], -(NOPE + ROPE) ** -0.5, None, ALU.mult
                                      ).then_inc(S("negmax"), 2)
                for hd in range(HEADS):
                    dve.wait_ge(S("exp_s"), 2 * hd + 2)
                    st.step(dve.reciprocal(psums[:, hd, :], psums[:, hd, :]))
                    st.sync()
                    st.step(dve.tensor_scalar(prob[hd][:, 0:P], prob[hd][:, 0:P], psums[:, hd, 0:1], None, ALU.mult))
                    dve.tensor_scalar(prob[hd][:, P:3 * P], prob[hd][:, P:3 * P], psums[:, hd, 1:2], None, ALU.mult
                                      ).then_inc(S("p_ready"), 1)
                dve.wait_ge(S("M_init"), 2)
                for lev in range(LEVELS):
                    for t in range(NT):
                        for w, X in (("MP", M), ("MPT", MT)):
                            job = f"{w}{t}.{lev}"
                            take(dve, job)
                            x = X[:, t, :, :].rearrange("p h j -> p (h j)")
                            dve.tensor_tensor(x, x, bank(job)[:, :], ALU.subtract).then_inc(free(job), 1)
                dve.wait_ge(S("eG_ready"), 1)
                dve.wait_ge(S("vb_ready"), 1)
                take(dve, "KS")
                for hd in range(HEADS):
                    ins = dve.scalar_tensor_tensor(Rn[:, hd, :], bank("KS")[:, hd * P:(hd + 1) * P], eG[:, 1, hd:hd + 1],
                                                   vt[:, 1, hd, :], ALU.mult, ALU.subtract)
                    if hd < HEADS - 1:
                        st.step(ins)
                ins.then_inc(free("KS"), 1)
                read(dve, "O0")
                read(dve, "O1")
                take(dve, "O1s")
                for hd in range(HEADS):
                    ins = dve.scalar_tensor_tensor(o[:, 1, hd, :], bank("O1s")[:, hd * P:(hd + 1) * P], eG[:, 1, hd:hd + 1],
                                                   o[:, 1, hd, :], ALU.mult, ALU.add)
                    if hd < HEADS - 1:
                        st.step(ins)
                ins.then_inc(free("O1s"), 1)
                read(dve, "O1s")
                fo = o[:, :, :, :].rearrange("p t h j -> p (t h j)")
                square = DT[:, :, :, :].rearrange("p t h j -> p (t h j)")
                st.step(dve.tensor_tensor(square, fo, fo, ALU.mult))
                st.sync()
                st.step(dve.tensor_reduce(rv[:, 0:8], square.rearrange("p (n j) -> p n j", j=HD), AX, ALU.add))
                st.sync()
                st.step(dve.tensor_scalar(rv[:, 0:8], rv[:, 0:8], 1.0 / HD, EPS, ALU.mult, ALU.add))
                rsq(ry[:, 0:8], rv[:, 0:8], rt[:, 0:8])
                st.step(scaled(flat(o[:, :, :, :]), flat(o[:, :, :, :]), ry[:, 0:8], 8))
                st.sync()
                read(dve, "z1")
                dve.tensor_tensor(fo, fo, z[:, :, :, :].rearrange("p t h j -> p (t h j)"), ALU.mult).then_inc(S("o_ready"), 1)
                for t in range(NT):
                    take(dve, f"cvt{t}")
                    st.step(dve.bn_stats(stats[:, t, 0, :], bank(f"cvt{t}")[:, :]))
                    st.sync()
                    st.step(dve.bn_aggr(mvar[:, t, :], stats[:, t, 0, :]))
                st.sync()
                st.step(dve.tensor_scalar(rv[:, 0:NT], mvar[:, :, 1], EPS, None, ALU.add))
                rsq(ry[:, 0:NT], rv[:, 0:NT], rt[:, 0:NT])
                for t in range(NT):
                    dve.tensor_scalar(cvn[:, t, :], bank(f"cvt{t}")[:, :], mvar[:, t, 0:1], ry[:, t:t + 1],
                                      ALU.subtract, ALU.mult).then_inc(free(f"cvt{t}"), 1)
                dve.wait_ge(S("cv_tanh"), 1)
                dve.scalar_tensor_tensor(cvu[:, :, :], cvg[:, :, :], 1.0, cvu[:, :, :], ALU.add, ALU.mult
                                         ).then_inc(S("cv_ready"), 1)
                with dve.Fori(0, KD // 2) as i:
                    for s in range(2):
                        n = i * 8 + 4 * s
                        dve.wait_ge(S("gate_act"), i * 6 + (3 * s + 3))
                        dve.scalar_tensor_tensor(gm[s], gth[s][0], 1.0, ps[s * 3][:, T:2 * T], ALU.add, ALU.mult
                                                 ).then_inc(S("gate_sum"), 1)
                        dve.scalar_tensor_tensor(gt[s], gth[s][1], 1.0, gyb[s], ALU.add, ALU.mult).then_inc(S("gate_sum"), 1)
                        dve.wait_ge(S("gate_sum"), n + 2)
                        dve.tensor_tensor(gm[s], gm[s], gt[s], ALU.add).then_inc(S("gate_sum"), 1)
                        dve.wait_ge(S("gate_sum"), n + 3)
                        dve.scalar_tensor_tensor(gt[s], gth[s][2], 1.0, ps[s * 3 + 2][:, T:2 * T], ALU.add, ALU.mult
                                                 ).then_inc(S("gate_sum"), 1)
                        dve.wait_ge(S("gate_sum"), n + 4)
                        dve.tensor_tensor(merged[:, ds(i * 2 + s, 1), :], gm[s].unsqueeze(1), gt[s].unsqueeze(1), ALU.add
                                          ).then_inc(S("gate_used"), 1)
                norm(1, 2, 2 * ALPHA, 4 * EPS)
                ffn(1)
                norm(2, 3, 4 * ALPHA, 16 * EPS)
                dve.wait_ge(S("hT_dve"), 3)
            second_vector(dve, st)

        @block.gpsimd
        def _(pool):
            st = Steps(pool, S("pool_steps"))
            for t in range(NT):
                pool.dma_start(pos[:, t:t + 1], A["positions"].rearrange("b p -> p b")[t * P:(t + 1) * P, :]
                               ).then_inc(S("pos_landed"), 16)
            st.step(pool.memset(ones[:, :], 1.0))
            pool.memset(cvpad[:, :, 0:PAD], 0.0).then_inc(S("cvpad_zero"), 1)

            def load_gain(l, which):
                for dst, name in ((gain, f"ln{which}_g"), (bias, f"ln{which}_b")):
                    pool.dma_start(dst[:, :], A[name][ds(l, 1), :].broadcast_to([P, D])).then_inc(S("gain_landed"), 16)

            def residual(k, l, nxt):
                pool.wait_ge(S("tr_full"), 4 * k + 4)
                pool.wait_ge(S("gain_landed"), l * 96 + (32 * k + 32))
                for by, op in ((gain, ALU.mult), (bias, ALU.add)):
                    st.sync()
                    for t in range(NT):
                        ins = pool.tensor_tensor(h[:, t, :], h[:, t, :], by[:, :], op)
                        if t == NT - 1 and op is ALU.add:
                            ins.then_inc(S("h_ready"), 1)
                        else:
                            st.step(ins)
                if nxt:
                    pool.wait_ge(S("h_ready"), k + 1)
                    load_gain(l, nxt)

            with pool.Fori(0, DEPTH) as l:
                meet(pool, "gpsimd", l, st)
                load_gain(l, 1)
                st.step(pool.memset(prow[:, :, :], 0.0))
                st.step(pool.memset(dnpad[:, :, 0:CONV - 1], 0.0))
                st.sync()
                pool.sem_inc(S("dn_zero"), 1)
                for name, (tile, at, n) in ROWS.items():
                    src = A[name][l]
                    if len(src.shape) == 2:
                        src = src.rearrange("k (c p) -> (k c) p", p=P)
                    else:
                        src = src.rearrange("(c p) -> c p", p=P)
                    pool.dma_start(prow[at:at + n, tile, :], src).then_inc(S("rows_landed"), 16)
                for n, name in enumerate(("dn_a_log", "dn_dt_bias")):
                    pool.dma_start(dtab[:, 4 * n:4 * n + 4], A[name][ds(l, 1), :].broadcast_to([P, 4])).then_inc(S("dt_landed"), 16)
                residual(0, l, 2)
                pool.wait_ge(S("beta_ready"), 1)
                read(pool, "tok_v0")
                read(pool, "tok_v1")
                fv = vt[:, :, :, :].rearrange("p t h j -> p (t h) j")
                pool.tensor_tensor(fv, fv, betah[:, :, :].rearrange("p t h -> p (t h)").unsqueeze(2).broadcast_to([P, 8, HD]),
                                   ALU.mult).then_inc(S("vb_ready"), 1)
                for X in (M, MT):
                    pool.tensor_copy(X.rearrange("p t h j -> p (t h) j"), ident.unsqueeze(1).broadcast_to([P, 8, P])
                                     ).then_inc(S("M_init"), 1)
                pool.wait_ge(S("eD_ready"), 1)
                pool.wait_ge(S("qk_norm"), 2)
                pool.tensor_tensor(kdec[:, :, :], kt[:, 0, :, :], eD[:, :].unsqueeze(2).broadcast_to([P, HEADS, HD]),
                                   ALU.mult).then_inc(S("kdec_ready"), 1)
                for lev in range(LEVELS):
                    for t in range(NT):
                        if lev == 0:
                            read(pool, f"kk{t}")
                        if lev >= 2:
                            take(pool, f"P{t}.{lev - 2}")
                        mask = cst[:, C_LEV + lev * P:C_LEV + (lev + 1) * P].unsqueeze(1).broadcast_to([P, HEADS, P])
                        pool.tensor_tensor(ATl[lev % 2][:, t, :, :], AT[:, t, :, :], mask, ALU.mult).then_inc(S("lev_mask"), 1)
                residual(1, l, 3)
                residual(2, l, 0)
                pool.wait_ge(S("h_ready"), 3)
            second_pool(pool, st)


NAMES = ['const', 'x', 'positions', 'ln1_g', 'ln1_b', 'ffn1_w_gate', 'ffn1_w_up', 'ffn1_w_down', 'w_in', 'b_gate', 'dn_conv_w', 'dn_a_log', 'dn_dt_bias', 'dn_norm_w', 'dn_w_o', 'cv_glu_b', 'cv_dw_w', 'cv_dw_b', 'cv_ln_g', 'cv_ln_b', 'cv_w_pw2', 'cv_b_pw2', 'mla_q_norm_w', 'mla_w_uq', 'mla_kv_norm_w', 'mla_w_ukv', 'mla_w_o', 'w_out', 'ln2_g', 'ln2_b', 'ffn2_w_gate', 'ffn2_w_up', 'ffn2_w_down', 'ln3_g', 'ln3_b', 'c_2', 'w_ada_2', 'b_ada_2', 'w_in_2', 'conv_w_2', 'conv_b_2', 'w_gate_a_2', 'b_gate_a_2', 'w_gate_x_2', 'b_gate_x_2', 'lru_lambda_2', 'rel_bias_2', 'norm_lru_g_2', 'norm_attn_g_2', 'w_out_2', 'ln1_g_2', 'ln1_b_2', 'w_router_group_2', 'b_router_group_2', 'w_router_expert_2', 'b_router_expert_2', 'w1_2', 'w3_2', 'w2_2', 'ln2_g_2', 'ln2_b_2']


def kernel(**inputs):
    import concourse.bacc as _bacc
    from concourse.bass_utils import run_bass_kernel_spmd as _run

    nc = _bacc.Bacc("TRN2", target_bir_lowering=False, num_devices=1)
    arrays, A = {}, {}
    for name in NAMES:
        a = np.ascontiguousarray(shape_constants() if name == "const" else inputs[name])
        arrays[f"in_{name}"] = a
        A[name] = nc.dram_tensor(f"in_{name}", a.shape, mybir.dt.from_np(a.dtype), kind="ExternalInput").ap()
    out = nc.dram_tensor("out_0", (1, T, D), F32, kind="ExternalOutput").ap()
    build(nc, A, out)
    return _run(nc, [arrays], core_ids=[0]).results[0]["out_0"]
```

```python
from contextlib import ExitStack

import numpy as np

import concourse.bass as bass
from concourse import mybir

F32 = mybir.dt.float32
F32R = mybir.dt.float32r
I32 = mybir.dt.int32
ALU = mybir.AluOpType
ACT = mybir.ActivationFunctionType
AX = mybir.AxisListType.X
ds = bass.ds

P = 128
T = 256
NT = T // P
D = 1024
KD = D // P
DEPTH = 2
FF = 2816
NF = FF // P
HEADS = 4
HD = 128
CONV = 4
CVC = 512
CVK = 31
QL, KVL, NOPE, ROPE, VD = 384, 256, 128, 64, 128
THETA = 10000.0
EPS = 1e-5
ALPHA = (2 * DEPTH) ** 0.25
ALPHA_2 = 2.0 ** 0.25
MASKED = -1e30
LEVELS = 7
DL = 512
H2 = 8
HD2 = 64
LRU_C = 8.0
GROUPS, PER_GROUP = 4, 8
EXPERTS = GROUPS * PER_GROUP
DE = 256
BUCKETS, MAX_DIST = 32, 128
PAD = CVK - 1
RAMP = 384

OFF_QKV = 0
OFF_Z = 3 * HEADS * HD
OFF_GLU = OFF_Z + HEADS * HD + 2 * HEADS
OFF_CQ = OFF_GLU + 2 * CVC
OFF_CKV = OFF_CQ + QL
OFF_GATE = OFF_CKV + KVL + ROPE

C_ID, C_TRI, C_LEV, C_CAUSAL = 0, 128, 256, 256 + 128 * LEVELS
C_BUCKET = C_CAUSAL + 3 * P
C_FREQ = C_BUCKET + RAMP
C_IOTA = C_FREQ + 32
C_ALL = C_IOTA + 32

ROWS = {}
for _tile, _group in enumerate((
        (("ln1_g", 8), ("ln1_b", 8), ("ln2_g", 8), ("ln2_b", 8), ("ln3_g", 8), ("ln3_b", 8),
         ("b_gate", 24), ("dn_conv_w", 48), ("cv_glu_b", 8)),
        (("cv_dw_w", 124),),
        (("cv_dw_b", 4), ("cv_ln_g", 4), ("cv_ln_b", 4), ("cv_b_pw2", 8), ("mla_q_norm_w", 3),
         ("mla_kv_norm_w", 2), ("dn_norm_w", 1)))):
    _at = 0
    for _name, _n in _group:
        ROWS[_name] = (_tile, _at, _n)
        _at += _n


def shape_constants():
    c = np.zeros((P, C_ALL), np.float32)
    i = np.arange(P)
    c[:, C_ID:C_ID + P] = np.eye(P)
    c[:, C_TRI:C_TRI + P] = i[:, None] <= i[None, :]
    for lev in range(LEVELS):
        s = 1 << lev
        pair = (i[:, None] // (2 * s)) == (i[None, :] // (2 * s))
        c[:, C_LEV + lev * P:C_LEV + (lev + 1) * P] = pair & (i[None, :] % (2 * s) >= s) & (i[:, None] % (2 * s) < s)
    above = np.where(i[None, :] > i[:, None], MASKED, 0.0)
    c[:, C_CAUSAL:C_CAUSAL + P] = above
    c[:, C_CAUSAL + 2 * P:C_CAUSAL + 3 * P] = above
    rel = T - 1 - np.arange(RAMP)
    n = np.maximum(rel, 0)
    exact = BUCKETS // 2
    large = exact + (np.log(np.maximum(n, 1).astype(np.float32) / np.float32(exact)) / np.float32(np.log(MAX_DIST / exact))
                     * np.float32(BUCKETS - exact)).astype(np.int32)
    bucket = np.where(n < exact, n, np.minimum(large, BUCKETS - 1))
    bucket = np.where(rel < 0, BUCKETS, bucket)
    c[bucket, C_BUCKET + np.arange(RAMP)] = 1.0
    half = ROPE // 2
    c[:, C_FREQ:C_FREQ + half] = np.float32(THETA) ** (-np.arange(half, dtype=np.float32) / np.float32(half))
    c[:, C_IOTA:C_IOTA + EXPERTS] = np.arange(EXPERTS)
    return c


UNITS = (["glu_value", "glu_gate", "q", "k", "v", "z_ab", "c_q", "c_kv", "w_uq", "w_ukv"]
         + ["gates"] * KD + ["w_out"] * 2)
UNIT_DMAS = {"gates": 6}
W_SLOT = 4608
F_SLOT = 3 * D
FFN_CHUNKS = 3 * NF
MOE_FIRST = 2 * DEPTH * FFN_CHUNKS
UNITS_PER_SLOT = len(UNITS) // 2
LANDED = []
for _u, _name in enumerate(UNITS):
    LANDED.append((LANDED[_u - 2] if _u >= 2 else 0) + 16 * UNIT_DMAS.get(_name, 1))
LANDED_PER_LAYER = [LANDED[-2], LANDED[-1]]

JOBS = (["gv0", "gv1", "gg0", "gg1", "q0", "q1", "k0", "k1", "v0", "v1", "z0", "z1", "ab",
         "cq0", "cq1", "ck0", "ck1", "G"]
        + ["tok_q0", "tok_q1", "tok_k0", "tok_k1", "tok_v0", "tok_v1"]
        + ["cqTa", "cqTb", "ckvT", "krT", "Gb0", "Gb1", "qn0", "qn1", "qr"]
        + ["qT0", "qT1", "kT0", "kT1", "kbT0", "kbT1", "kn0", "kn1", "mv0", "mv1"]
        + ["kk0", "kk1", "qk0", "qk1", "qrT", "s0", "s1", "s2", "s3"]
        + [f"{w}{t}.{lev}" for lev in range(LEVELS) for w in ("P", "MP", "MPT") for t in range(NT)]
        + ["p0", "p1", "p2", "p3", "mo0", "mo1", "vn0", "S1", "KS", "vn1", "O0", "O1", "O1s", "oT0", "oT1"]
        + ["cvt0", "cvt1", "cvb0", "cvb1"])
JOBS_2 = (["rows2"] + [f"ramp{n}" for n in range(H2)] + [f"ada{n}" for n in range(4)] + [f"u{n}" for n in range(4)]
          + ["xl0", "xl1", "yl0", "yl1", "ada4", "ada5", "qq0", "qq1", "ada6", "kk20", "kk21", "ada7", "vv0", "vv1",
             "g1b0", "g1b1", "ga0", "ga1", "gx0", "gx1"]
          + [f"a{n}" for n in range(H2)] + ["rms0"]
          + ["b0", "b1", "c0", "b2", "b3", "c1", "b4", "b5", "c2", "b6", "b7", "c3"]
          + ["rms1", "ada8", "ada9", "ada10", "ada11", "wo00", "wo10", "wo01", "wo11", "g2b0", "g2b1"]
          + [f"w{n}" for n in range(4)] + ["router"])
BANKS = 8
BANK = {name: n % BANKS for jobs in (JOBS, JOBS_2) for n, name in enumerate(jobs)}
ROUND = {name: n // BANKS for jobs in (JOBS, JOBS_2) for n, name in enumerate(jobs)}


TWO_PI = (6.28125, 0.001934051513671875, float(2 * np.pi - 6.28125 - 0.001934051513671875))


class Steps:

    def __init__(self, eng, sem):
        self.eng, self.sem, self.n = eng, sem, 0

    def step(self, ins):
        ins.then_inc(self.sem, 1)
        self.n += 1
        return self.n

    def sync(self, n=None):
        if n is None:
            n = self.n
        if n > 0:
            self.eng.wait_ge(self.sem, n)

    def restart(self):
        self.eng.sem_clear(self.sem)
        self.n = 0


def build(nc, A, out):
    ctx = ExitStack()
    with ctx:
        def sb(name, shape, dt=F32):
            return ctx.enter_context(nc.sbuf_tensor(name, shape, dt))

        names = {}

        def S(name):
            if name not in names:
                names[name] = ctx.enter_context(nc.semaphore(name))
            return names[name]

        cst = sb("cst", [P, C_ALL])
        ones = sb("ones", [P, P])
        h = sb("h", [P, NT, D])
        hT = sb("hT", [P, KD, T])
        hh, hl = sb("hh", [P, KD, T], F32R), sb("hl", [P, KD, T], F32R)
        wh, wl = sb("wh", [P, 2, D], F32R), sb("wl", [P, 2, D], F32R)
        ah, al = sb("ah", [P, 2, T], F32R), sb("al", [P, 2, T], F32R)
        wbuf = sb("wbuf", [P, 2 * W_SLOT])
        R1 = sb("R1", [P, 12 * (T + CONV - 1)])
        R2 = sb("R2", [P, 12 * T])
        R3 = sb("R3", [P, 12 * T])
        cvpad = sb("cvpad", [P, 4, T + PAD])
        cvu = sb("cvu", [P, 4, T])
        cvg = sb("cvg", [P, 4, T])
        mA = sb("mA", [P, 2176])
        ckvT = sb("ckvT", [P, 2, T])
        qnT = sb("qnT", [P, HEADS, T])
        qr = sb("qr", [P, NT, HEADS, ROPE])
        qrT = sb("qrT", [P, 2, T])
        krT = sb("krT", [P, T])
        krd = sb("krd", [P, NT, 2, ROPE])
        knT = sb("knT", [P, HEADS, T])
        mv = sb("mv", [P, NT, HEADS, VD])
        qt = sb("qt", [P, NT, HEADS, HD])
        kt = sb("kt", [P, NT, HEADS, HD])
        vt = sb("vt", [P, NT, HEADS, HD])
        kdec = sb("kdec", [P, HEADS, HD])
        qT = sb("qT", [P, NT, HEADS, P])
        kT = sb("kT", [P, NT, HEADS, P])
        kbT = sb("kbT", [P, NT, HEADS, P])
        z = sb("z", [P, NT, HEADS, HD])
        pcol = sb("pcol", [P, 3, P])
        phalf = sb("phalf", [P, 3, P])
        cos = sb("cos", [P, NT, 32])
        sin = sb("sin", [P, NT, 32])
        stats = sb("stats", [P, NT, 2, 6])
        mvar = sb("mvar", [P, NT, 2])
        ry = sb("ry", [P, 16])
        rt = sb("rt", [P, 16])
        rv = sb("rv", [P, 16])
        dtab = sb("dtab", [P, 8])
        rel = sb("rel", [BUCKETS + 1, H2])
        pos = sb("pos", [P, NT], I32)
        abt = sb("abt", [P, NT, 8])
        ab1 = sb("ab1", [P, NT, 4])
        ab2 = sb("ab2", [P, NT, 4])
        ea = sb("ea", [P, 4])
        beta = sb("beta", [P, NT, 4])
        betah = sb("betah", [P, NT, 4])
        g = sb("g", [P, NT, 4])
        Gs = sb("Gs", [P, NT, 8])
        eG = sb("eG", [P, NT, 4])
        dG = sb("dG", [P, 4])
        eD = sb("eD", [P, 4])
        nmax = sb("nmax", [P, HEADS, 2])
        psums = sb("psums", [P, HEADS, 2])
        ps = [ctx.enter_context(nc.psum_tensor(f"bank{b}", [P, 512], F32)) for b in range(BANKS)]

        ident = cst[:, C_ID:C_ID + P]
        tri = cst[:, C_TRI:C_TRI + P]
        dnpad = R1[:, :].rearrange("p (c t) -> p c t", c=12)
        AT = R1[:, 0:1024].rearrange("p (t h j) -> p t h j", t=NT, h=HEADS)
        Pm = R1[:, 1024:2048].rearrange("p (t h j) -> p t h j", t=NT, h=HEADS)
        ATl = [R1[:, 2048:3072].rearrange("p (t h j) -> p t h j", t=NT, h=HEADS), qt[:, :, :, :]]
        kb = ATl[0]
        dn = R2[:, :].rearrange("p (c t) -> p c t", c=12)
        M = R2[:, 0:1024].rearrange("p (t h j) -> p t h j", t=NT, h=HEADS)
        MT = R2[:, 1024:2048].rearrange("p (t h j) -> p t h j", t=NT, h=HEADS)
        DT = R2[:, 2048:3072].rearrange("p (t h j) -> p t h j", t=NT, h=HEADS)
        merged = R2[:, 0:2048].rearrange("p (k t) -> p k t", k=KD)
        prow = mA[:, 0:384].rearrange("p (a n) -> p a n", a=3)
        dnth = R3[:, :].rearrange("p (c t) -> p c t", c=12)
        QK = R3[:, 0:1024].rearrange("p (t h j) -> p t h j", t=NT, h=HEADS)
        vn0 = R3[:, 1024:1536].rearrange("p (h j) -> p h j", h=HEADS)
        S1 = R3[:, 1536:2048].rearrange("p (h j) -> p h j", h=HEADS)
        Rn = R3[:, 2048:2560].rearrange("p (h j) -> p h j", h=HEADS)
        vn1 = R3[:, 2560:3072].rearrange("p (h j) -> p h j", h=HEADS)
        o = qt
        oT = kt[:, :, :, :].rearrange("p a b c -> p (a b c)").rearrange("p (h t) -> p h t", h=HEADS)
        th = [R3[:, 256 * s:256 * s + 256] for s in range(2)]
        yb = [R3[:, 512 + 256 * s:768 + 256 * s] for s in range(2)]
        act = [R3[:, 1024 + 256 * s:1280 + 256 * s] for s in range(2)]
        gth = [[R3[:, 768 * s + 256 * b:768 * s + 256 * b + 256] for b in range(3)] for s in range(2)]
        gyb = [R3[:, 1536 + 256 * s:1792 + 256 * s] for s in range(2)]
        gm = [R3[:, 2048 + 512 * s:2304 + 512 * s] for s in range(2)]
        gt = [R3[:, 2304 + 512 * s:2560 + 512 * s] for s in range(2)]
        cqn = mA[:, 0:768].rearrange("p (t n) -> p t n", t=NT)
        ckn = mA[:, 768:1408].rearrange("p (t n) -> p t n", t=NT)
        cqT = mA[:, 1408:2176].rearrange("p (k t) -> p k t", k=3)
        PT = mA[:, 0:1536].rearrange("p (h n) -> p h n", h=HEADS)
        moT = qnT
        cvg_flat = cvg[:, :, :].rearrange("p a b -> p (a b)")
        cvn = cvg_flat.rearrange("p (t n) -> p t n", t=NT)
        sq = cvg_flat[:, 0:QL]
        qraw = cvg_flat[:, 640:896].rearrange("p (a b) -> p a b", a=HEADS)
        rope1, rope2 = cvg_flat[:, 384:512], cvg_flat[:, 512:640]
        angle, turnsf = (R3[:, 64 * n:64 * n + 64].rearrange("p (t n) -> p t n", t=NT) for n in range(2))
        turnsi = R3[:, 128:192].bitcast(I32).rearrange("p (t n) -> p t n", t=NT)
        prob = [qr[:, :, :, :].rearrange("p a b c -> p (a b c)")[:, 0:384], mA[:, 1536:1920], cvg_flat[:, 0:384], cvg_flat[:, 384:768]]
        W = [wbuf[:, s * W_SLOT:(s + 1) * W_SLOT] for s in range(2)]
        F = [R1[:, 0:F_SLOT], R2[:, 0:F_SLOT]]
        gain = vt[:, :, :, :].rearrange("p t h j -> p (t h j)")
        bias = z[:, :, :, :].rearrange("p t h j -> p (t h j)")

        def col(name, k=0, half=False):
            tile, at, _ = ROWS[name]
            return (phalf if half else pcol)[:, tile, at + k:at + k + 1]

        bank_full = [S(f"bank_full{b}") for b in range(BANKS)]
        bank_free = [S(f"bank_free{b}") for b in range(BANKS)]
        F_gu_landed = [S(f"ffn_gate_up_landed{s}") for s in range(2)]
        F_d_landed = [S(f"ffn_down_landed{s}") for s in range(2)]
        high, low, used = S("chunk_high"), S("chunk_low"), S("chunk_used")
        hT_high, hT_split = S("hT_high"), S("hT_split")
        W_landed = [S(f"unit_landed{s}") for s in range(2)]
        W_free = [S(f"unit_free{s}") for s in range(2)]
        all_in, all_out, met = S("all_in"), S("all_out"), S("met")

        def take(eng, job):
            eng.wait_ge(bank_full[BANK[job]], ROUND[job] + 1)

        def bank(job):
            return ps[BANK[job]]

        def read(eng, job):
            eng.wait_ge(bank_free[BANK[job]], ROUND[job] + 1)

        def free(job):
            return bank_free[BANK[job]]

        per_layer = [f"bank_full{b}" for b in range(BANKS)] + [f"bank_free{b}" for b in range(BANKS)] + [
            "gu_full", "ffn_tanh", "ffn_y", "ffn_act", "act_high", "act_split", "acc_full", "xn_ready", "tr_full", "hT_act", "hT_dve",
            "h_ready", "rows_full", "cols_ready", "half_ready",
            "glu_pad", "tap", "dn_zero", "dn_tap", "dn_tanh", "dn_silu", "z_tanh",
            "beta_tanh", "nabs", "ln_ready", "expa", "beta_ready", "g_ready", "eG_ready", "dG_ready", "eD_ready",
            "qk_norm", "kb_ready", "vb_ready", "kdec_ready", "trig", "dt_exp", "cq_ready", "ck_ready",
            "kr_ready", "qr_ready", "M_init", "lev_mask", "negmax", "exp_s", "p_ready", "o_ready",
            "cv_tanh", "cv_ready", "gate_full", "gate_act", "gate_sum", "gate_used"]
        for name in per_layer:
            S(name)
        clears = {"tensor": per_layer[0::4], "scalar": per_layer[1::4], "vector": per_layer[2::4],
                  "gpsimd": per_layer[3::4]}

        def meet(eng, who, l, steps):
            steps.sync()
            eng.sem_inc(all_in, 1)
            eng.wait_ge(all_in, l * 4 + 4)
            eng.sem_inc(met, 1)
            for name in clears[who]:
                eng.sem_clear(S(name))
            steps.restart()
            eng.sem_inc(all_out, 1)
            eng.wait_ge(all_out, l * 4 + 4)
            eng.sem_inc(met, 1)

        def split_high(act_, n, src):
            n, s = n
            act_.wait_ge(used, n + 1)
            dst = wh[:, s, :]
            if len(src.shape) == 3:
                dst = dst.rearrange("p (k n) -> p k n", k=src.shape[1])
            nc.scalar.activation(dst, src, ACT.Copy).then_inc(high, 1)

        def split_low(dve, n, src):
            n, s = n
            dve.wait_ge(high, n + 1)
            dst, first = wl[:, s, :], wh[:, s, :]
            if len(src.shape) == 3:
                dst, first = (x.rearrange("p (k n) -> p k n", k=src.shape[1]) for x in (dst, first))
            dve.tensor_tensor(dst, src, first.bitcast(F32), ALU.subtract).then_inc(low, 1)

        def split_act(dve, n, src, dst):
            dve.tensor_copy(dst(ah), src).then_inc(S("act_high"), 1)
            dve.wait_ge(S("act_high"), n + 1)
            dve.tensor_tensor(dst(al), src, dst(ah).bitcast(F32), ALU.subtract).then_inc(S("act_split"), 1)

        def expert_chunk(s, c):
            if c >= 4:
                return D2[s][:, (c - 4) * D:(c - 3) * D]
            at, fc = (c % 2) * 2048, c // 2
            return E[s][:, at:at + 2048].rearrange("p (k n) -> p k n", k=KD)[:, :, fc * P:(fc + 1) * P]

        def rsqrt(dve, st, y, v, tmp):
            st.sync()
            st.step(dve.tensor_scalar(y.bitcast(I32), v.bitcast(I32), -0.5, 1597463007.0, ALU.mult, ALU.add))
            for _ in range(4):
                st.sync()
                st.step(dve.tensor_tensor(tmp, y, y, ALU.mult))
                st.sync()
                st.step(dve.scalar_tensor_tensor(tmp, tmp, -0.5, v, ALU.mult, ALU.mult))
                st.sync()
                st.step(dve.scalar_tensor_tensor(y, tmp, 1.5, y, ALU.add, ALU.mult))
            st.sync()


        rows2 = R2[:, 1024:1152]
        ramp_tab = R2[:, 0:1024].rearrange("p (h n) -> p h n", h=H2)
        toep = R2[:, 0:2048].rearrange("p (h n) -> p h n", h=H2)
        yacc = R2[:, 0:2048].rearrange("p (t n) -> p t n", t=NT)
        pflat = pcol[:, :, :].rearrange("p a b -> p (a b)")
        hflat = phalf[:, :, :].rearrange("p a b -> p (a b)")
        modc = pflat[:, 96:144]
        silc = pflat[:, 144:152]
        rbias = pflat[:, 160:196]
        lamc = pflat[:, 200:204]
        lam1 = pflat[:, 204:208]
        lam2 = pflat[:, 208:212]
        cvflat = cvpad[:, :, :].rearrange("p a b -> p (a b)")
        ktflat = kt[:, :, :, :].rearrange("p t h j -> p (t h j)")
        stage = [mA[:, RAMP * n:RAMP * (n + 1)] for n in range(5)] + [ktflat[:, 0:RAMP], ktflat[:, RAMP:2 * RAMP], cvflat[:, 0:RAMP]]
        xlpad = R1[:, 0:4 * (T + CONV - 1)].rearrange("p (c t) -> p c t", c=4)
        ada_acc = [R1[:, 1036 + 512 * n:1036 + 512 * (n + 1)] for n in range(4)]
        yl, xc = cvu, cvg
        gate_a, gate_x = qnT, knT
        decay = mv[:, :, :, :].rearrange("p t h j -> p (t h j)").rearrange("p (c t) -> p c t", c=4)
        lru = z[:, :, :, :].rearrange("p t h j -> p (t h j)").rearrange("p (c t) -> p c t", c=4)
        attn = decay
        spare = R3[:, 2048:3072].rearrange("p (c t) -> p c t", c=4)
        xn = R3[:, 0:2048].rearrange("p (t n) -> p t n", t=NT)
        wbd = qt[:, :, :, :].rearrange("p t h j -> p (t h) j")
        diag = kdec
        g1row = kt[:, :, :, :].rearrange("p t h j -> p (t h j)")
        g2row = vt[:, :, :, :].rearrange("p t h j -> p (t h j)")
        q2T = kT[:, :, :, :].rearrange("p t h j -> p (t h j)").rearrange("p (c t) -> p c t", c=4)
        k2T = kbT[:, :, :, :].rearrange("p t h j -> p (t h j)").rearrange("p (c t) -> p c t", c=4)
        v2 = qT[:, :, :, :].rearrange("p t h j -> p t (h j)")
        rms_v, rms_y, rms_t = krT[:, :], ckvT[:, 0, :], ckvT[:, 1, :]
        probs2 = R3[:, :].rearrange("p (h n) -> p h n", h=H2)
        PT2 = mA[:, 0:4 * 3 * P].rearrange("p (h n) -> p h n", h=4)
        nmax2 = hflat[:, 96:112].rearrange("p (h t) -> p h t", t=NT)
        sums2 = hflat[:, 112:128].rearrange("p (h t) -> p h t", t=NT)
        logit = cvflat[:, 400:472].rearrange("p (t n) -> p t n", t=NT)
        rt1, rt2, rt3, oh1, oh2, gate_e = (cvflat[:, 480 + 64 * n:544 + 64 * n].rearrange("p (t n) -> p t n", t=NT)
                                          for n in range(6))
        ohg = cvflat[:, 864:872].rearrange("p (t n) -> p t n", t=NT)
        rg1 = cvflat[:, 872:880].rearrange("p (t n) -> p t n", t=NT)
        rg2 = cvflat[:, 880:888].rearrange("p (t n) -> p t n", t=NT)
        rmx, rix, rs1, rs2, rs3, rm1 = (cvflat[:, 896 + 2 * n:898 + 2 * n] for n in range(6))
        moe_t = [qT[:, :, :, :].rearrange("p t h j -> p (t h j)")[:, 256 * n:256 * (n + 1)] for n in range(2)]
        moe_a = R3[:, 2048:2560].rearrange("p (n t) -> p n t", n=2)
        gain2, bias2 = (x[:, :, :, :].rearrange("p t h j -> p (t h j)") for x in (kT, kbT))
        E = W
        D2 = [R1[:, 0:2048], mA[:, 0:2048]]
        E_landed = [S(f"expert_unit_landed{s}") for s in range(2)]
        E_free = [S(f"expert_unit_free{s}") for s in range(2)]
        D_landed = [S(f"expert_w2_landed{s}") for s in range(2)]
        ramp_dram = nc.dram_tensor("ramp", (H2, P, RAMP), F32, kind="Internal").ap()

        ADA_FIRST = 4
        UNITS2 = (["ada"] * 4 + ["x_lru", "y_lru", "ada", "ada", "q", "ada", "k", "ada", "v", "ada", "ada", "ada", "ada",
                  "w_out0", "w_out1", "router"])
        ada_units = [u for u, name in enumerate(UNITS2) if name == "ada"]
        assert len(ada_units) == 12 and len(UNITS2) % 2 == 0
        landed2 = []
        for u, name in enumerate(UNITS2):
            landed2.append((landed2[u - 2] if u >= 2 else 0) + (32 if name == "router" else 16))

        def land2(eng, name, n=0):
            u = [k for k, x in enumerate(UNITS2) if x == name][n]
            eng.wait_ge(E_landed[u % 2], landed2[u])
            return E[u % 2]

        def second_sync(sp):
            for s in range(2):
                sp.wait_ge(W_free[s], DEPTH * UNITS_PER_SLOT + 1)
            w_ada = A["w_ada_2"][0].rearrange("(k p) n -> p k n", p=P)
            w_in2 = A["w_in_2"][0].rearrange("(k p) n -> p k n", p=P)
            w_out2 = A["w_out_2"][0].rearrange("(k p) n -> p k n", p=P)
            source = {"x_lru": w_in2[:, :, 0:512], "y_lru": w_in2[:, :, 512:1024], "q": w_in2[:, :, 1024:1536],
                      "k": w_in2[:, :, 1536:2048], "v": w_in2[:, :, 2048:2560], "w_out0": w_out2[:, :, 0:512],
                      "w_out1": w_out2[:, :, 512:1024]}
            stored = False
            n_ada = 0
            for u, name in enumerate(UNITS2):
                s = u % 2
                if u >= 2:
                    sp.wait_ge(E_free[s], u // 2)
                if name == "router":
                    sp.dma_start(E[s][:, 0:KD * 4].rearrange("p (k n) -> p k n", k=KD),
                                 A["w_router_group_2"][0].rearrange("(k p) n -> p k n", p=P)).then_inc(E_landed[s], 16)
                    sp.dma_start(E[s][:, 32:32 + KD * 32].rearrange("p (k n) -> p k n", k=KD),
                                 A["w_router_expert_2"][0].rearrange("(k p) n -> p k n", p=P)).then_inc(E_landed[s], 16)
                    continue
                src = source.get(name)
                if name == "ada":
                    src = w_ada[:, :, n_ada * 512:(n_ada + 1) * 512]
                    n_ada += 1
                sp.dma_start(E[s][:, 0:4096].rearrange("p (k n) -> p k n", k=KD), src).then_inc(E_landed[s], 16)
            def expert(e, s, first):
                n = MOE_FIRST + (e * 6 if first else e * 6 - 12)
                if not first:
                    slot_wait2(sp, low, n + 5)
                for x, w in enumerate(("w1_2", "w3_2")):
                    sp.dma_start(E[s][:, x * 2048:(x + 1) * 2048].rearrange("p (k n) -> p k n", k=KD),
                                 A[w][0].rearrange("e (k p) n -> e p k n", p=P)[e]).then_inc(E_landed[s], 16)
                if not first:
                    slot_wait2(sp, low, n + 11)
                sp.dma_start(D2[s].rearrange("p (k n) -> p k n", k=2),
                             A["w2_2"][0].rearrange("e (k p) n -> e p k n", p=P)[e]).then_inc(D_landed[s], 16)

            for s in range(2):
                sp.wait_ge(E_free[s], len(UNITS2) // 2)
                if s == 0:
                    sp.wait_ge(S("w2_room"), 1)
                expert(s, s, True)
            with sp.Fori(0, EXPERTS // 2 - 1) as i:
                for s in range(2):
                    expert(i * 2 + (2 + s), s, False)
            sp.wait_ge(S("out_ready"), 2)
            sp.dma_start(out.rearrange("b (t p) d -> p (b t) d", p=P), h[:, :, :]).then_inc(S("out_stored"), 16)
            sp.wait_ge(S("out_stored"), 16)

        def slot_wait2(sp, sem, n):
            sp.wait_ge(sem, n)
            sp.sem_inc(S("sp_waited"), 1)

        def second_tensor(pe, mm, turn, owed, begin, end, wide_product, tall_product):
            meet(pe, "tensor", DEPTH, Steps(pe, S("pe_steps2")))

            def features(name, jobs, rhs):
                w = land2(pe, name)
                for n, job in enumerate(jobs):
                    b = begin(job)
                    for c in range(2):
                        for k in range(KD):
                            ins = mm(b[:, c * T:(c + 1) * T], w[:, k * 512 + (2 * n + c) * P:k * 512 + (2 * n + c + 1) * P],
                                     rhs[:, k, :], k == 0, k == KD - 1)
                    end(job, ins)
                owed.append(E_free[UNITS2.index(name) % 2])

            def ada(n):
                b = begin(f"ada{n}")
                pe.wait_ge(S("ada_acc"), n + 1)
                for c in range(4):
                    ins = mm(b[:, c:c + 1], ada_acc[n % 4][:, c * P:(c + 1) * P], ones[:, 0:1], True, True)
                end(f"ada{n}", ins)

            def turn_rows(prefix, sem):
                pe.wait_ge(sem, 2)
                for b4 in range(4):
                    b = begin(f"{prefix}{b4}")
                    for c in range(2):
                        for t in range(NT):
                            ins = turn(b[:, c * T + t * P:c * T + (t + 1) * P], xn[:, t, (2 * b4 + c) * P:(2 * b4 + c + 1) * P])
                    end(f"{prefix}{b4}", ins)

            def row_of(jobs, sem):
                for n, job in enumerate(jobs):
                    pe.wait_ge(sem, n + 1)
                    b = begin(job)
                    for c in range(4):
                        ins = mm(b[:, c * P:(c + 1) * P], ones[:, :], diag[:, c, :], True, True)
                    end(job, ins)

            pe.wait_ge(S("rows2_landed"), 16 * 9)
            b = begin("rows2")
            end("rows2", turn(b[:, 0:P], rows2))
            pe.wait_ge(S("ramp_tab"), 1)
            for hd in range(H2):
                b = begin(f"ramp{hd}")
                end(f"ramp{hd}", mm(b[:, 0:RAMP], ramp_tab[0:BUCKETS + 1, hd, :], cst[0:BUCKETS + 1, C_BUCKET:C_BUCKET + RAMP],
                                    True, True))
            for n in range(4):
                ada(n)
            turn_rows("u", S("xn2_ready"))
            for n in range(4):
                read(pe, f"u{n}")
            features("x_lru", ("xl0", "xl1"), hT)
            features("y_lru", ("yl0", "yl1"), hT)
            ada(4)
            ada(5)
            features("q", ("qq0", "qq1"), hT)
            ada(6)
            features("k", ("kk20", "kk21"), hT)
            ada(7)
            w = land2(pe, "v")
            for t in range(NT):
                b = begin(f"vv{t}")
                for k in range(KD):
                    ins = mm(b[:, :], hT[:, k, t * P:(t + 1) * P], w[:, k * 512:(k + 1) * 512], k == 0, k == KD - 1)
                end(f"vv{t}", ins)
            owed.append(E_free[UNITS2.index("v") % 2])
            row_of(("g1b0", "g1b1"), S("diag1"))
            pe.wait_ge(S("wbd_landed"), 32 * H2)
            pe.wait_ge(S("xc_ready"), 1)
            for n, name in enumerate(("ga", "gx")):
                for pr in range(2):
                    b = begin(f"{name}{pr}")
                    for c in range(2):
                        ins = mm(b[:, c * T:(c + 1) * T], wbd[:, n * 4 + 2 * pr + c, :], xc[:, 2 * pr + c, :], True, True)
                    end(f"{name}{pr}", ins)
            for job in ("qq0", "qq1", "kk20", "kk21", "vv0", "vv1"):
                read(pe, job)
            for hd in range(H2):
                b = begin(f"a{hd}")
                half = slice(64 * (hd % 2), 64 * (hd % 2) + 64)
                for t in range(NT):
                    n = (t + 1) * P
                    ins = mm(b[:, t * P:t * P + n], q2T[half, hd // 2, t * P:(t + 1) * P], k2T[half, hd // 2, 0:n], True, True)
                end(f"a{hd}", ins)
            pe.wait_ge(S("sq_ready"), 1)
            b = begin("rms0")
            for c in range(4):
                ins = mm(b[:, 0:T], ones[:, :], lsq[:, c, :], c == 0, c == 3)
            end("rms0", ins)
            for hd in range(H2):
                pe.wait_ge(S("p2_ready"), hd + 1)
                b = begin(f"b{hd}")
                for c in range(3):
                    ins = turn(b[:, c * P:(c + 1) * P], probs2[:, hd, c * P:(c + 1) * P])
                end(f"b{hd}", ins)
                if hd >= 1:
                    value(pe, mm, begin, end, hd - 1)
            value(pe, mm, begin, end, H2 - 1)
            pe.wait_ge(S("sq_ready"), 2)
            b = begin("rms1")
            for c in range(4):
                ins = mm(b[:, 0:T], ones[:, :], lsq[:, c, :], c == 0, c == 3)
            end("rms1", ins)
            for n in range(8, 12):
                ada(n)
            pe.wait_ge(S("merged2"), 8)
            for n in range(2):
                w = land2(pe, f"w_out{n}")
                for t in range(NT):
                    b = begin(f"wo{t}{n}")
                    for k in range(KD):
                        src = lru if k < 4 else attn
                        ins = mm(b[:, :], src[:, k % 4, t * P:(t + 1) * P], w[:, k * 512:(k + 1) * 512], k == 0, k == KD - 1)
                    end(f"wo{t}{n}", ins)
                owed.append(E_free[UNITS2.index(f"w_out{n}") % 2])
            take(pe, "wo11")
            pe.sem_inc(S("w2_room"), 1)
            row_of(("g2b0", "g2b1"), S("diag2"))
            turn_rows("w", S("xn3_ready"))
            for n in range(4):
                read(pe, f"w{n}")
            w = land2(pe, "router")
            b = begin("router")
            for t in range(NT):
                for at, width, src in ((0, GROUPS, w[:, 0:32]), (GROUPS, EXPERTS, w[:, 32:288])):
                    for k in range(KD):
                        ins = mm(b[:, t * 36 + at:t * 36 + at + width], hT[:, k, t * P:(t + 1) * P],
                                 src[:, k * width:(k + 1) * width], k == 0, k == KD - 1)
            end("router", ins)
            owed.append(E_free[1])
            read(pe, "router")

            def up(n, s):
                for fc in range(2):
                    for x in range(2):
                        ins = wide_product(ps[2 * s + fc][:, x * T:(x + 1) * T], n + (2 * fc + x), x)
                        if x == 0:
                            ins.then_inc(used, 1)
                    ins.then_inc(S("up_full"), 1)
                    owed.append(used)

            def down2(e1, n, s):
                pe.wait_ge(S("act_split"), e1)
                pe.wait_ge(S("down_used"), e1)
                for fc in range(2):
                    ins = tall_product(4, n + fc, fc, fc, fc == 0, fc == 1)
                    if fc == 0:
                        ins.then_inc(used, 1)
                ins.then_inc(S("down_full"), 1)
                owed.append(used)

            pe.sem_inc(S("down_used"), 1)
            pe.wait_ge(hT_split, 2 * DEPTH + 2)
            up(MOE_FIRST, 0)
            up(MOE_FIRST + 4, 1)
            with pe.Fori(0, EXPERTS // 2 - 1) as i:
                n = i * 12 + MOE_FIRST
                down2(i * 2 + 1, n + 8, 0)
                up(n + 10, 0)
                down2(i * 2 + 2, n + 14, 1)
                up(n + 16, 1)
            last = MOE_FIRST + 6 * EXPERTS
            down2(EXPERTS - 1, last - 4, 0)
            down2(EXPERTS, last - 2, 1)
            owed.clear()

        lsq = cvu

        def value(pe, mm, begin, end, hd):
            job = f"c{hd // 2}"
            b = begin(job) if hd % 2 == 0 else bank(job)
            read(pe, f"b{hd}")
            half = slice(64 * (hd % 2), 64 * (hd % 2) + 64)
            p = PT2[:, hd % 4, :]
            v = slice(hd * HD2, (hd + 1) * HD2)
            mm(b[half, 0:P], v2[:, 0, v], p[:, 0:P], True, True)
            mm(b[half, P:T], v2[:, 0, v], p[:, P:2 * P], True, False)
            ins = mm(b[half, P:T], v2[:, 1, v], p[:, 2 * P:3 * P], False, True)
            if hd % 2:
                end(job, ins)

        def second_scalar(act_, st, copy):
            sc = nc.scalar
            meet(act_, "scalar", DEPTH, st)
            take(act_, "rows2")
            sc.activation(pflat[:, 0:96], bank("rows2")[:, 0:96], ACT.Copy).then_inc(free("rows2"), 1)
            read(act_, "rows2")
            sc.activation(silc, pflat[:, 0:8], ACT.Tanh, scale=0.5).then_inc(S("sil_tanh"), 1)
            for hd in range(H2):
                copy(f"ramp{hd}", stage[hd], n=RAMP)
            for hd in range(H2):
                read(act_, f"ramp{hd}")
                act_.dma_start(ramp_dram[hd], stage[hd]).then_inc(S("ramp_stored"), 16)
            for n in range(4):
                take(act_, f"u{n}")
                for c in (2 * n, 2 * n + 1):
                    if n == 0 and c == 0:
                        act_.wait_ge(S("scale1"), 1)
                    ins = sc.activation(hT[:, c, :], bank(f"u{n}")[:, (c % 2) * T:(c % 2 + 1) * T], ACT.Identity,
                                        bias=modc[:, c:c + 1], scale=modc[:, 8 + c:9 + c])
                    if c % 2 == 0:
                        st.step(ins)
                ins.then_inc(free(f"u{n}"), 1)
            act_.wait_ge(S("ramp_stored"), 16 * H2)
            skew = bass.AP(ramp_dram.tensor, P - 1, [[RAMP - 1, P], [P * RAMP, H2], [1, T]])
            act_.dma_start(toep, skew).then_inc(S("toep_landed"), 16)
            act_.wait_ge(S("xl_zero"), 1)
            for n in range(2):
                copy(f"xl{n}", xlpad[:, 2 * n:2 * n + 2, CONV - 1:])
            for n in range(2):
                copy(f"yl{n}", yl[:, 2 * n:2 * n + 2, :])
            for n in range(2):
                copy(f"qq{n}", q2T[:, 2 * n:2 * n + 2, :])
            for n in range(2):
                copy(f"kk2{n}", k2T[:, 2 * n:2 * n + 2, :])
            for t in range(NT):
                copy(f"vv{t}", v2[:, t, :])
            for n in range(2):
                copy(f"g1b{n}", g1row[:, n * 512:(n + 1) * 512])
            for x, (name, dst, at) in enumerate((("ga", gate_a, 76), ("gx", gate_x, 80))):
                for n in range(2):
                    take(act_, f"{name}{n}")
                    for c in (2 * n, 2 * n + 1):
                        ins = sc.activation(dst[:, c, :], bank(f"{name}{n}")[:, (c % 2) * T:(c % 2 + 1) * T], ACT.Tanh,
                                            bias=hflat[:, at + c:at + c + 1], scale=0.5)
                        if c % 2 == 0:
                            st.step(ins)
                    ins.then_inc(free(f"{name}{n}"), 1)
            act_.wait_ge(S("lam_abs"), 1)
            st.step(sc.activation(lam2, lam2, ACT.Exp))
            st.sync()
            sc.activation(lam2, lam2, ACT.Ln, bias=1.0).then_inc(S("lam_ln"), 1)
            act_.wait_ge(S("log_a"), 1)
            sc.activation(decay, gate_a[:, :, :], ACT.Exp).then_inc(S("decay_ready"), 1)
            sc.activation(spare, gate_a[:, :, :], ACT.Tanh).then_inc(S("tanh_log_a"), 1)
            act_.wait_ge(S("gelu_in"), 1)
            sc.activation(gelu_t, gelu_t, ACT.Tanh, scale=0.7978845608028654).then_inc(S("gelu_tanh"), 1)
            act_.wait_ge(S("mult2"), 1)
            sc.activation(spare, spare, ACT.Sqrt).then_inc(S("mult_ready"), 1)
            for hd in range(H2):
                act_.wait_ge(S("negmax2"), hd + 1)
                for t in range(NT):
                    cols = slice(0, P) if t == 0 else slice(P, 3 * P)
                    sc.activation(probs2[:, hd, cols], probs2[:, hd, cols], ACT.Exp, bias=nmax2[:, hd, t:t + 1],
                                  accum_out=sums2[:, hd, t:t + 1]).then_inc(S("exp2"), 1)
            for hd in range(H2):
                if hd >= 4:
                    take(act_, f"c{(hd - 4) // 2}")
                copy(f"b{hd}", PT2[:, hd % 4, :], n=3 * P)
                if hd % 2 and hd >= 3:
                    copy(f"c{hd // 2 - 1}", attn[:, hd // 2 - 1, :], n=T)
            copy("c3", attn[:, 3, :], n=T)
            for n in range(2):
                copy(f"g2b{n}", g2row[:, n * 512:(n + 1) * 512])
            for n in range(4):
                take(act_, f"w{n}")
                for c in (2 * n, 2 * n + 1):
                    if c == 0:
                        act_.wait_ge(S("scale2"), 1)
                    ins = sc.activation(hT[:, c, :], bank(f"w{n}")[:, (c % 2) * T:(c % 2 + 1) * T], ACT.Identity,
                                        bias=modc[:, 24 + c:25 + c], scale=modc[:, 32 + c:33 + c])
                    if c % 2 == 0:
                        st.step(ins)
                ins.then_inc(free(f"w{n}"), 1)
            st.sync()
            read(act_, "w3")
            sc.activation(hh[:, :, :], hT[:, :, :], ACT.Copy).then_inc(hT_high, 1)
            def high_of(n, s, c, use=None):
                if c == 0:
                    act_.wait_ge(E_landed[s], use * 32 + landed2[-2 + s])
                if c == 4:
                    act_.wait_ge(D_landed[s], use * 16)
                split_high(act_, (n, c % 2), expert_chunk(s, c))

            def first_chunks(a, b):
                for c in range(a, b):
                    high_of(MOE_FIRST + c, c // 4, c % 4, 1)

            first_chunks(0, 2)
            act_.wait_ge(S("group_shift"), 1)
            sc.activation(rg2, rg2, ACT.Exp).then_inc(S("group_exp"), 1)
            first_chunks(2, 4)
            act_.wait_ge(S("pair_shift"), 1)
            sc.activation(rs2, rs2, ACT.Exp).then_inc(S("pair_exp"), 1)
            def tanh(e, s):
                for fc in range(2):
                    n = e * 2 + (fc + 1)
                    act_.wait_ge(S("up_full"), n)
                    act_.wait_ge(S("moe_act"), n)
                    sc.activation(moe_t[fc], ps[2 * s + fc][:, 0:T], ACT.Tanh, scale=0.5).then_inc(S("moe_tanh"), 1)

            first_chunks(4, 6)
            tanh(0, 0)
            first_chunks(6, 8)
            with act_.Fori(0, EXPERTS // 2 - 1) as i:
                for s in range(2):
                    n = i * 12 + (MOE_FIRST + 8 + 6 * s)
                    high_of(n, s, 4, i + 1)
                    tanh(i * 2 + (s + 1), 1 - s)
                    high_of(n + 1, s, 5)
                    for c in range(4):
                        high_of(n + (2 + c), s, c, i + 2)
            last = MOE_FIRST + 6 * EXPERTS
            high_of(last - 4, 0, 4, EXPERTS // 2)
            tanh(EXPERTS - 1, 1)
            high_of(last - 3, 0, 5)
            high_of(last - 2, 1, 4, EXPERTS // 2)
            high_of(last - 1, 1, 5)

        gelu_t = R1[:, 0:1024].rearrange("p (c t) -> p c t", c=4)

        def second_vector(dve, st):
            meet(dve, "vector", DEPTH, st)

            def rsq(y, v, tmp):
                rsqrt(dve, st, y, v, tmp)

            dve.wait_ge(S("rel_landed"), 16)
            dve.wait_ge(S("rel_mask"), 1)
            dve.tensor_copy(ramp_tab[0:BUCKETS + 1, :, :], rel[:, :].unsqueeze(2).broadcast_to([BUCKETS + 1, H2, P])
                            ).then_inc(S("ramp_tab"), 1)

            def moments(src, eps=EPS):
                for t in range(NT):
                    for n in range(2):
                        st.step(dve.bn_stats(stats[:, t, n, :], src[:, t, n * 512:(n + 1) * 512]))
                    st.sync()
                    st.step(dve.bn_aggr(mvar[:, t, :], stats[:, t, :, :].rearrange("p a b -> p (a b)")))
                st.sync()
                st.step(dve.tensor_scalar(rv[:, 0:NT], mvar[:, :, 1], eps, None, ALU.add))
                rsq(ry[:, 0:NT], rv[:, 0:NT], rt[:, 0:NT])

            def normed(dst, sem):
                for t in range(NT):
                    ins = dve.tensor_scalar(dst[:, t, :], h[:, t, :], mvar[:, t, 0:1], ry[:, t:t + 1], ALU.subtract, ALU.mult)
                    if sem is None:
                        st.step(ins)
                    else:
                        ins.then_inc(sem, 1)

            moments(h)
            normed(xn, S("xn2_ready"))
            read(dve, "rows2")
            st.step(dve.tensor_scalar(hflat[:, 0:96], pflat[:, 0:96], 0.5, None, ALU.mult))
            dve.wait_ge(S("sil_tanh"), 1)
            st.sync()
            st.step(dve.scalar_tensor_tensor(silc, silc, 1.0, hflat[:, 0:8], ALU.add, ALU.mult))
            st.sync()

            def ada(n):
                u = ada_units[n]
                w = E[u % 2]
                dve.wait_ge(E_landed[u % 2], landed2[u])
                if n >= 4:
                    take(dve, f"ada{n - 4}")
                acc = ada_acc[n % 4]
                st.step(dve.tensor_scalar(acc, w[:, 0:512], silc[:, 0:1], None, ALU.mult))
                for k in range(1, KD):
                    st.sync()
                    ins = dve.scalar_tensor_tensor(acc, w[:, k * 512:(k + 1) * 512], silc[:, k:k + 1], acc, ALU.mult, ALU.add)
                    if k < KD - 1:
                        st.step(ins)
                ins.then_inc(S("ada_acc"), 1)
                dve.wait_ge(S("ada_acc"), n + 1)
                dve.sem_inc(E_free[u % 2], 1)

            def ada_out(n):
                take(dve, f"ada{n}")
                dve.tensor_tensor(modc[:, 4 * n:4 * n + 4], bank(f"ada{n}")[:, 0:4], pflat[:, 8 + 4 * n:12 + 4 * n], ALU.add
                                  ).then_inc(free(f"ada{n}"), 1)

            def conv_tap(k, c):
                w = pflat[:, 56 + 4 * k + c:57 + 4 * k + c]
                src = xlpad[:, c, k:k + T]
                if k == 0:
                    return dve.tensor_scalar(xc[:, c, :], src, w, pflat[:, 72 + c:73 + c], ALU.mult, ALU.add)
                return dve.scalar_tensor_tensor(xc[:, c, :], src, w, xc[:, c, :], ALU.mult, ALU.add)

            for n in range(4):
                ada(n)
            for n in range(4):
                ada_out(n)
            read(dve, "ada3")
            dve.tensor_scalar(modc[:, 8:16], modc[:, 8:16], 1.0, None, ALU.add).then_inc(S("scale1"), 1)
            ada(4)
            ada(5)
            read(dve, "xl0")
            read(dve, "xl1")
            for k in range(CONV):
                for c in range(4):
                    if k:
                        st.sync(st.n - 3)
                    if (k, c) == (CONV - 1, 3):
                        conv_tap(k, c).then_inc(S("xc_ready"), 1)
                    else:
                        st.step(conv_tap(k, c))
            ada_out(4)
            ada_out(5)
            read(dve, "ada5")
            ada(6)
            ada(7)
            ada_out(6)
            ada_out(7)
            for half in range(2):
                if half:
                    take(dve, "g1b0")
                for c in range(4):
                    at = 16 + 4 * half + c
                    ins = dve.tensor_scalar(diag[:, c, :], ident, modc[:, at:at + 1], None, ALU.mult)
                    if c < 3:
                        st.step(ins)
                ins.then_inc(S("diag1"), 1)
            lam = pflat[:, 84:88]
            st.step(dve.tensor_scalar(lam1, lam, -1.0, None, ALU.mult))
            st.sync()
            dve.tensor_tensor(lam2, lam, lam1, ALU.min).then_inc(S("lam_abs"), 1)
            dve.wait_ge(S("lam_ln"), 1)
            st.step(dve.scalar_tensor_tensor(lamc, lam1, 0.0, lam2, ALU.max, ALU.add))
            st.sync()
            st.step(dve.tensor_scalar(lamc, lamc, -LRU_C / 2, None, ALU.mult))
            st.sync()
            for n in range(2):
                read(dve, f"ga{n}")
            for c in range(4):
                ins = dve.tensor_scalar(gate_a[:, c, :], gate_a[:, c, :], 1.0, lamc[:, c:c + 1], ALU.add, ALU.mult)
                if c < 3:
                    st.step(ins)
            ins.then_inc(S("log_a"), 1)
            for n in range(2):
                read(dve, f"yl{n}")
            dve.wait_ge(S("xc_ready"), 1)
            st.step(dve.tensor_tensor(gelu_t, yl[:, :, :], yl[:, :, :], ALU.mult))
            st.sync()
            st.step(dve.tensor_scalar(gelu_t, gelu_t, 0.044715, 1.0, ALU.mult, ALU.add))
            st.sync()
            dve.tensor_tensor(gelu_t, gelu_t, yl[:, :, :], ALU.mult).then_inc(S("gelu_in"), 1)
            dve.wait_ge(S("tanh_log_a"), 1)
            st.step(dve.tensor_scalar(gate_a[:, :, :], spare, -1.0, 1.0, ALU.mult, ALU.add))
            st.sync()
            st.step(dve.reciprocal(gate_a[:, :, :], gate_a[:, :, :]))
            st.sync()
            dve.scalar_tensor_tensor(spare, spare, -2.0, gate_a[:, :, :], ALU.mult, ALU.mult).then_inc(S("mult2"), 1)
            for n in range(2):
                read(dve, f"gx{n}")
            st.step(dve.scalar_tensor_tensor(gate_x[:, :, :], gate_x[:, :, :], 1.0, xc[:, :, :], ALU.add, ALU.mult))
            st.sync()
            dve.wait_ge(S("mult_ready"), 1)
            st.step(dve.scalar_tensor_tensor(gate_x[:, :, :], gate_x[:, :, :], 0.5, spare, ALU.mult, ALU.mult))
            st.sync()
            dve.wait_ge(S("decay_ready"), 1)
            for c in range(4):
                st.step(dve.tensor_tensor_scan(lru[:, c, :], decay[:, c, :], gate_x[:, c, :], 0.0, ALU.mult, ALU.add))
            dve.wait_ge(S("gelu_tanh"), 1)
            st.step(dve.scalar_tensor_tensor(yl[:, :, :], gelu_t, 1.0, yl[:, :, :], ALU.add, ALU.mult))
            st.sync()
            st.step(dve.scalar_tensor_tensor(lru, lru, 0.5, yl[:, :, :], ALU.mult, ALU.mult))
            st.sync()
            dve.tensor_tensor(lsq[:, :, :], lru, lru, ALU.mult).then_inc(S("sq_ready"), 1)

            def rms(job, x, at):
                take(dve, job)
                dve.tensor_scalar(rms_v, bank(job)[:, 0:T], 1.0 / DL, EPS, ALU.mult, ALU.add).then_inc(free(job), 1)
                read(dve, job)
                rsq(rms_y, rms_v, rms_t)
                for c in range(4):
                    dve.scalar_tensor_tensor(x[:, c, :], x[:, c, :], pflat[:, at + c:at + c + 1], rms_y, ALU.mult, ALU.mult
                                             ).then_inc(S("merged2"), 1)

            dve.wait_ge(S("toep_landed"), 16)
            for hd in range(H2):
                take(dve, f"a{hd}")
                b = bank(f"a{hd}")
                st.step(dve.scalar_tensor_tensor(probs2[:, hd, 0:P], b[:, 0:P], HD2 ** -0.5, toep[:, hd, P:T], ALU.mult, ALU.add))
                dve.scalar_tensor_tensor(probs2[:, hd, P:3 * P], b[:, P:3 * P], HD2 ** -0.5, toep[:, hd, :], ALU.mult, ALU.add
                                         ).then_inc(free(f"a{hd}"), 1)
                read(dve, f"a{hd}")
                st.step(dve.tensor_reduce(nmax2[:, hd, 0:1], probs2[:, hd, 0:P], AX, ALU.max))
                st.step(dve.tensor_reduce(nmax2[:, hd, 1:2], probs2[:, hd, P:3 * P], AX, ALU.max))
                st.sync()
                dve.tensor_scalar(nmax2[:, hd, :], nmax2[:, hd, :], -1.0, None, ALU.mult).then_inc(S("negmax2"), 1)
            rms("rms0", lru, 88)
            for hd in range(H2):
                dve.wait_ge(S("exp2"), 2 * hd + 2)
                st.step(dve.reciprocal(sums2[:, hd, :], sums2[:, hd, :]))
                st.sync()
                st.step(dve.tensor_scalar(probs2[:, hd, 0:P], probs2[:, hd, 0:P], sums2[:, hd, 0:1], None, ALU.mult))
                dve.tensor_scalar(probs2[:, hd, P:3 * P], probs2[:, hd, P:3 * P], sums2[:, hd, 1:2], None, ALU.mult
                                  ).then_inc(S("p2_ready"), 1)
            for c in range(4):
                read(dve, f"c{c}")
            dve.tensor_tensor(lsq[:, :, :], attn, attn, ALU.mult).then_inc(S("sq_ready"), 1)
            for n in range(8, 12):
                ada(n)
            rms("rms1", attn, 92)
            for n in range(8, 12):
                ada_out(n)
            read(dve, "ada11")
            dve.tensor_scalar(modc[:, 32:40], modc[:, 32:40], 1.0, None, ALU.add).then_inc(S("scale2"), 1)
            for half in range(2):
                take(dve, "g2b0" if half else "g1b1")
                for c in range(4):
                    at = 40 + 4 * half + c
                    ins = dve.tensor_scalar(diag[:, c, :], ident, modc[:, at:at + 1], None, ALU.mult)
                    if c < 3:
                        st.step(ins)
                ins.then_inc(S("diag2"), 1)
            read(dve, "g1b0")
            read(dve, "g1b1")
            for n in range(2):
                for t in range(NT):
                    job = f"wo{t}{n}"
                    take(dve, job)
                    part = h[:, t, n * 512:(n + 1) * 512]
                    tmp = xn[:, t, n * 512:(n + 1) * 512]
                    dve.tensor_tensor(tmp, bank(job)[:, :], g1row[:, n * 512:(n + 1) * 512], ALU.mult).then_inc(free(job), 1)
                    read(dve, job)
                    st.step(dve.scalar_tensor_tensor(part, part, ALPHA_2, tmp, ALU.mult, ALU.add))
            st.sync()
            moments(h)
            normed(h, None)
            st.sync()
            dve.wait_ge(S("gain2_landed"), 32)
            affine(dve, st)
            st.sync()
            moments(h)
            normed(xn, S("xn3_ready"))
            dve.wait_ge(S("xn3_ready"), 2)
            dve.sem_inc(S("gain_used"), 1)
            dve.wait_ge(hT_high, 4 * DEPTH + 3)
            dve.tensor_tensor(hl[:, :, :], hT[:, :, :], hh[:, :, :].bitcast(F32), ALU.subtract).then_inc(hT_split, 1)
            fed = []

            def feed(n):
                for _ in range(n):
                    c = len(fed)
                    split_low(dve, (MOE_FIRST + c, c % 2), expert_chunk(c // 4, c % 4))
                    fed.append(c)

            take(dve, "router")
            dve.wait_ge(S("rbias_landed"), 32)
            dve.tensor_tensor(logit, bank("router")[:, 0:72].rearrange("p (t n) -> p t n", t=NT),
                              rbias.unsqueeze(1).broadcast_to([P, NT, 36]), ALU.add).then_inc(free("router"), 1)
            read(dve, "router")

            feed(2)

            def wide(x, n):
                return x.unsqueeze(2).broadcast_to([P, NT, n])

            def first_max(src, n, mx, t1, dst):
                iota = cst[:, C_IOTA:C_IOTA + n].unsqueeze(1).broadcast_to([P, NT, n])
                st.sync()
                st.step(dve.tensor_reduce(mx, src, AX, ALU.max))
                st.sync()
                st.step(dve.tensor_tensor(t1, src, wide(mx, n), ALU.is_lt))
                st.sync()
                st.step(dve.scalar_tensor_tensor(t1, t1, 100.0, iota, ALU.mult, ALU.add))
                st.sync()
                st.step(dve.tensor_reduce(rix, t1, AX, ALU.min))
                st.sync()
                st.step(dve.tensor_tensor(dst, iota, wide(rix, n), ALU.is_equal))
                st.sync()

            first_max(logit[:, :, 0:4], GROUPS, rmx, rg1, ohg)
            dve.tensor_tensor(rg2, logit[:, :, 0:4], wide(rmx, 4), ALU.subtract).then_inc(S("group_shift"), 1)
            dve.wait_ge(S("group_exp"), 1)
            st.step(dve.tensor_reduce(rs1, rg2, AX, ALU.add))
            st.sync()
            st.step(dve.reciprocal(rs1, rs1))
            feed(1)
            st.step(dve.tensor_scalar(rg1, ohg, 1.0, 1e30, ALU.subtract, ALU.mult))
            st.sync()
            for t in range(NT):
                st.step(dve.tensor_tensor(rt1[:, t, :].rearrange("p (g n) -> p g n", g=GROUPS),
                                          logit[:, t, 4:36].rearrange("p (g n) -> p g n", g=GROUPS),
                                          rg1[:, t, :].unsqueeze(2).broadcast_to([P, GROUPS, PER_GROUP]), ALU.add))
            first_max(rt1, EXPERTS, rm1, rt2, oh1)
            feed(1)
            st.step(dve.scalar_tensor_tensor(rt3, oh1, -3e30, rt1, ALU.mult, ALU.add))
            first_max(rt3, EXPERTS, rmx, rt2, oh2)
            dve.tensor_tensor(rs2, rmx, rm1, ALU.subtract).then_inc(S("pair_shift"), 1)
            feed(1)
            dve.wait_ge(S("pair_exp"), 1)
            st.step(dve.tensor_scalar(rs3, rs2, 1.0, None, ALU.add))
            st.sync()
            st.step(dve.reciprocal(rs3, rs3))
            st.sync()
            st.step(dve.tensor_tensor(rs3, rs3, rs1, ALU.mult))
            st.sync()
            st.step(dve.tensor_tensor(rs2, rs2, rs3, ALU.mult))
            st.sync()
            st.step(dve.tensor_tensor(rt1, oh1, wide(rs3, EXPERTS), ALU.mult))
            st.step(dve.tensor_tensor(rt2, oh2, wide(rs2, EXPERTS), ALU.mult))
            st.sync()
            st.step(dve.tensor_tensor(gate_e, rt1, rt2, ALU.add))
            st.step(dve.memset(yacc, 0.0))
            st.sync()
            dve.sem_inc(S("moe_act"), 2)

            def low_of(n, s, c):
                split_low(dve, (n, c % 2), expert_chunk(s, c))

            def hidden(e, s):
                for fc in range(2):
                    n = e * 2 + (fc + 1)
                    b = ps[2 * s + fc]
                    dve.wait_ge(S("moe_tanh"), n)
                    dve.scalar_tensor_tensor(moe_t[fc], moe_t[fc], 1.0, b[:, 0:T], ALU.add, ALU.mult).then_inc(S("moe_y"), 1)
                    dve.wait_ge(S("moe_y"), n)
                    dve.scalar_tensor_tensor(moe_a[:, fc, :], moe_t[fc], 0.5, b[:, T:2 * T], ALU.mult, ALU.mult
                                             ).then_inc(S("moe_act"), 1)

            def parts(e):
                dve.wait_ge(S("moe_act"), e * 2 + 4)
                split_act(dve, e, moe_a, lambda x: x[:, :, :])

            def weigh(e):
                for t in range(NT):
                    for n in range(2):
                        acc = yacc[:, t, n * 512:(n + 1) * 512]
                        ins = dve.scalar_tensor_tensor(acc, ps[4 + 2 * t + n][:, :], gate_e[:, t, ds(e, 1)], acc,
                                                       ALU.mult, ALU.add)
                ins.then_inc(S("down_used"), 1)

            feed(1)
            hidden(0, 0)
            parts(0)
            feed(2)
            with dve.Fori(0, EXPERTS // 2 - 1) as i:
                for s in range(2):
                    e = i * 2 + s
                    n = i * 12 + (MOE_FIRST + 8 + 6 * s)
                    low_of(n, s, 4)
                    hidden(e + 1, 1 - s)
                    low_of(n + 1, s, 5)
                    low_of(n + 2, s, 0)
                    dve.wait_ge(S("down_full"), e + 1)
                    parts(e + 1)
                    low_of(n + 3, s, 1)
                    weigh(e)
                    low_of(n + 4, s, 2)
                    low_of(n + 5, s, 3)
            last = MOE_FIRST + 6 * EXPERTS
            low_of(last - 4, 0, 4)
            hidden(EXPERTS - 1, 1)
            low_of(last - 3, 0, 5)
            dve.wait_ge(S("down_full"), EXPERTS - 1)
            parts(EXPERTS - 1)
            low_of(last - 2, 1, 4)
            weigh(EXPERTS - 2)
            low_of(last - 1, 1, 5)
            dve.wait_ge(S("down_full"), EXPERTS)
            weigh(EXPERTS - 1)
            dve.wait_ge(S("down_used"), EXPERTS + 1)
            read(dve, "g2b0")
            read(dve, "g2b1")
            for t in range(NT):
                st.step(dve.tensor_tensor(yacc[:, t, :], yacc[:, t, :], g2row, ALU.mult))
                st.sync()
                st.step(dve.scalar_tensor_tensor(h[:, t, :], h[:, t, :], ALPHA_2, yacc[:, t, :], ALU.mult, ALU.add))
            st.sync()
            moments(h)
            normed(h, None)
            st.sync()
            dve.wait_ge(S("gain2_landed"), 64)
            for t in range(NT):
                st.step(dve.tensor_tensor(h[:, t, :], h[:, t, :], gain2, ALU.mult))
                st.sync()
                dve.tensor_tensor(h[:, t, :], h[:, t, :], bias2, ALU.add).then_inc(S("out_ready"), 1)

        def affine(dve, st):
            for t in range(NT):
                st.step(dve.tensor_tensor(h[:, t, :], h[:, t, :], gain2, ALU.mult))
                st.sync()
                st.step(dve.tensor_tensor(h[:, t, :], h[:, t, :], bias2, ALU.add))

        def second_pool(pool, st):
            meet(pool, "gpsimd", DEPTH, st)
            st.step(pool.memset(rows2, 0.0))
            st.sync()
            at = 0
            for name, src in (("c", A["c_2"].rearrange("b (c p) -> (b c) p", p=P)),
                              ("ada", A["b_ada_2"].rearrange("l (c p) -> (l c) p", p=P)),
                              ("conv", A["conv_w_2"].rearrange("l k (c p) -> (l k c) p", p=P)),
                              ("conv_b", A["conv_b_2"].rearrange("l (c p) -> (l c) p", p=P)),
                              ("ba", A["b_gate_a_2"].rearrange("l (c two) n -> (l c) (two n)", two=2)),
                              ("bx", A["b_gate_x_2"].rearrange("l (c two) n -> (l c) (two n)", two=2)),
                              ("lam", A["lru_lambda_2"].rearrange("l (c p) -> (l c) p", p=P)),
                              ("nl", A["norm_lru_g_2"].rearrange("l (c p) -> (l c) p", p=P)),
                              ("na", A["norm_attn_g_2"].rearrange("l (c p) -> (l c) p", p=P))):
                n = src.shape[0]
                pool.dma_start(rows2[at:at + n, :], src).then_inc(S("rows2_landed"), 16)
                at += n
            assert at == 96
            pool.dma_start(rel[0:BUCKETS, :], A["rel_bias_2"]).then_inc(S("rel_landed"), 16)
            pool.memset(rel[BUCKETS:BUCKETS + 1, :], MASKED).then_inc(S("rel_mask"), 1)
            pool.wait_ge(S("rel_mask"), 1)
            st.step(pool.memset(wbd, 0.0))
            pool.memset(xlpad[:, :, 0:CONV - 1], 0.0).then_inc(S("xl_zero"), 1)
            st.sync()
            for n, name in enumerate(("w_gate_a_2", "w_gate_x_2")):
                for b in range(H2):
                    half = slice(64 * (b % 2), 64 * (b % 2) + 64)
                    pool.dma_start(wbd[half, 4 * n + b // 2, half], A[name][0, b]).then_inc(S("wbd_landed"), 16)
            pool.wait_ge(S("p2_ready"), H2)
            for dst, name in ((gain2, "ln1_g_2"), (bias2, "ln1_b_2")):
                pool.dma_start(dst, A[name].broadcast_to([P, D])).then_inc(S("gain2_landed"), 16)
            pool.wait_ge(S("gain2_landed"), 32)
            read(pool, "rows2")
            for at, n, name in ((0, GROUPS, "b_router_group_2"), (GROUPS, EXPERTS, "b_router_expert_2")):
                pool.dma_start(rbias[:, at:at + n], A[name].broadcast_to([P, n])).then_inc(S("rbias_landed"), 16)
            pool.wait_ge(S("gain_used"), 1)
            for dst, name in ((gain2, "ln2_g_2"), (bias2, "ln2_b_2")):
                pool.dma_start(dst, A[name].broadcast_to([P, D])).then_inc(S("gain2_landed"), 16)


        block = ctx.enter_context(nc.Block())

        @block.sync
        def _(sp):
            def slot_wait(sem, n):
                sp.wait_ge(sem, n)
                sp.sem_inc(S("sp_waited"), 1)

            sp.dma_start(cst[:, :], A["const"]).then_inc(S("const_landed"), 16)
            sp.dma_start(h[:, :, :], A["x"].rearrange("b (t p) d -> p (b t) d", p=P)).then_inc(S("x_landed"), 16)

            def ffn_weights(l, f):
                wg, wu, wd = A[f"ffn{f + 1}_w_gate"], A[f"ffn{f + 1}_w_up"], A[f"ffn{f + 1}_w_down"]
                base = l * (2 * FFN_CHUNKS) + f * FFN_CHUNKS

                def pair(i, later):
                    for s in range(2):
                        cols = ds(i * (2 * P) + s * P, P)
                        if later is not None:
                            slot_wait(low, later + (3 * s + 3))
                        for n, w in enumerate((wg, wu)):
                            sp.dma_start(F[s][:, n * D:(n + 1) * D].rearrange("p (k n) -> p k n", k=KD),
                                         w[l].rearrange("(k p) n -> p k n", p=P)[:, :, cols]).then_inc(F_gu_landed[s], 16)
                        if later is not None:
                            slot_wait(low, later + (3 * s + 6))
                        sp.dma_start(F[s][:, 2 * D:3 * D], wd[l, cols, :]).then_inc(F_d_landed[s], 16)

                slot_wait(low, base + 1)
                pair(0, None)
                with sp.Fori(0, NF // 2 - 1) as i:
                    pair(i + 1, base + i * 6)

            w_in = A["w_in"].rearrange("l (k p) n -> l p k n", p=P)

            def unit(l, u, src, cols, at=0, wait=True):
                s = u % 2
                if wait:
                    slot_wait(W_free[s], l * UNITS_PER_SLOT + (u // 2 + 1))
                k = src.shape[1]
                sp.dma_start(W[s][:, at:at + k * cols].rearrange("p (k n) -> p k n", k=k), src).then_inc(W_landed[s], 16)

            with sp.Fori(0, DEPTH) as l:
                ffn_weights(l, 0)
                win = w_in[l]
                for u, (at, n) in enumerate(((OFF_GLU, 512), (OFF_GLU + 512, 512), (0, 512), (512, 512), (1024, 512),
                                             (OFF_Z, 520), (OFF_CQ, QL), (OFF_CKV, KVL + ROPE))):
                    unit(l, u, win[:, :, at:at + n], n)
                unit(l, 8, A["mla_w_uq"][l].rearrange("(k p) n -> p k n", p=P), HEADS * (NOPE + ROPE))
                unit(l, 9, A["mla_w_ukv"][l].rearrange("(k p) n -> p k n", p=P), HEADS * (NOPE + VD))
                with sp.Fori(0, KD // 2) as i:
                    for s in range(2):
                        slot_wait(W_free[s], l * UNITS_PER_SLOT + i + 6)
                        for b, w in enumerate(("dn_w_o", "cv_w_pw2", "mla_w_o")):
                            sp.dma_start(W[s][:, b * D:(b + 1) * D].rearrange("p (k n) -> p k n", k=KD),
                                         win[:, :, ds(i * (2 * P) + (OFF_GATE + b * D + s * P), P)]).then_inc(W_landed[s], 16)
                            sp.dma_start(W[s][:, 3 * D + b * 512:3 * D + (b + 1) * 512].rearrange("p (k n) -> p k n", k=4),
                                         A[w][l].rearrange("(k p) n -> p k n", p=P)[:, :, ds(i * (2 * P) + s * P, P)]
                                         ).then_inc(W_landed[s], 16)
                for n in range(2):
                    unit(l, 18 + n, A["w_out"][l].rearrange("(k p) n -> p k n", p=P)[:, :, n * 512:(n + 1) * 512], 512)
                slot_wait(S("mixer_read"), l + 1)
                ffn_weights(l, 1)
            second_sync(sp)

        @block.tensor
        def _(pe):
            owed = []

            def mm(out_, lhsT, rhs, start, stop):
                ins = pe.matmul(out_, lhsT, rhs, start=start, stop=stop)
                if owed:
                    ins.then_inc(owed.pop(0), 1)
                return ins

            def turn(out_, in_, n=P):
                ins = pe.transpose(out_, in_, ident[0:n, 0:n])
                if owed:
                    ins.then_inc(owed.pop(0), 1)
                return ins

            def begin(job):
                if ROUND[job]:
                    pe.wait_ge(bank_free[BANK[job]], ROUND[job])
                return ps[BANK[job]]

            def end(job, ins):
                ins.then_inc(bank_full[BANK[job]], 1)

            def wide_product(dst, n, s):
                pe.wait_ge(high, n + 1)
                for x in (hh, hl):
                    for k in range(KD):
                        mm(dst, wh[:, s, k * P:(k + 1) * P], x[:, k, :], x is hh and k == 0, False)
                pe.wait_ge(low, n + 2)
                for k in range(KD):
                    ins = mm(dst, wl[:, s, k * P:(k + 1) * P], hh[:, k, :], False, k == KD - 1)
                return ins

            def tall_product(first_bank, n, s, a, start, stop):
                pe.wait_ge(high, n + 1)
                for t in range(NT):
                    for c in range(2):
                        for x in (ah, al):
                            mm(ps[first_bank + t * 2 + c][:, :], x[:, a, t * P:(t + 1) * P], wh[:, s, c * 512:(c + 1) * 512],
                               start and x is ah, False)
                pe.wait_ge(low, n + 2)
                for t in range(NT):
                    for c in range(2):
                        ins = mm(ps[first_bank + t * 2 + c][:, :], ah[:, a, t * P:(t + 1) * P],
                                 wl[:, s, c * 512:(c + 1) * 512], False, stop)
                return ins

            def gate_up(c, s, n, first=False, base=0):
                if not first:
                    pe.wait_ge(S("ffn_act"), c + (base - 1))
                n, at = n
                for x in range(2):
                    ins = wide_product(ps[4 + s][:, x * T:(x + 1) * T], n + x, (at + x) % 2)
                    if x == 0:
                        ins.then_inc(used, 1)
                ins.then_inc(S("gu_full"), 1)
                owed.append(used)

            def down(c, n, start=False, stop=False, base=0):
                pe.wait_ge(S("act_split"), c + (base + 1))
                n, at = n
                ins = tall_product(0, n, at, 0, start, stop)
                if stop:
                    ins.then_inc(S("acc_full"), 1)
                    owed.append(used)
                else:
                    ins.then_inc(used, 1)

            def ffn(l, f):
                n = l * (2 * FFN_CHUNKS) + f * FFN_CHUNKS
                b = f * NF
                pe.wait_ge(hT_split, l * 2 + (f + 1))
                gate_up(0, 0, (n, 0), first=True)
                gate_up(1, 1, (n + 2, 0), first=True)
                down(0, (n + 4, 0), start=True, base=b)
                with pe.Fori(0, NF // 2 - 1) as i:
                    c = i * 2
                    m = n + i * 6
                    gate_up(c, 0, (m + 5, 1), base=b + 2)
                    down(c, (m + 7, 1), base=b + 1)
                    gate_up(c, 1, (m + 8, 0), base=b + 3)
                    down(c, (m + 10, 0), base=b + 2)
                down(NF - 1, (n + (FFN_CHUNKS - 1), 1), stop=True, base=b)

            def turn_h(k):
                for t in range(NT):
                    pe.wait_ge(S("xn_ready"), NT * k + t + 1)
                    for c in range(KD):
                        ins = turn(ps[4 + c // 2][:, (c % 2) * T + t * P:(c % 2) * T + (t + 1) * P],
                                   h[:, t, c * P:(c + 1) * P])
                        if t == NT - 1 and c % 2:
                            ins.then_inc(S("tr_full"), 1)

            def hT_wait(k):
                pe.wait_ge(S("hT_act"), k)
                pe.wait_ge(S("hT_dve"), k)

            def land(l, u):
                pe.wait_ge(W_landed[u % 2], l * LANDED_PER_LAYER[u % 2] + LANDED[u])

            def features(l, u, jobs, width, K, rhs, offs):
                land(l, u)
                for n, job in enumerate(jobs):
                    b = begin(job)
                    for c in range(2):
                        off = offs[2 * n + c]
                        for k in range(K):
                            ins = mm(b[:, c * T:(c + 1) * T], W[u % 2][:, k * width + off:k * width + off + P],
                                     rhs[:, k, :], k == 0, k == K - 1)
                    end(job, ins)

            def tokens(l, u, jobs, width, K, lhs, a, n):
                for t, job in enumerate(jobs):
                    b = begin(job)
                    for k in range(K):
                        ins = mm(b[:, 0:n], lhs[:, k, t * P:(t + 1) * P],
                                 W[u % 2][:, k * width + a:k * width + a + n], k == 0, k == K - 1)
                    end(job, ins)

            def turns(job, blocks):
                b = begin(job)
                for at, src in blocks:
                    ins = turn(b[:, at:at + P], src)
                end(job, ins)

            def heads(job, lhs, rhs):
                b = begin(job)
                for hd in range(HEADS):
                    ins = mm(b[:, hd * P:(hd + 1) * P], lhs(hd), rhs(hd), True, True)
                end(job, ins)

            for s in range(2):
                pe.sem_inc(W_free[s], 1)
            pe.sem_inc(used, 2)
            pe.wait_ge(S("const_landed"), 16)
            pe.wait_ge(S("x_landed"), 16)
            for c in range(KD):
                for t in range(NT):
                    ins = turn(ps[4 + c // 2][:, (c % 2) * T + t * P:(c % 2) * T + (t + 1) * P], h[:, t, c * P:(c + 1) * P])
                if c % 2:
                    ins.then_inc(S("x_turned"), 1)

            with pe.Fori(0, DEPTH) as l:
                meet(pe, "tensor", l, Steps(pe, S("pe_steps")))
                ffn(l, 0)
                pe.wait_ge(S("rows_landed"), l * (16 * len(ROWS)) + 16 * len(ROWS))
                for a in range(3):
                    ins = turn(ps[6][:, a * P:(a + 1) * P], prow[:, a, :])
                ins.then_inc(S("rows_full"), 1)
                pe.wait_ge(S("cols_ready"), 1)
                turn_h(0)
                hT_wait(1)

                for u, jobs in enumerate((("gv0", "gv1"), ("gg0", "gg1"), ("q0", "q1"), ("k0", "k1"), ("v0", "v1"))):
                    features(l, u, jobs, 512, KD, hT, [0, P, 2 * P, 3 * P])
                    owed.append(W_free[u % 2])
                land(l, 5)
                tokens(l, 5, ("z0", "z1"), 520, KD, hT, 0, 512)
                b = begin("ab")
                for t in range(NT):
                    for k in range(KD):
                        ins = mm(b[:, t * 8:(t + 1) * 8], hT[:, k, t * P:(t + 1) * P],
                                 W[1][:, k * 520 + 512:k * 520 + 520], k == 0, k == KD - 1)
                end("ab", ins)
                owed.append(W_free[1])
                land(l, 6)
                tokens(l, 6, ("cq0", "cq1"), QL, KD, hT, 0, QL)
                owed.append(W_free[0])
                land(l, 7)
                tokens(l, 7, ("ck0", "ck1"), KVL + ROPE, KD, hT, 0, KVL + ROPE)
                owed.append(W_free[1])

                b = begin("G")
                pe.wait_ge(S("g_ready"), 1)
                for t in range(NT):
                    mm(b[:, t * 8:t * 8 + 4], tri, g[:, t, :], True, True)
                    ins = mm(b[:, t * 8 + 4:t * 8 + 8], ones[:, :], g[:, t, :], True, True)
                end("G", ins)
                for x, part in enumerate("qkv"):
                    pe.wait_ge(S("dn_silu"), x + 1)
                    for t in range(NT):
                        turns(f"tok_{part}{t}", [(hd * P, dn[:, x * 4 + hd, t * P:(t + 1) * P]) for hd in range(HEADS)])
                pe.wait_ge(S("cq_ready"), 2)
                turns("cqTa", [(c * T + t * P, cqn[:, t, c * P:(c + 1) * P]) for c in range(2) for t in range(NT)])
                turns("cqTb", [(t * P, cqn[:, t, 2 * P:3 * P]) for t in range(NT)])
                pe.wait_ge(S("ck_ready"), 2)
                turns("ckvT", [(c * T + t * P, ckn[:, t, c * P:(c + 1) * P]) for c in range(2) for t in range(NT)])
                pe.wait_ge(S("kr_ready"), 1)
                turns("krT", [(t * P, krd[:, t, :, :].rearrange("p a b -> p (a b)")) for t in range(NT)])
                for t in range(NT):
                    b = begin(f"Gb{t}")
                    pe.wait_ge(S("trig"), 1)
                    end(f"Gb{t}", mm(b[:, :], ones[:, :], Pm[:, t, :, :].rearrange("p h j -> p (h j)"), True, True))
                for job in ("cqTa", "cqTb", "ckvT"):
                    read(pe, job)
                features(l, 8, ("qn0", "qn1"), HEADS * (NOPE + ROPE), 3, cqT, [hd * (NOPE + ROPE) for hd in range(HEADS)])
                b = begin("qr")
                uq = W[0][:, 0:3 * HEADS * (NOPE + ROPE)].rearrange("p (k h n) -> p k h n", k=3, h=HEADS)
                for t in range(NT):
                    for k in range(3):
                        ins = mm(b[:, t * T:(t + 1) * T], cqT[:, k, t * P:(t + 1) * P], uq[:, k, :, NOPE:], k == 0, k == 2)
                end("qr", ins)
                owed.append(W_free[0])
                pe.wait_ge(S("qk_norm"), 2)
                for t in range(NT):
                    turns(f"qT{t}", [(hd * P, qt[:, t, hd, :]) for hd in range(HEADS)])
                for t in range(NT):
                    turns(f"kT{t}", [(hd * P, kt[:, t, hd, :]) for hd in range(HEADS)])
                pe.wait_ge(S("kb_ready"), 1)
                for t in range(NT):
                    turns(f"kbT{t}", [(hd * P, kb[:, t, hd, :]) for hd in range(HEADS)])
                features(l, 9, ("kn0", "kn1"), HEADS * (NOPE + VD), 2, ckvT, [hd * (NOPE + VD) for hd in range(HEADS)])
                ukv = W[1][:, 0:2 * HEADS * (NOPE + VD)].rearrange("p (k h n) -> p k h n", k=2, h=HEADS)
                for t in range(NT):
                    b = begin(f"mv{t}")
                    for k in range(2):
                        ins = mm(b[:, :], ckvT[:, k, t * P:(t + 1) * P], ukv[:, k, :, NOPE:], k == 0, k == 1)
                    end(f"mv{t}", ins)
                owed.append(W_free[1])
                for job in ("qT0", "qT1", "kT0", "kT1", "kbT0", "kbT1"):
                    read(pe, job)
                for t in range(NT):
                    heads(f"kk{t}", lambda hd: kT[:, t, hd, :], lambda hd: kbT[:, t, hd, :])
                for t in range(NT):
                    heads(f"qk{t}", lambda hd: kT[:, t, hd, :], lambda hd: qT[:, t, hd, :])
                pe.wait_ge(S("qr_ready"), 2)
                turns("qrT", [(pr * T + t * P, qr[:, t, 2 * pr:2 * pr + 2, :].rearrange("p a b -> p (a b)"))
                              for pr in range(2) for t in range(NT)])
                for job in ("qn0", "qn1", "kn0", "kn1", "krT", "qrT"):
                    read(pe, job)
                for hd in range(HEADS):
                    b = begin(f"s{hd}")
                    half = slice(64 * (hd % 2), 64 * (hd % 2) + 64)
                    for t in range(NT):
                        n = (t + 1) * P
                        o_ = b[:, t * P:t * P + n]
                        mm(o_, qnT[:, hd, t * P:(t + 1) * P], knT[:, hd, 0:n], True, False)
                        ins = mm(o_, qrT[half, hd // 2, t * P:(t + 1) * P], krT[half, 0:n], False, True)
                    end(f"s{hd}", ins)
                for lev in range(LEVELS):
                    for t in range(NT):
                        pe.wait_ge(S("lev_mask"), NT * lev + t + 1)
                        if lev:
                            read(pe, f"MP{t}.{lev - 1}")
                        else:
                            pe.wait_ge(S("M_init"), 2)
                        heads(f"P{t}.{lev}", lambda hd: ATl[lev % 2][:, t, hd, :], lambda hd: M[:, t, hd, :])
                    for t in range(NT):
                        read(pe, f"P{t}.{lev}")
                        if lev:
                            read(pe, f"MPT{t}.{lev - 1}")
                        heads(f"MP{t}.{lev}", lambda hd: MT[:, t, hd, :], lambda hd: Pm[:, t, hd, :])
                        heads(f"MPT{t}.{lev}", lambda hd: Pm[:, t, hd, :], lambda hd: MT[:, t, hd, :])
                for hd in range(HEADS):
                    pe.wait_ge(S("p_ready"), hd + 1)
                    turns(f"p{hd}", [(c * P, prob[hd][:, c * P:(c + 1) * P]) for c in range(3)])
                read(pe, "mv0")
                read(pe, "mv1")
                for pr in range(2):
                    b = begin(f"mo{pr}")
                    for hd in (2 * pr, 2 * pr + 1):
                        read(pe, f"p{hd}")
                        at = (hd % 2) * T
                        mm(b[:, at:at + P], mv[:, 0, hd, :], PT[:, hd, 0:P], True, True)
                        mm(b[:, at + P:at + T], mv[:, 0, hd, :], PT[:, hd, P:2 * P], True, False)
                        ins = mm(b[:, at + P:at + T], mv[:, 1, hd, :], PT[:, hd, 2 * P:3 * P], False, True)
                    end(f"mo{pr}", ins)
                for t in range(NT):
                    read(pe, f"MPT{t}.{LEVELS - 1}")
                pe.wait_ge(S("vb_ready"), 1)
                heads("vn0", lambda hd: MT[:, 0, hd, :], lambda hd: vt[:, 0, hd, :])
                pe.wait_ge(S("kdec_ready"), 1)
                read(pe, "vn0")
                heads("S1", lambda hd: kdec[:, hd, :], lambda hd: vn0[:, hd, :])
                read(pe, "S1")
                heads("KS", lambda hd: kbT[:, 1, hd, :], lambda hd: S1[:, hd, :])
                read(pe, "KS")
                heads("vn1", lambda hd: MT[:, 1, hd, :], lambda hd: Rn[:, hd, :])
                read(pe, "qk0")
                read(pe, "qk1")
                heads("O0", lambda hd: QK[:, 0, hd, :], lambda hd: vn0[:, hd, :])
                read(pe, "vn1")
                heads("O1", lambda hd: QK[:, 1, hd, :], lambda hd: vn1[:, hd, :])
                heads("O1s", lambda hd: qT[:, 1, hd, :], lambda hd: S1[:, hd, :])
                pe.wait_ge(S("o_ready"), 1)
                for pr in range(2):
                    turns(f"oT{pr}", [(c * T + t * P, o[:, t, 2 * pr + c, :]) for c in range(2) for t in range(NT)])
                pe.wait_ge(S("tap"), 4 * CVK)
                for t in range(NT):
                    turns(f"cvt{t}", [(c * P, cvu[:, c, t * P:(t + 1) * P]) for c in range(4)])
                read(pe, "cvt0")
                read(pe, "cvt1")
                for pr in range(2):
                    turns(f"cvb{pr}", [(c * T + t * P, cvn[:, t, (2 * pr + c) * P:(2 * pr + c + 1) * P])
                                       for c in range(2) for t in range(NT)])
                read(pe, "oT0")
                read(pe, "oT1")
                read(pe, "mo0")
                read(pe, "mo1")
                pe.wait_ge(S("cv_ready"), 1)
                pe.sem_inc(S("gate_used"), 2)
                with pe.Fori(0, KD // 2) as i:
                    for s in range(2):
                        pe.wait_ge(W_landed[s], l * LANDED_PER_LAYER[s] + i * 96 + LANDED[10 + s])
                        pe.wait_ge(S("gate_used"), i * 2 + (s + 1))
                        for b, y in enumerate((oT, cvu, moT)):
                            bk = ps[s * 3 + b]
                            for k in range(KD):
                                mm(bk[:, 0:T], W[s][:, b * D + k * P:b * D + (k + 1) * P], hT[:, k, :], k == 0, k == KD - 1)
                            for k in range(4):
                                ins = mm(bk[:, T:2 * T], W[s][:, 3 * D + b * 512 + k * P:3 * D + b * 512 + (k + 1) * P],
                                         y[:, k, :], k == 0, k == 3)
                            ins.then_inc(S("gate_full"), 1)
                        pe.wait_ge(S("gate_full"), i * 6 + (3 * s + 3))
                        pe.sem_inc(W_free[s], 1)
                pe.wait_ge(S("gate_used"), KD + 2)
                for n in range(2):
                    land(l, 18 + n)
                    for t in range(NT):
                        for k in range(KD):
                            ins = mm(ps[t * 2 + n][:, :], merged[:, k, t * P:(t + 1) * P],
                                     W[n][:, k * 512:(k + 1) * 512], k == 0, k == KD - 1)
                    if n == 0:
                        owed.append(W_free[0])
                ins.then_inc(S("acc_full"), 1)
                owed.append(W_free[1])
                pe.wait_ge(S("acc_full"), 2)
                pe.sem_inc(S("mixer_read"), 1)
                turn_h(1)
                ffn(l, 1)
                turn_h(2)
                assert not owed
            second_tensor(pe, mm, turn, owed, begin, end, wide_product, tall_product)

        @block.scalar
        def _(act_):
            sc = nc.scalar
            st = Steps(act_, S("act_steps"))

            def ffn(l, f):
                base = l * (2 * FFN_CHUNKS) + f * FFN_CHUNKS
                turn = l * NF + f * (NF // 2)

                def high_of(n, at, s, c, use=None):
                    if c == 0:
                        act_.wait_ge(F_gu_landed[s], use * 32)
                    if c == 2:
                        act_.wait_ge(F_d_landed[s], use * 16)
                    split_high(act_, (n, at), F[s][:, c * D:(c + 1) * D])

                def tanh(c, s):
                    act_.wait_ge(S("gu_full"), c + (f * NF + 1))
                    sc.activation(th[s], ps[4 + s][:, 0:T], ACT.Tanh, scale=0.5).then_inc(S("ffn_tanh"), 1)

                high_of(base, 0, 0, 0, turn + 1)
                high_of(base + 1, 1, 0, 1)
                high_of(base + 2, 0, 1, 0, turn + 1)
                tanh(0, 0)
                high_of(base + 3, 1, 1, 1)
                high_of(base + 4, 0, 0, 2, turn + 1)
                with act_.Fori(0, NF // 2 - 1) as i:
                    m = base + i * 6
                    high_of(m + 5, 1, 0, 0, turn + i + 2)
                    tanh(i * 2 + 1, 1)
                    high_of(m + 6, 0, 0, 1)
                    high_of(m + 7, 1, 1, 2, turn + i + 1)
                    high_of(m + 8, 0, 1, 0, turn + i + 2)
                    tanh(i * 2 + 2, 0)
                    high_of(m + 9, 1, 1, 1)
                    high_of(m + 10, 0, 0, 2, turn + i + 2)
                tanh(NF - 1, 1)
                high_of(base + (FFN_CHUNKS - 1), 1, 1, 2, turn + NF // 2)

            def high_banks(n):
                sc.activation(hh[:, 2 * n:2 * n + 2, :], hT[:, 2 * n:2 * n + 2, :], ACT.Copy).then_inc(hT_high, 1)

            def columns(k, which):
                for b in (0, 2):
                    act_.wait_ge(S("tr_full"), 4 * k + b + 1)
                    for c in (2 * b, 2 * b + 1):
                        ins = sc.activation(hT[:, c, :], ps[4 + b][:, (c % 2) * T:(c % 2 + 1) * T], ACT.Identity,
                                            bias=col(f"ln{which}_b", c), scale=col(f"ln{which}_g", c))
                        if c < 5 or k:
                            st.step(ins)
                    if k:
                        st.sync()
                        high_banks(b)
                if not k:
                    ins.then_inc(S("hT_act"), 1)

            def copy(job, dst, scale=1.0, n=512):
                take(act_, job)
                src = bank(job)[:, 0:n]
                if len(dst.shape) == 3:
                    src = src.rearrange("p (a b) -> p a b", a=dst.shape[1])
                sc.activation(dst, src, ACT.Copy, scale=scale).then_inc(free(job), 1)

            for b in (0, 2):
                act_.wait_ge(S("x_turned"), b + 1)
                st.step(sc.activation(hT[:, 2 * b:2 * b + 2, :].rearrange("p a b -> p (a b)"), ps[4 + b][:, :], ACT.Copy))
                st.sync()
                high_banks(b)
            act_.wait_ge(S("angle_ready"), 2)
            st.step(sc.activation(cos[:, :, :], cos[:, :, :], ACT.Sin))
            st.step(sc.activation(sin[:, :, :], sin[:, :, :], ACT.Sin))

            with act_.Fori(0, DEPTH) as l:
                meet(act_, "scalar", l, st)
                ffn(l, 0)
                act_.wait_ge(S("rows_full"), 1)
                sc.activation(pcol[:, :, :], ps[6][:, 0:384].rearrange("p (a n) -> p a n", a=3),
                              ACT.Copy).then_inc(S("cols_ready"), 1)
                act_.wait_ge(S("cols_ready"), 1)
                columns(0, 1)
                act_.wait_ge(S("half_ready"), 1)
                for n in range(2):
                    take(act_, f"gg{n}")
                    for c in (2 * n, 2 * n + 1):
                        ins = sc.activation(cvg[:, c, :], bank(f"gg{n}")[:, (c % 2) * T:(c % 2 + 1) * T], ACT.Tanh,
                                            bias=col("cv_glu_b", 4 + c, half=True), scale=0.5)
                        if c % 2 == 0:
                            st.step(ins)
                    ins.then_inc(free(f"gg{n}"), 1)
                for x, part in enumerate("qkv"):
                    for n in range(2):
                        copy(f"{part}{n}", dnpad[:, 4 * x + 2 * n:4 * x + 2 * n + 2, CONV - 1:])
                act_.wait_ge(S("h_ready"), 1)
                for t in range(NT):
                    take(act_, f"z{t}")
                    sc.activation(z[:, t, :, :].rearrange("p a b -> p (a b)"), bank(f"z{t}")[:, :], ACT.Tanh,
                                  scale=0.5).then_inc(S("z_tanh"), 1)
                for x in range(3):
                    act_.wait_ge(S("dn_tap"), 16 * (x + 1))
                    sc.activation(dnth[:, 4 * x:4 * x + 4, :], dn[:, 4 * x:4 * x + 4, :], ACT.Tanh,
                                  scale=0.5).then_inc(S("dn_tanh"), 1)
                read(act_, "ab")
                sc.activation(beta[:, :, :], abt[:, :, 4:8], ACT.Tanh, scale=0.5).then_inc(S("beta_tanh"), 1)
                act_.wait_ge(S("dt_landed"), l * 32 + 32)
                sc.activation(ea[:, :], dtab[:, 0:4], ACT.Exp).then_inc(S("expa"), 1)
                act_.wait_ge(S("nabs"), 1)
                n = st.step(sc.activation(ab2[:, :, :], ab2[:, :, :], ACT.Exp))
                st.sync(n)
                sc.activation(ab2[:, :, :], ab2[:, :, :], ACT.Ln, bias=1.0).then_inc(S("ln_ready"), 1)
                read(act_, "G")
                sc.activation(eG[:, :, :], Gs[:, :, 0:4], ACT.Exp).then_inc(S("eG_ready"), 1)
                act_.wait_ge(S("dG_ready"), 1)
                sc.activation(eD[:, :], dG[:, :], ACT.Exp).then_inc(S("eD_ready"), 1)
                for part, dst in (("q", qt), ("k", kt), ("v", vt)):
                    for t in range(NT):
                        copy(f"tok_{part}{t}", dst[:, t, :, :])
                for job, chunks in (("cqTa", (0, 1)), ("cqTb", (2,))):
                    take(act_, job)
                    for c in chunks:
                        ins = sc.activation(cqT[:, c, :], bank(job)[:, (c % 2) * T:(c % 2 + 1) * T], ACT.Copy,
                                            scale=col("mla_q_norm_w", c))
                        if c == 0:
                            st.step(ins)
                    ins.then_inc(free(job), 1)
                take(act_, "ckvT")
                for c in range(2):
                    ins = sc.activation(ckvT[:, c, :], bank("ckvT")[:, c * T:(c + 1) * T], ACT.Copy,
                                        scale=col("mla_kv_norm_w", c))
                    if c == 0:
                        st.step(ins)
                ins.then_inc(free("ckvT"), 1)
                copy("krT", krT[:, :], n=T)
                for t in range(NT):
                    read(act_, f"Gb{t}")
                    sc.activation(DT[:, t, :, :], DT[:, t, :, :], ACT.Exp).then_inc(S("dt_exp"), 1)
                for n in range(2):
                    copy(f"qn{n}", qnT[:, 2 * n:2 * n + 2, :])
                for part, dst in (("q", qT), ("k", kT), ("kb", kbT)):
                    for t in range(NT):
                        copy(f"{part}T{t}", dst[:, t, :, :])
                for n in range(2):
                    copy(f"kn{n}", knT[:, 2 * n:2 * n + 2, :])
                for t in range(NT):
                    copy(f"mv{t}", mv[:, t, :, :])
                copy("qrT", qrT[:, :, :])
                for hd in range(HEADS):
                    act_.wait_ge(S("negmax"), 2 * hd + 2)
                    for t in range(NT):
                        cols = slice(0, P) if t == 0 else slice(P, 3 * P)
                        sc.activation(prob[hd][:, cols], prob[hd][:, cols], ACT.Exp, bias=nmax[:, hd, t:t + 1],
                                      scale=(NOPE + ROPE) ** -0.5, accum_out=psums[:, hd, t:t + 1]).then_inc(S("exp_s"), 1)
                for lev in range(LEVELS):
                    for t in range(NT):
                        copy(f"P{t}.{lev}", Pm[:, t, :, :])
                for hd in range(HEADS):
                    copy(f"p{hd}", PT[:, hd, :], n=3 * P)
                for n in range(2):
                    copy(f"mo{n}", moT[:, 2 * n:2 * n + 2, :])
                copy("vn0", vn0)
                copy("S1", S1)
                copy("vn1", vn1, scale=-1.0)
                copy("O0", o[:, 0, :, :])
                copy("O1", o[:, 1, :, :])
                for n in range(2):
                    take(act_, f"oT{n}")
                    sc.activation(oT[:, 2 * n:2 * n + 2, :], bank(f"oT{n}")[:, :].rearrange("p (a b) -> p a b", a=2),
                                  ACT.Copy, scale=col("dn_norm_w", half=True)).then_inc(free(f"oT{n}"), 1)
                for n in range(2):
                    take(act_, f"cvb{n}")
                    for c in (2 * n, 2 * n + 1):
                        ins = sc.activation(cvu[:, c, :], bank(f"cvb{n}")[:, (c % 2) * T:(c % 2 + 1) * T], ACT.Identity,
                                            bias=col("cv_ln_b", c), scale=col("cv_ln_g", c))
                        if c % 2 == 0:
                            st.step(ins)
                    ins.then_inc(free(f"cvb{n}"), 1)
                for n in range(2):
                    read(act_, f"cvb{n}")
                sc.activation(cvg[:, :, :], cvu[:, :, :], ACT.Tanh, scale=0.5).then_inc(S("cv_tanh"), 1)
                with act_.Fori(0, KD // 2) as i:
                    for s in range(2):
                        for b in range(3):
                            act_.wait_ge(S("gate_full"), i * 6 + (3 * s + b + 1))
                            tile, at, _ = ROWS["cv_b_pw2"]
                            if b == 1:
                                sc.activation(gyb[s], ps[s * 3 + b][:, T:2 * T], ACT.Identity,
                                              bias=pcol[:, tile, ds(i * 2 + (at + s), 1)], scale=0.5)
                            tile, at, _ = ROWS["b_gate"]
                            sc.activation(gth[s][b], ps[s * 3 + b][:, 0:T], ACT.Tanh,
                                          bias=phalf[:, tile, ds(i * 2 + (at + b * KD + s), 1)],
                                          scale=0.5).then_inc(S("gate_act"), 1)
                columns(1, 2)
                ffn(l, 1)
                columns(2, 3)
                act_.wait_ge(hT_high, l * 4 + 6)
            second_scalar(act_, st, copy)

        @block.vector
        def _(dve):
            st = Steps(dve, S("dve_steps"))
            dve.sem_inc(low, 1)

            def rsq(y, v, tmp):
                rsqrt(dve, st, y, v, tmp)

            def ffn(l, f):
                base = l * (2 * FFN_CHUNKS) + f * FFN_CHUNKS

                def low_of(n, at, s, c):
                    split_low(dve, (n, at), F[s][:, c * D:(c + 1) * D])

                def hidden(c, s, m=None):
                    done = c + (f * NF + 1)
                    dve.wait_ge(S("ffn_tanh"), done)
                    dve.scalar_tensor_tensor(yb[s], th[s], 1.0, ps[4 + s][:, 0:T], ALU.add, ALU.mult
                                             ).then_inc(S("ffn_y"), 1)
                    dve.wait_ge(S("ffn_y"), done)
                    dve.tensor_tensor(act[s], yb[s], ps[4 + s][:, T:2 * T], ALU.mult).then_inc(S("ffn_act"), 1)
                    if m is not None:
                        dve.wait_ge(used, m + 3)
                    dve.wait_ge(S("ffn_act"), done)
                    split_act(dve, c + f * NF, act[s], lambda x: x[:, 0, :])

                low_of(base, 0, 0, 0)
                low_of(base + 1, 1, 0, 1)
                low_of(base + 2, 0, 1, 0)
                hidden(0, 0)
                low_of(base + 3, 1, 1, 1)
                low_of(base + 4, 0, 0, 2)
                with dve.Fori(0, NF // 2 - 1) as i:
                    m = base + i * 6
                    low_of(m + 5, 1, 0, 0)
                    hidden(i * 2 + 1, 1, m + 4)
                    low_of(m + 6, 0, 0, 1)
                    low_of(m + 7, 1, 1, 2)
                    low_of(m + 8, 0, 1, 0)
                    hidden(i * 2 + 2, 0, m + 7)
                    low_of(m + 9, 1, 1, 1)
                    low_of(m + 10, 0, 0, 2)
                hidden(NF - 1, 1, base + (FFN_CHUNKS - 2))
                low_of(base + (FFN_CHUNKS - 1), 1, 1, 2)

            def pair_of(n):
                return slice(2 * n, 2 * n + 2)

            def low_banks(before):
                st.sync()
                for b in (1, 3):
                    st.step(dve.tensor_copy(hh[:, pair_of(b), :], hT[:, pair_of(b), :]))
                st.sync()
                for b in (1, 3):
                    st.step(dve.tensor_tensor(hl[:, pair_of(b), :], hT[:, pair_of(b), :], hh[:, pair_of(b), :].bitcast(F32),
                                              ALU.subtract))
                st.sync()
                for n, b in enumerate((0, 2)):
                    dve.wait_ge(hT_high, before + (n + 1))
                    ins = dve.tensor_tensor(hl[:, pair_of(b), :], hT[:, pair_of(b), :], hh[:, pair_of(b), :].bitcast(F32),
                                            ALU.subtract)
                    if b == 0:
                        st.step(ins)
                ins.then_inc(hT_split, 1)

            def norm(l, k, which, scale, eps):
                dve.wait_ge(S("acc_full"), k + 1)
                if k:
                    dve.wait_ge(S("h_ready"), k)
                at = {}
                for t in range(NT):
                    for n in range(2):
                        part = h[:, t, n * 512:(n + 1) * 512]
                        at[t, n] = st.step(dve.scalar_tensor_tensor(part, part, scale, ps[t * 2 + n][:, :], ALU.mult, ALU.add))
                for t in range(NT):
                    for n in range(2):
                        st.sync(at[t, n])
                        st.step(dve.bn_stats(stats[:, t, n, :], h[:, t, n * 512:(n + 1) * 512]))
                    st.sync()
                    st.step(dve.bn_aggr(mvar[:, t, :], stats[:, t, :, :].rearrange("p a b -> p (a b)")))
                st.sync()
                st.step(dve.tensor_scalar(rv[:, 0:NT], mvar[:, :, 1], eps, None, ALU.add))
                rsq(ry[:, 0:NT], rv[:, 0:NT], rt[:, 0:NT])
                for t in range(NT):
                    dve.tensor_scalar(h[:, t, :], h[:, t, :], mvar[:, t, 0:1], ry[:, t:t + 1], ALU.subtract, ALU.mult
                                      ).then_inc(S("xn_ready"), 1)
                for b in (1, 3):
                    dve.wait_ge(S("tr_full"), 4 * k + b + 1)
                    for c in (2 * b, 2 * b + 1):
                        ins = dve.tensor_scalar(hT[:, c, :], ps[4 + b][:, (c % 2) * T:(c % 2 + 1) * T],
                                                col(f"ln{which}_g", c), col(f"ln{which}_b", c), ALU.mult, ALU.add)
                        if c < 7 or k:
                            st.step(ins)
                if k:
                    low_banks(l * 4 + 2 * k)
                else:
                    ins.then_inc(S("hT_dve"), 1)

            def scaled(out_, in_, by, n):
                return dve.tensor_tensor(out_, in_, by.unsqueeze(2).broadcast_to([P, n, HD]), ALU.mult)

            def flat(x):
                return x.rearrange("p t h j -> p (t h) j")

            for b in (1, 3):
                dve.wait_ge(S("x_turned"), b + 1)
                st.step(dve.tensor_copy(hT[:, 2 * b:2 * b + 2, :].rearrange("p a b -> p (a b)"), ps[4 + b][:, :]))
            low_banks(0)
            dve.wait_ge(S("pos_landed"), 16 * NT)
            dve.wait_ge(S("const_landed"), 16)
            st.step(dve.tensor_copy(mvar[:, :, 0], pos[:, :]))
            for t in range(NT):
                st.sync()
                st.step(dve.tensor_scalar(angle[:, t, :], cst[:, C_FREQ:C_FREQ + 32], mvar[:, t, 0:1], None, ALU.mult))
            for tab, shift in ((cos, 0.25), (sin, 0.0)):
                st.sync()
                st.step(dve.tensor_scalar(turnsi[:, :, :], angle[:, :, :], 1.0 / (2 * np.pi), shift, ALU.mult, ALU.add))
                st.sync()
                st.step(dve.tensor_copy(turnsf[:, :, :], turnsi[:, :, :]))
                st.sync()
                st.step(dve.scalar_tensor_tensor(tab[:, :, :], turnsf[:, :, :], -TWO_PI[0], angle[:, :, :], ALU.mult, ALU.add))
                for piece in TWO_PI[1:]:
                    st.sync()
                    st.step(dve.scalar_tensor_tensor(tab[:, :, :], turnsf[:, :, :], -piece, tab[:, :, :], ALU.mult, ALU.add))
                st.sync()
                if shift:
                    st.step(dve.tensor_scalar(tab[:, :, :], tab[:, :, :], float(np.pi / 2), None, ALU.add))
                    st.sync()
                dve.tensor_scalar(tab[:, :, :], tab[:, :, :], 3.1415925, -3.1415925, ALU.min, ALU.max
                                  ).then_inc(S("angle_ready"), 1)

            with dve.Fori(0, DEPTH) as l:
                meet(dve, "vector", l, st)
                ffn(l, 0)
                dve.wait_ge(S("cols_ready"), 1)
                dve.tensor_scalar(phalf[:, :, :], pcol[:, :, :], 0.5, None, ALU.mult).then_inc(S("half_ready"), 1)
                norm(l, 0, 1, 4 * ALPHA, 16 * EPS)
                for n in range(2):
                    take(dve, f"gv{n}")
                    for c in (2 * n, 2 * n + 1):
                        ins = dve.tensor_scalar(cvu[:, c, :], bank(f"gv{n}")[:, (c % 2) * T:(c % 2 + 1) * T],
                                                col("cv_glu_b", c), None, ALU.add)
                        if c % 2 == 0:
                            st.step(ins)
                    ins.then_inc(free(f"gv{n}"), 1)
                for n in range(2):
                    read(dve, f"gg{n}")
                    read(dve, f"gv{n}")
                dve.wait_ge(S("half_ready"), 1)
                dve.wait_ge(S("cvpad_zero"), 1)
                dve.scalar_tensor_tensor(cvpad[:, :, PAD:], cvg[:, :, :], 1.0, cvu[:, :, :], ALU.add, ALU.mult
                                         ).then_inc(S("glu_pad"), 1)
                dve.wait_ge(S("glu_pad"), 1)
                tile, at, _ = ROWS["cv_dw_w"]
                for c in range(4):
                    dve.tensor_scalar(cvu[:, c, :], cvpad[:, c, 0:T], phalf[:, tile, at + c:at + c + 1],
                                      col("cv_dw_b", c), ALU.mult, ALU.add).then_inc(S("tap"), 1)
                with dve.Fori(1, CVK) as k:
                    for c in range(4):
                        dve.wait_ge(S("tap"), k * 4 + (c - 3))
                        dve.scalar_tensor_tensor(cvu[:, c, :], cvpad[:, c, ds(k, T)], phalf[:, tile, ds(k * 4 + (at + c), 1)],
                                                 cvu[:, c, :], ALU.mult, ALU.add).then_inc(S("tap"), 1)
                dve.wait_ge(S("dn_zero"), 1)
                tile, at, _ = ROWS["dn_conv_w"]
                for job in ("q0", "q1", "k0", "k1", "v0", "v1"):
                    read(dve, job)
                with dve.Fori(0, 3) as x:
                    for k in range(CONV):
                        for c in range(4):
                            w = pcol[:, tile, ds(x * 4 + (at + 12 * k + c), 1)]
                            src = dnpad[:, ds(x * 4 + c, 1), k:k + T]
                            dst = dn[:, ds(x * 4 + c, 1), :]
                            if k == 0:
                                dve.tensor_scalar(dst, src, w, None, ALU.mult).then_inc(S("dn_tap"), 1)
                            else:
                                dve.wait_ge(S("dn_tap"), x * 16 + (4 * k + c - 3))
                                dve.scalar_tensor_tensor(dst, src, w, dst, ALU.mult, ALU.add).then_inc(S("dn_tap"), 1)
                for x in range(3):
                    dve.wait_ge(S("dn_tanh"), x + 1)
                    part = dn[:, 4 * x:4 * x + 4, :]
                    dve.scalar_tensor_tensor(part, dnth[:, 4 * x:4 * x + 4, :], 1.0, part, ALU.add, ALU.mult
                                             ).then_inc(S("dn_silu"), 1)
                for t in range(NT):
                    dve.wait_ge(S("z_tanh"), t + 1)
                    zt = z[:, t, :, :].rearrange("p a b -> p (a b)")
                    dve.scalar_tensor_tensor(zt, zt, 1.0, bank(f"z{t}")[:, :], ALU.add, ALU.mult).then_inc(free(f"z{t}"), 1)
                take(dve, "ab")
                dve.tensor_copy(abt[:, :, :], bank("ab")[:, 0:16].rearrange("p (t n) -> p t n", t=NT)).then_inc(free("ab"), 1)
                read(dve, "ab")
                dve.wait_ge(S("dt_landed"), l * 32 + 32)
                st.step(dve.tensor_tensor(ab1[:, :, :], abt[:, :, 0:4], dtab[:, 4:8].unsqueeze(1).broadcast_to([P, NT, 4]), ALU.add))
                st.sync()
                st.step(dve.tensor_scalar(ab2[:, :, :], ab1[:, :, :], -1.0, None, ALU.mult))
                st.sync()
                dve.tensor_tensor(ab2[:, :, :], ab2[:, :, :], ab1[:, :, :], ALU.min).then_inc(S("nabs"), 1)
                dve.wait_ge(S("beta_tanh"), 1)
                st.step(dve.tensor_scalar(betah[:, :, :], beta[:, :, :], 0.25, 0.25, ALU.mult, ALU.add))
                dve.tensor_scalar(beta[:, :, :], beta[:, :, :], 0.5, 0.5, ALU.mult, ALU.add).then_inc(S("beta_ready"), 1)
                dve.wait_ge(S("ln_ready"), 1)
                st.step(dve.scalar_tensor_tensor(ab1[:, :, :], ab1[:, :, :], 0.0, ab2[:, :, :], ALU.max, ALU.add))
                st.sync()
                dve.wait_ge(S("expa"), 1)
                dve.scalar_tensor_tensor(g[:, :, :], ab1[:, :, :], -1.0, ea[:, :].unsqueeze(1).broadcast_to([P, NT, 4]),
                                         ALU.mult, ALU.mult).then_inc(S("g_ready"), 1)
                dve.wait_ge(S("g_ready"), 1)
                for t in range(NT):
                    for hd in range(HEADS):
                        ins = dve.tensor_scalar(Pm[:, t, hd, :], tri, g[:, t, hd:hd + 1], None, ALU.mult)
                        if (t, hd) != (NT - 1, HEADS - 1):
                            st.step(ins)
                ins.then_inc(S("trig"), 1)
                for t in range(NT):
                    for n, (job, dst, width, w) in enumerate(((f"cq{t}", cqn, QL, QL), (f"ck{t}", ckn, KVL + ROPE, KVL))):
                        take(dve, job)
                        dve.tensor_copy(dst[:, t, :], bank(job)[:, 0:width]).then_inc(free(job), 1)
                        read(dve, job)
                        st.step(dve.tensor_tensor(sq[:, 0:w], dst[:, t, 0:w], dst[:, t, 0:w], ALU.mult))
                        st.sync()
                        st.step(dve.tensor_reduce(rv[:, 2 * n + t:2 * n + t + 1], sq[:, 0:w], AX, ALU.add))
                st.sync()
                st.step(dve.tensor_scalar(rv[:, 0:2], rv[:, 0:2], 1.0 / QL, EPS, ALU.mult, ALU.add))
                st.step(dve.tensor_scalar(rv[:, 2:4], rv[:, 2:4], 1.0 / KVL, EPS, ALU.mult, ALU.add))
                rsq(ry[:, 0:4], rv[:, 0:4], rt[:, 0:4])
                for t in range(NT):
                    dve.tensor_scalar(cqn[:, t, :], cqn[:, t, :], ry[:, t:t + 1], None, ALU.mult).then_inc(S("cq_ready"), 1)
                for t in range(NT):
                    dve.tensor_scalar(ckn[:, t, 0:KVL], ckn[:, t, 0:KVL], ry[:, 2 + t:3 + t], None, ALU.mult
                                      ).then_inc(S("ck_ready"), 1)
                def rotate(x, y, cs, sn, n, sig):
                    t1 = rope1[:, 0:n].rearrange("p (a b) -> p a b", b=32)
                    t2 = rope2[:, 0:n].rearrange("p (a b) -> p a b", b=32)
                    lo, hi = x[:, :, 0:32], x[:, :, 32:64]
                    for first, second, op, dst in ((lo, hi, ALU.subtract, y[:, :, 0:32]), (hi, lo, ALU.add, y[:, :, 32:64])):
                        st.sync()
                        st.step(dve.tensor_tensor(t1, first, cs, ALU.mult))
                        st.step(dve.tensor_tensor(t2, second, sn, ALU.mult))
                        st.sync()
                        last = dve.tensor_tensor(dst, t1, t2, op)
                        if op is ALU.subtract or sig is None:
                            st.step(last)
                    if sig is not None:
                        last.then_inc(sig, 1)

                dve.wait_ge(S("ck_ready"), 2)
                rotate(ckn[:, :, KVL:], krd[:, :, 0, :], cos[:, :, :], sin[:, :, :], 2 * 32, None)
                st.sync()
                dve.tensor_copy(krd[:, :, 1, :], krd[:, :, 0, :]).then_inc(S("kr_ready"), 1)
                take(dve, "G")
                dve.tensor_copy(Gs[:, :, :], bank("G")[:, 0:16].rearrange("p (t n) -> p t n", t=NT)).then_inc(free("G"), 1)
                read(dve, "G")
                dve.tensor_tensor(dG[:, :], Gs[:, 0, 4:8], Gs[:, 0, 0:4], ALU.subtract).then_inc(S("dG_ready"), 1)
                square = R1[:, 0:1024]
                for n, (x, part) in enumerate(((qt, "q"), (kt, "k"))):
                    for t in range(NT):
                        read(dve, f"tok_{part}{t}")
                    st.sync()
                    fx = x[:, :, :, :].rearrange("p t h j -> p (t h j)")
                    st.step(dve.tensor_tensor(square, fx, fx, ALU.mult))
                    st.sync()
                    st.step(dve.tensor_reduce(rv[:, 8 * n:8 * n + 8], square.rearrange("p (n j) -> p n j", j=HD), AX, ALU.add))
                st.sync()
                st.step(dve.tensor_scalar(rv[:, :], rv[:, :], 4e-6, None, ALU.add))
                rsq(ry[:, :], rv[:, :], rt[:, :])
                st.step(dve.tensor_scalar(ry[:, 0:8], ry[:, 0:8], HD ** -0.5, None, ALU.mult))
                st.sync()
                scaled(flat(qt[:, :, :, :]), flat(qt[:, :, :, :]), ry[:, 0:8], 8).then_inc(S("qk_norm"), 1)
                scaled(flat(kt[:, :, :, :]), flat(kt[:, :, :, :]), ry[:, 8:16], 8).then_inc(S("qk_norm"), 1)
                dve.wait_ge(S("qk_norm"), 2)
                dve.wait_ge(S("beta_ready"), 1)
                scaled(flat(kb), flat(kt[:, :, :, :]), beta[:, :, :].rearrange("p t h -> p (t h)"), 8
                       ).then_inc(S("kb_ready"), 1)
                for t in range(NT):
                    take(dve, f"Gb{t}")
                    for hd in range(HEADS):
                        ins = dve.tensor_scalar(DT[:, t, hd, :], bank(f"Gb{t}")[:, hd * P:(hd + 1) * P],
                                                Gs[:, t, hd:hd + 1], 0.0, ALU.subtract, ALU.min)
                        if hd < HEADS - 1:
                            st.step(ins)
                    ins.then_inc(free(f"Gb{t}"), 1)
                for t in range(NT):
                    dve.wait_ge(S("dt_exp"), t + 1)
                    st.step(dve.tensor_tensor(DT[:, t, :, :], DT[:, t, :, :], tri.unsqueeze(1).broadcast_to([P, HEADS, P]), ALU.mult))
                take(dve, "qr")
                qr_in = bank("qr")[:, :].rearrange("p (t h n) -> p t h n", t=NT, h=HEADS)
                for t in range(NT):
                    st.step(dve.tensor_copy(qraw[:, :, :], qr_in[:, t, :, :]))
                    rotate(qraw, qr[:, t, :, :], cos[:, t:t + 1, :].broadcast_to([P, HEADS, 32]),
                           sin[:, t:t + 1, :].broadcast_to([P, HEADS, 32]), HEADS * 32, S("qr_ready"))
                    dve.wait_ge(S("qr_ready"), t + 1)
                dve.sem_inc(free("qr"), 1)
                for w, dst in (("kk", AT), ("qk", QK)):
                    for t in range(NT):
                        take(dve, f"{w}{t}")
                        st.sync()
                        dve.tensor_tensor(dst[:, t, :, :].rearrange("p h j -> p (h j)"), bank(f"{w}{t}")[:, :],
                                          DT[:, t, :, :].rearrange("p h j -> p (h j)"), ALU.mult).then_inc(free(f"{w}{t}"), 1)
                for hd in range(HEADS):
                    take(dve, f"s{hd}")
                    dve.tensor_tensor(prob[hd], bank(f"s{hd}")[:, 0:3 * P], cst[:, C_CAUSAL:C_CAUSAL + 3 * P], ALU.add
                                      ).then_inc(free(f"s{hd}"), 1)
                    read(dve, f"s{hd}")
                    st.step(dve.tensor_reduce(nmax[:, hd, 0:1], prob[hd][:, 0:P], AX, ALU.max))
                    st.step(dve.tensor_reduce(nmax[:, hd, 1:2], prob[hd][:, P:3 * P], AX, ALU.max))
                    st.sync()
                    dve.tensor_scalar(nmax[:, hd, :], nmax[:, hd, :], -(NOPE + ROPE) ** -0.5, None, ALU.mult
                                      ).then_inc(S("negmax"), 2)
                for hd in range(HEADS):
                    dve.wait_ge(S("exp_s"), 2 * hd + 2)
                    st.step(dve.reciprocal(psums[:, hd, :], psums[:, hd, :]))
                    st.sync()
                    st.step(dve.tensor_scalar(prob[hd][:, 0:P], prob[hd][:, 0:P], psums[:, hd, 0:1], None, ALU.mult))
                    dve.tensor_scalar(prob[hd][:, P:3 * P], prob[hd][:, P:3 * P], psums[:, hd, 1:2], None, ALU.mult
                                      ).then_inc(S("p_ready"), 1)
                dve.wait_ge(S("M_init"), 2)
                for lev in range(LEVELS):
                    for t in range(NT):
                        for w, X in (("MP", M), ("MPT", MT)):
                            job = f"{w}{t}.{lev}"
                            take(dve, job)
                            x = X[:, t, :, :].rearrange("p h j -> p (h j)")
                            dve.tensor_tensor(x, x, bank(job)[:, :], ALU.subtract).then_inc(free(job), 1)
                dve.wait_ge(S("eG_ready"), 1)
                dve.wait_ge(S("vb_ready"), 1)
                take(dve, "KS")
                for hd in range(HEADS):
                    ins = dve.scalar_tensor_tensor(Rn[:, hd, :], bank("KS")[:, hd * P:(hd + 1) * P], eG[:, 1, hd:hd + 1],
                                                   vt[:, 1, hd, :], ALU.mult, ALU.subtract)
                    if hd < HEADS - 1:
                        st.step(ins)
                ins.then_inc(free("KS"), 1)
                read(dve, "O0")
                read(dve, "O1")
                take(dve, "O1s")
                for hd in range(HEADS):
                    ins = dve.scalar_tensor_tensor(o[:, 1, hd, :], bank("O1s")[:, hd * P:(hd + 1) * P], eG[:, 1, hd:hd + 1],
                                                   o[:, 1, hd, :], ALU.mult, ALU.add)
                    if hd < HEADS - 1:
                        st.step(ins)
                ins.then_inc(free("O1s"), 1)
                read(dve, "O1s")
                fo = o[:, :, :, :].rearrange("p t h j -> p (t h j)")
                square = DT[:, :, :, :].rearrange("p t h j -> p (t h j)")
                st.step(dve.tensor_tensor(square, fo, fo, ALU.mult))
                st.sync()
                st.step(dve.tensor_reduce(rv[:, 0:8], square.rearrange("p (n j) -> p n j", j=HD), AX, ALU.add))
                st.sync()
                st.step(dve.tensor_scalar(rv[:, 0:8], rv[:, 0:8], 1.0 / HD, EPS, ALU.mult, ALU.add))
                rsq(ry[:, 0:8], rv[:, 0:8], rt[:, 0:8])
                st.step(scaled(flat(o[:, :, :, :]), flat(o[:, :, :, :]), ry[:, 0:8], 8))
                st.sync()
                read(dve, "z1")
                dve.tensor_tensor(fo, fo, z[:, :, :, :].rearrange("p t h j -> p (t h j)"), ALU.mult).then_inc(S("o_ready"), 1)
                for t in range(NT):
                    take(dve, f"cvt{t}")
                    st.step(dve.bn_stats(stats[:, t, 0, :], bank(f"cvt{t}")[:, :]))
                    st.sync()
                    st.step(dve.bn_aggr(mvar[:, t, :], stats[:, t, 0, :]))
                st.sync()
                st.step(dve.tensor_scalar(rv[:, 0:NT], mvar[:, :, 1], EPS, None, ALU.add))
                rsq(ry[:, 0:NT], rv[:, 0:NT], rt[:, 0:NT])
                for t in range(NT):
                    dve.tensor_scalar(cvn[:, t, :], bank(f"cvt{t}")[:, :], mvar[:, t, 0:1], ry[:, t:t + 1],
                                      ALU.subtract, ALU.mult).then_inc(free(f"cvt{t}"), 1)
                dve.wait_ge(S("cv_tanh"), 1)
                dve.scalar_tensor_tensor(cvu[:, :, :], cvg[:, :, :], 1.0, cvu[:, :, :], ALU.add, ALU.mult
                                         ).then_inc(S("cv_ready"), 1)
                with dve.Fori(0, KD // 2) as i:
                    for s in range(2):
                        n = i * 8 + 4 * s
                        dve.wait_ge(S("gate_act"), i * 6 + (3 * s + 3))
                        dve.scalar_tensor_tensor(gm[s], gth[s][0], 1.0, ps[s * 3][:, T:2 * T], ALU.add, ALU.mult
                                                 ).then_inc(S("gate_sum"), 1)
                        dve.scalar_tensor_tensor(gt[s], gth[s][1], 1.0, gyb[s], ALU.add, ALU.mult).then_inc(S("gate_sum"), 1)
                        dve.wait_ge(S("gate_sum"), n + 2)
                        dve.tensor_tensor(gm[s], gm[s], gt[s], ALU.add).then_inc(S("gate_sum"), 1)
                        dve.wait_ge(S("gate_sum"), n + 3)
                        dve.scalar_tensor_tensor(gt[s], gth[s][2], 1.0, ps[s * 3 + 2][:, T:2 * T], ALU.add, ALU.mult
                                                 ).then_inc(S("gate_sum"), 1)
                        dve.wait_ge(S("gate_sum"), n + 4)
                        dve.tensor_tensor(merged[:, ds(i * 2 + s, 1), :], gm[s].unsqueeze(1), gt[s].unsqueeze(1), ALU.add
                                          ).then_inc(S("gate_used"), 1)
                norm(l, 1, 2, 2 * ALPHA, 4 * EPS)
                ffn(l, 1)
                norm(l, 2, 3, 4 * ALPHA, 16 * EPS)
                dve.wait_ge(hT_split, l * 2 + 3)
            second_vector(dve, st)

        @block.gpsimd
        def _(pool):
            st = Steps(pool, S("pool_steps"))
            for t in range(NT):
                pool.dma_start(pos[:, t:t + 1], A["positions"].rearrange("b p -> p b")[t * P:(t + 1) * P, :]
                               ).then_inc(S("pos_landed"), 16)
            st.step(pool.memset(ones[:, :], 1.0))
            pool.memset(cvpad[:, :, 0:PAD], 0.0).then_inc(S("cvpad_zero"), 1)

            def load_gain(l, which):
                for dst, name in ((gain, f"ln{which}_g"), (bias, f"ln{which}_b")):
                    pool.dma_start(dst, A[name][ds(l, 1), :].broadcast_to([P, D])).then_inc(S("gain_landed"), 16)

            def residual(k, l, nxt):
                pool.wait_ge(S("tr_full"), 4 * k + 4)
                pool.wait_ge(S("gain_landed"), l * 96 + (32 * k + 32))
                for by, op in ((gain, ALU.mult), (bias, ALU.add)):
                    st.sync()
                    for t in range(NT):
                        ins = pool.tensor_tensor(h[:, t, :], h[:, t, :], by, op)
                        if t == NT - 1 and op is ALU.add:
                            ins.then_inc(S("h_ready"), 1)
                        else:
                            st.step(ins)
                if nxt:
                    pool.wait_ge(S("h_ready"), k + 1)
                    load_gain(l, nxt)

            with pool.Fori(0, DEPTH) as l:
                meet(pool, "gpsimd", l, st)
                load_gain(l, 1)
                st.step(pool.memset(prow[:, :, :], 0.0))
                st.sync()
                for name, (tile, at, n) in ROWS.items():
                    src = A[name][l]
                    if len(src.shape) == 2:
                        src = src.rearrange("k (c p) -> (k c) p", p=P)
                    else:
                        src = src.rearrange("(c p) -> c p", p=P)
                    pool.dma_start(prow[at:at + n, tile, :], src).then_inc(S("rows_landed"), 16)
                for n, name in enumerate(("dn_a_log", "dn_dt_bias")):
                    pool.dma_start(dtab[:, 4 * n:4 * n + 4], A[name][ds(l, 1), :].broadcast_to([P, 4])).then_inc(S("dt_landed"), 16)
                pool.wait_ge(S("tr_full"), 4)
                pool.memset(dnpad[:, :, 0:CONV - 1], 0.0).then_inc(S("dn_zero"), 1)
                residual(0, l, 0)
                pool.wait_ge(S("beta_ready"), 1)
                read(pool, "tok_v0")
                read(pool, "tok_v1")
                fv = vt[:, :, :, :].rearrange("p t h j -> p (t h) j")
                pool.tensor_tensor(fv, fv, betah[:, :, :].rearrange("p t h -> p (t h)").unsqueeze(2).broadcast_to([P, 8, HD]),
                                   ALU.mult).then_inc(S("vb_ready"), 1)
                for X in (M, MT):
                    pool.tensor_copy(X.rearrange("p t h j -> p (t h) j"), ident.unsqueeze(1).broadcast_to([P, 8, P])
                                     ).then_inc(S("M_init"), 1)
                pool.wait_ge(S("eD_ready"), 1)
                pool.wait_ge(S("qk_norm"), 2)
                pool.tensor_tensor(kdec[:, :, :], kt[:, 0, :, :], eD[:, :].unsqueeze(2).broadcast_to([P, HEADS, HD]),
                                   ALU.mult).then_inc(S("kdec_ready"), 1)
                for lev in range(LEVELS):
                    for t in range(NT):
                        if lev == 0:
                            read(pool, f"kk{t}")
                        if lev >= 2:
                            take(pool, f"P{t}.{lev - 2}")
                        mask = cst[:, C_LEV + lev * P:C_LEV + (lev + 1) * P].unsqueeze(1).broadcast_to([P, HEADS, P])
                        pool.tensor_tensor(ATl[lev % 2][:, t, :, :], AT[:, t, :, :], mask, ALU.mult).then_inc(S("lev_mask"), 1)
                pool.wait_ge(S("o_ready"), 1)
                load_gain(l, 2)
                residual(1, l, 3)
                residual(2, l, 0)
                pool.wait_ge(S("h_ready"), 3)
            second_pool(pool, st)


NAMES = ['const', 'x', 'positions', 'ln1_g', 'ln1_b', 'ffn1_w_gate', 'ffn1_w_up', 'ffn1_w_down', 'w_in', 'b_gate', 'dn_conv_w', 'dn_a_log', 'dn_dt_bias', 'dn_norm_w', 'dn_w_o', 'cv_glu_b', 'cv_dw_w', 'cv_dw_b', 'cv_ln_g', 'cv_ln_b', 'cv_w_pw2', 'cv_b_pw2', 'mla_q_norm_w', 'mla_w_uq', 'mla_kv_norm_w', 'mla_w_ukv', 'mla_w_o', 'w_out', 'ln2_g', 'ln2_b', 'ffn2_w_gate', 'ffn2_w_up', 'ffn2_w_down', 'ln3_g', 'ln3_b', 'c_2', 'w_ada_2', 'b_ada_2', 'w_in_2', 'conv_w_2', 'conv_b_2', 'w_gate_a_2', 'b_gate_a_2', 'w_gate_x_2', 'b_gate_x_2', 'lru_lambda_2', 'rel_bias_2', 'norm_lru_g_2', 'norm_attn_g_2', 'w_out_2', 'ln1_g_2', 'ln1_b_2', 'w_router_group_2', 'b_router_group_2', 'w_router_expert_2', 'b_router_expert_2', 'w1_2', 'w3_2', 'w2_2', 'ln2_g_2', 'ln2_b_2']


def kernel(**inputs):
    import concourse.bacc as _bacc
    from concourse.bass_utils import run_bass_kernel_spmd as _run

    nc = _bacc.Bacc("TRN2", target_bir_lowering=False, num_devices=1)
    arrays, A = {}, {}
    for name in NAMES:
        a = np.ascontiguousarray(shape_constants() if name == "const" else inputs[name])
        arrays[f"in_{name}"] = a
        A[name] = nc.dram_tensor(f"in_{name}", a.shape, mybir.dt.from_np(a.dtype), kind="ExternalInput").ap()
    out = nc.dram_tensor("out_0", (1, T, D), F32, kind="ExternalOutput").ap()
    build(nc, A, out)
    return _run(nc, [arrays], core_ids=[0]).results[0]["out_0"]
```
